# Optimizing a Trainium2 kernel written in Bass

```python
import jax, jax.numpy as jnp
from jax import lax
import numpy as np

D_MODEL = 1024
BATCH = 1
SEQ = 512
DEPTH = 2
DEC_BATCH = 8
DEC_SEQ = 4
PAST_LEN = 2048
PAGE_SIZE = 128

N_META = 16
BLOCK = 128
META_PAD = BLOCK - N_META
CHUNK_A = 128
CHUNK_C = 64
H_A = 4
DK_A = 128
DV_A = 128
H_B = 8
DH_B = 64
H_C = 4
DK_C = 128
DV_C = 256
GATE_RANK = 16
GATE_TAU = 16.0
SB_BIAS_INIT = -6.5
D_FF = 4 * D_MODEL
N_EVEN = (DEPTH + 1) // 2
N_ODD = DEPTH // 2
MIX_EVEN = H_A * DV_A + H_B * DH_B
MIX_ODD = H_C * DV_C
EVEN_SPLITS = (H_A * DK_A, H_A * DK_A, H_A * DV_A, H_A * DV_A, H_A, H_A, H_B * DH_B, H_B * DH_B, H_B * DH_B)
ODD_SPLITS = (H_C * DK_C, H_C * DK_C, H_C * DV_C, H_C * DV_C, GATE_RANK)
EVEN_IN = sum(EVEN_SPLITS)
ODD_IN = sum(ODD_SPLITS)
EPS = 1e-6

kernel_name = "hybrid_mlstm_stickbreak_gla_decode_step"

f32 = jnp.float32

def _rms(x, g):
    xf = x.astype(f32)
    y = xf * lax.rsqrt(jnp.mean(xf * xf, axis=-1, keepdims=True) + EPS)
    return (y * g.astype(f32)).astype(x.dtype)

def _head_rms(h, g, n_heads):
    shp = h.shape
    hf = h.astype(f32).reshape(shp[:-1] + (n_heads, shp[-1] // n_heads))
    hf = hf * lax.rsqrt(jnp.mean(hf * hf, axis=-1, keepdims=True) + EPS)
    return hf.reshape(shp) * g.astype(f32)

def _split(x, sizes):
    out, off = [], 0
    for s in sizes:
        out.append(x[..., off:off + s])
        off += s
    return out

def _heads(t, h):
    return t.reshape(t.shape[:-1] + (h, t.shape[-1] // h))

def _to_chunks(x, c):
    B, L, H = x.shape[:3]
    rest = x.shape[3:]
    x = x.reshape((B, L // c, c, H) + rest)
    return x.transpose((1, 0, 3, 2) + tuple(range(4, x.ndim)))

def _from_chunks(y):
    nc, B, H, c, d = y.shape
    return y.transpose(1, 0, 3, 2, 4).reshape(B, nc * c, H, d)

def _mlstm_chunked(q, k, v, log_i, log_f, C0, n0, m0, chunk):
    xs = tuple(_to_chunks(a.astype(f32), chunk) for a in (q, k, v, log_i, log_f))
    causal = jnp.tril(jnp.ones((chunk, chunk), bool))

    def step(carry, inp):
        C, n, m = carry
        qc, kc, vc, ic, fc = inp
        b = jnp.cumsum(fc, axis=-1)
        d_log = jnp.where(causal, b[..., :, None] - b[..., None, :] + ic[..., None, :], -jnp.inf)
        inter = b + m[..., None]
        m_t = jnp.maximum(inter, jnp.max(d_log, axis=-1))
        s = jnp.einsum('bhtk,bhsk->bhts', qc, kc) * jnp.exp(d_log - m_t[..., None])
        w_inter = jnp.exp(inter - m_t)
        num = w_inter[..., None] * jnp.einsum('bhtk,bhkv->bhtv', qc, C) + jnp.einsum('bhts,bhsv->bhtv', s, vc)
        den = w_inter * jnp.einsum('bhtk,bhk->bht', qc, n) + jnp.sum(s, axis=-1)
        h = num / jnp.maximum(jnp.abs(den), jnp.exp(-m_t))[..., None]
        b_last = b[..., -1]
        g = b_last[..., None] - b + ic
        m_new = jnp.maximum(b_last + m, jnp.max(g, axis=-1))
        w_k = jnp.exp(g - m_new[..., None])
        w_d = jnp.exp(b_last + m - m_new)
        C_new = w_d[..., None, None] * C + jnp.einsum('bhs,bhsk,bhsv->bhkv', w_k, kc, vc)
        n_new = w_d[..., None] * n + jnp.einsum('bhs,bhsk->bhk', w_k, kc)
        return (C_new, n_new, m_new), h

    (C, n, m), hs = lax.scan(step, (C0.astype(f32), n0.astype(f32), m0.astype(f32)), xs)
    return _from_chunks(hs), C, n, m

def _gla_chunked(q, k, v, log_g, S0, chunk):
    xs = tuple(_to_chunks(a.astype(f32), chunk) for a in (q, k, v, log_g))
    causal = jnp.tril(jnp.ones((chunk, chunk), bool))

    def step(S, inp):
        qc, kc, vc, gc = inp
        b = jnp.cumsum(gc, axis=2)
        o_inter = jnp.einsum('bhtk,bhkv->bhtv', qc * jnp.exp(b), S)
        rel = jnp.where(causal[:, :, None], b[:, :, :, None, :] - b[:, :, None, :, :], -jnp.inf)
        a = jnp.einsum('bhtk,bhsk,bhtsk->bhts', qc, kc, jnp.exp(rel))
        o = o_inter + jnp.einsum('bhts,bhsv->bhtv', a, vc)
        b_last = b[:, :, -1]
        S_new = jnp.exp(b_last)[..., None] * S + jnp.einsum('bhsk,bhsv->bhkv', kc * jnp.exp(b_last[:, :, None, :] - b), vc)
        return S_new, o

    S, os_ = lax.scan(step, S0.astype(f32), xs)
    return _from_chunks(os_), S

def _stick_breaking(q, k, v, mask, bias):
    z = jnp.einsum('bthd,bshd->bhts', q.astype(f32), k.astype(f32)) * (DH_B ** -0.5) + bias.astype(f32)[None, :, None, None]
    log_stay = jnp.where(mask, jax.nn.log_sigmoid(-z), 0.0)
    after = lax.cumsum(log_stay, axis=3, reverse=True)
    after = jnp.concatenate([after[..., 1:], jnp.zeros_like(after[..., :1])], axis=-1)
    w = jnp.where(mask, jnp.exp(jax.nn.log_sigmoid(z) + after), 0.0)
    return jnp.einsum('bhts,bshd->bthd', w, v.astype(f32))

def _sb_prompt(q, k, v, valid, bias):
    B, L, H, d = q.shape
    nb = L // BLOCK
    qb = q.reshape(B, nb, BLOCK, H, d).transpose(1, 0, 2, 3, 4)
    pos = jnp.arange(L)

    def one(args):
        q_blk, blk = args
        t_pos = blk * BLOCK + jnp.arange(BLOCK)
        mask = (pos[None, :] < t_pos[:, None]) & valid[None, :]
        return _stick_breaking(q_blk, k, v, mask, bias)

    out = lax.map(one, (qb, jnp.arange(nb)))
    return out.transpose(1, 0, 2, 3, 4).reshape(B, L, H, d)

def _even_proj(xn, w_in, b_gate):
    q_a, k_a, v_a, o_a, i_a, f_a, q_b, k_b, v_b = _split(xn @ w_in, EVEN_SPLITS)
    log_i = i_a.astype(f32) + b_gate[:H_A].astype(f32)
    log_f = jax.nn.log_sigmoid(f_a.astype(f32) + b_gate[H_A:].astype(f32))
    return (_heads(q_a, H_A), _heads(k_a, H_A) * (DK_A ** -0.5), _heads(v_a, H_A), o_a, log_i, log_f,
            _heads(q_b, H_B), _heads(k_b, H_B), _heads(v_b, H_B))

def _even_out(h_a, o_a, h_b, g_head, w_out, dt):
    B, L = h_a.shape[:2]
    y_a = _head_rms(h_a.reshape(B, L, -1), g_head, H_A) * jax.nn.sigmoid(o_a.astype(f32))
    y = jnp.concatenate([y_a, h_b.reshape(B, L, -1)], axis=-1).astype(dt)
    return y @ w_out

def _odd_proj(xn, w_in, w_gate_up, b_gate_up):
    q, k, v, r, g_down = _split(xn @ w_in, ODD_SPLITS)
    log_g = jax.nn.log_sigmoid((g_down @ w_gate_up).astype(f32) + b_gate_up.astype(f32)) / GATE_TAU
    return _heads(q, H_C) * (DK_C ** -0.5), _heads(k, H_C), _heads(v, H_C), r, _heads(log_g, H_C)

def _odd_out(o, r, g_head, w_out, dt):
    B, L = o.shape[:2]
    y = _head_rms(o.reshape(B, L, -1), g_head, H_C) * jax.nn.silu(r.astype(f32))
    return y.astype(dt) @ w_out

def _mlp(x, w_up, w_down):
    h = jax.nn.relu(x @ w_up)
    return (h * h) @ w_down

def setup_inputs(seed: int = 0) -> dict:
    key = jax.random.key(seed)
    ks = jax.random.split(key, 24)
    n_pages = PAST_LEN // PAGE_SIZE
    n_pool = (DEC_BATCH * n_pages * 5) // 4
    nrm = jax.random.normal
    page_table = jax.random.permutation(ks[8], n_pool)[:DEC_BATCH * n_pages].reshape(DEC_BATCH, n_pages).astype(jnp.int32)
    b_gate_even = jnp.concatenate([0.1 * nrm(ks[12], (N_EVEN, H_A)), 3.0 + 0.1 * nrm(ks[13], (N_EVEN, H_A))], axis=-1)
    return {
        "x_prompt": nrm(ks[0], (BATCH, SEQ, D_MODEL), f32),
        "x_sample": nrm(ks[1], (DEC_BATCH, DEC_SEQ, D_MODEL), f32),
        "cache_sb_k": nrm(ks[2], (N_EVEN, n_pool, PAGE_SIZE, H_B, DH_B), f32),
        "cache_sb_v": nrm(ks[3], (N_EVEN, n_pool, PAGE_SIZE, H_B, DH_B), f32),
        "state_mlstm_c": nrm(ks[4], (N_EVEN, DEC_BATCH, H_A, DK_A, DV_A), f32),
        "state_mlstm_n": nrm(ks[5], (N_EVEN, DEC_BATCH, H_A, DK_A), f32),
        "state_mlstm_m": nrm(ks[6], (N_EVEN, DEC_BATCH, H_A), f32),
        "state_gla_s": 0.1 * nrm(ks[7], (N_ODD, DEC_BATCH, H_C, DK_C, DV_C), f32),
        "page_table": page_table,
        "meta_tokens": nrm(ks[9], (N_META, D_MODEL), f32),
        "norm_gains": 1.0 + 0.02 * nrm(ks[10], (DEPTH, 4, D_MODEL), f32),
        "w_in_even": nrm(ks[11], (N_EVEN, D_MODEL, EVEN_IN), f32) * D_MODEL ** -0.5,
        "b_gate_even": b_gate_even,
        "b_sb_even": SB_BIAS_INIT + 0.3 * nrm(ks[23], (N_EVEN, H_B), f32),
        "g_head_even": 1.0 + 0.02 * nrm(ks[14], (N_EVEN, H_A * DV_A), f32),
        "w_out_even": nrm(ks[15], (N_EVEN, MIX_EVEN, D_MODEL), f32) * MIX_EVEN ** -0.5,
        "w_in_odd": nrm(ks[16], (N_ODD, D_MODEL, ODD_IN), f32) * D_MODEL ** -0.5,
        "w_gate_up_odd": nrm(ks[17], (N_ODD, GATE_RANK, H_C * DK_C), f32) * GATE_RANK ** -0.5,
        "b_gate_up_odd": 0.1 * nrm(ks[18], (N_ODD, H_C * DK_C), f32),
        "g_head_odd": 1.0 + 0.02 * nrm(ks[19], (N_ODD, H_C * DV_C), f32),
        "w_out_odd": nrm(ks[20], (N_ODD, MIX_ODD, D_MODEL), f32) * MIX_ODD ** -0.5,
        "w_up": nrm(ks[21], (DEPTH, D_MODEL, D_FF), f32) * D_MODEL ** -0.5,
        "w_down": nrm(ks[22], (DEPTH, D_FF, D_MODEL), f32) * D_FF ** -0.5,
    }

def reference(x_prompt, x_sample, cache_sb_k, cache_sb_v, state_mlstm_c, state_mlstm_n, state_mlstm_m, state_gla_s,
              page_table, meta_tokens, norm_gains, w_in_even, b_gate_even, b_sb_even, g_head_even, w_out_even,
              w_in_odd, w_gate_up_odd, b_gate_up_odd, g_head_odd, w_out_odd, w_up, w_down):
    dt = x_prompt.dtype
    B = x_prompt.shape[0]
    DB, T = x_sample.shape[:2]
    pad = jnp.zeros((B, META_PAD, D_MODEL), dt)
    meta = jnp.broadcast_to(meta_tokens.astype(dt)[None], (B, N_META, D_MODEL))
    hp = jnp.concatenate([pad, meta, x_prompt], axis=1)
    Lp = hp.shape[1]
    valid = jnp.arange(Lp) >= META_PAD
    hs = x_sample

    p_k, p_v, p_c, p_n, p_m, p_s = [], [], [], [], [], []
    s_k, s_v, s_c, s_n, s_m, s_s = [], [], [], [], [], []

    for layer in range(DEPTH):
        g = norm_gains[layer]
        xpn = _rms(hp, g[0])
        xsn = _rms(hs, g[0])
        if layer % 2 == 0:
            e = layer // 2
            qa, ka, va, oa, li, lf, qb, kb, vb = _even_proj(xpn, w_in_even[e], b_gate_even[e])
            li = jnp.where(valid[None, :, None], li, -jnp.inf)
            lf = jnp.where(valid[None, :, None], lf, 0.0)
            ha, C, n, m = _mlstm_chunked(qa, ka, va, li, lf,
                                         jnp.zeros((B, H_A, DK_A, DV_A), f32), jnp.zeros((B, H_A, DK_A), f32),
                                         jnp.zeros((B, H_A), f32), CHUNK_A)
            hb = _sb_prompt(qb, kb, vb, valid, b_sb_even[e])
            mix_p = _even_out(ha, oa, hb, g_head_even[e], w_out_even[e], dt)
            p_k.append(kb[:, META_PAD:])
            p_v.append(vb[:, META_PAD:])
            p_c.append(C)
            p_n.append(n)
            p_m.append(m)
            qa, ka, va, oa, li, lf, qb, kb, vb = _even_proj(xsn, w_in_even[e], b_gate_even[e])
            ha, C, n, m = _mlstm_chunked(qa, ka, va, li, lf, state_mlstm_c[e], state_mlstm_n[e], state_mlstm_m[e], T)
            k_past = cache_sb_k[e][page_table].reshape(DB, -1, H_B, DH_B)
            v_past = cache_sb_v[e][page_table].reshape(DB, -1, H_B, DH_B)
            P = k_past.shape[1]
            k_all = jnp.concatenate([k_past, kb.astype(k_past.dtype)], axis=1)
            v_all = jnp.concatenate([v_past, vb.astype(v_past.dtype)], axis=1)
            mask = jnp.arange(P + T)[None, :] < (P + jnp.arange(T))[:, None]
            hb = _stick_breaking(qb, k_all, v_all, mask, b_sb_even[e])
            mix_s = _even_out(ha, oa, hb, g_head_even[e], w_out_even[e], dt)
            s_k.append(kb)
            s_v.append(vb)
            s_c.append(C)
            s_n.append(n)
            s_m.append(m)
        else:
            o_i = layer // 2
            q, k, v, r, lg = _odd_proj(xpn, w_in_odd[o_i], w_gate_up_odd[o_i], b_gate_up_odd[o_i])
            k = jnp.where(valid[None, :, None, None], k, 0.0)
            lg = jnp.where(valid[None, :, None, None], lg, 0.0)
            o, S = _gla_chunked(q, k, v, lg, jnp.zeros((B, H_C, DK_C, DV_C), f32), CHUNK_C)
            mix_p = _odd_out(o, r, g_head_odd[o_i], w_out_odd[o_i], dt)
            p_s.append(S)
            q, k, v, r, lg = _odd_proj(xsn, w_in_odd[o_i], w_gate_up_odd[o_i], b_gate_up_odd[o_i])
            o, S = _gla_chunked(q, k, v, lg, state_gla_s[o_i], T)
            mix_s = _odd_out(o, r, g_head_odd[o_i], w_out_odd[o_i], dt)
            s_s.append(S)
        hp = hp + _rms(mix_p.astype(dt), g[1])
        hs = hs + _rms(mix_s.astype(dt), g[1])
        hp = hp + _rms(_mlp(_rms(hp, g[2]), w_up[layer], w_down[layer]).astype(dt), g[3])
        hs = hs + _rms(_mlp(_rms(hs, g[2]), w_up[layer], w_down[layer]).astype(dt), g[3])

    y_prompt = hp[:, META_PAD + N_META:]
    return (y_prompt, hs,
            jnp.stack(p_k), jnp.stack(p_v), jnp.stack(p_c), jnp.stack(p_n), jnp.stack(p_m), jnp.stack(p_s),
            jnp.stack(s_k), jnp.stack(s_v), jnp.stack(s_c), jnp.stack(s_n), jnp.stack(s_m), jnp.stack(s_s))


_drawn_inputs = setup_inputs


def setup_inputs(seed=0):
    import zlib

    import numpy as np

    out = dict(_drawn_inputs(seed))
    spreads = {}
    factors = {}
    for name, (base, spread) in spreads.items():
        noise = np.random.default_rng([zlib.crc32(name.encode()), seed]).standard_normal(out[name].shape)
        drawn = base * np.exp(spread * noise) if base else spread * noise
        out[name] = __import__('jax').numpy.asarray(drawn.astype(out[name].dtype))
    for name, factor in factors.items():
        out[name] = (out[name] * factor).astype(out[name].dtype)
    return out
```

```python
from contextlib import ExitStack

import numpy as np

import concourse.bass as bass
from concourse import mybir

D = 1024
P = 128
KB = D // P
SEQ, N_META, DEC_B, DEC_T = 512, 16, 8, 4
N_SAMP = DEC_B * DEC_T
N_TOK = SEQ + N_SAMP + N_META
HALF = N_TOK // 2
N_TILE = SEQ // P
SAMP0, META0 = SEQ, SEQ + N_SAMP
T4 = N_SAMP + N_META
H_A, H_B, H_C = 4, 8, 4
DH_B = 64
DV_C = 256
N_PAGES = 16
D_FF = 4 * D
EPS = 1e-6
N_EVEN_BLK = 28
QA, KA, VA, OA, QB, KBB, VB = range(0, 28, 4)
N_ODD_BLK = 24
QC, KC, VC, RC = 0, 4, 8, 16
SLAB_TILES = 16
SLAB = SLAB_TILES * P
MLP_GROUPS = D_FF // 512
S_EVEN, S_OUT, S_MLP, S_ODD = 14, 4, 4 * MLP_GROUPS, 12
SLAB0 = {"even": 0, "out0": 14, "mlp0": 18, "odd": 50, "out1": 62, "mlp1": 66}
N_SLABS = 98
NEG = -1e30

C_ID, C_ONE, C_U, C_NEG, C_NEG4, C_SBM, C_SEL, C_SEQM = 0, 128, 256, 384, 512, 560, 688, 1200
C_NEWM = 1208
C_END = C_NEWM + 32


def constants():
    c = np.zeros((P, C_END), np.float32)
    i = np.arange(P)
    c[:, C_ID:C_ID + P] = i[:, None] == i[None, :]
    c[:, C_ONE:C_ONE + P] = 1
    c[:, C_U:C_U + P] = i[:, None] > i[None, :]
    c[:, C_NEG:C_NEG + P] = np.where(i[:, None] <= i[None, :], 0, NEG)
    grp = np.where(i[:T4] < N_SAMP, i[:T4] // DEC_T, DEC_B)
    same = (grp[:, None] == grp[None, :]) & (i[:T4, None] <= i[None, :T4])
    c[:T4, C_NEG4:C_NEG4 + T4] = np.where(same, 0, NEG)
    c[:, C_SBM:C_SBM + P] = i[:, None] < i[None, :]
    for h in range(H_A):
        c[h, C_SEL + h * P:C_SEL + (h + 1) * P] = 1
    c[:N_SAMP, C_SEQM:C_SEQM + DEC_B] = (i[:N_SAMP, None] // DEC_T) == np.arange(DEC_B)[None, :]
    c[:N_SAMP, C_NEWM:C_NEWM + N_SAMP] = same[:N_SAMP, :N_SAMP] & (i[:N_SAMP, None] < i[None, :N_SAMP])
    return c


def reset_row():
    r = np.ones((P, N_TOK), np.float32)
    r[:, 0:SEQ:P] = 0
    r[:, SAMP0:META0:DEC_T] = 0
    r[:, META0] = 0
    return r


def level_masks(n, decode, levels):
    i = np.arange(n)
    out = np.zeros((n, len(levels), n), np.int32)
    for a, w in enumerate(levels):
        m = i[:, None] == i[None, :]
        if w:
            m = (i[:, None] // (2 * w) == i[None, :] // (2 * w)) & (i[:, None] % (2 * w) < w) & (i[None, :] % (2 * w) >= w)
            if 2 * w > DEC_T:
                m &= (decode[:, None] == 0) & (decode[None, :] == 0)
        out[:, a, :] = m
    return out


class Own:

    def __init__(self, eng, sem):
        self.eng, self.sem, self.n, self.loop, self.per = eng, sem, 0, 0, 0

    def link(self, ins):
        self.n += 1
        ins.then_inc(self.sem, 1)
        self.eng.wait_ge(self.sem, self.loop + self.n)

    def start(self, i, per):
        self.loop, self.per, self.n0 = i * per, per, self.n

    def end(self, trips):
        assert self.n - self.n0 == self.per, f"steps per iteration: {self.n - self.n0}"
        self.n, self.loop = self.n0 + trips * self.per, 0



def build(nc, x, weights, w_gate, w_gdn, w_gup, k_cache, v_cache, pages, c_in, gla_in, m_in, gains, g_even, g_odd,
          b_gate, b_gup, b_sb, b_sbrow, const, reset, masks, masks4,
          y_out, kv_out, c_prompt, c_sample, m_prompt, m_sample, s_prompt, s_sample):
    f32, f32r, i32 = mybir.dt.float32, mybir.dt.float32r, mybir.dt.int32
    ALU, ACT = mybir.AluOpType, mybir.ActivationFunctionType
    ctx = ExitStack()
    with ctx:
        sbuf0 = (nc.sbuf_base + 63) // 64 * 64

        def at(name, off, shape, dt=f32):
            return nc.alloc_sbuf_tensor_at(name, shape, dt, offset=sbuf0 + off)

        def sem(name):
            return ctx.enter_context(nc.semaphore(name))

        ROW = N_TOK * 4
        o_hT = 0
        o_M = o_hT + KB * ROW
        o_xn = o_M + 24 * ROW
        o_raw = o_xn + KB * ROW
        o_hi = o_raw + 2 * SLAB * 4
        o_lo = o_hi + 2 * SLAB * 4
        o_pj = o_lo + 2 * SLAB * 4
        o_c = o_pj + N_EVEN_BLK * ROW
        o_s = o_c + C_END * 4
        hT = at("hT", o_hT, [P, KB, N_TOK])
        xhi = at("xhi", o_M, [P, KB, N_TOK], f32r)
        xlo = at("xlo", o_M + KB * ROW, [P, KB, N_TOK], f32r)
        dhi = at("dhi", o_M + 16 * ROW, [P, 4, N_TOK], f32r)
        dlo = at("dlo", o_M + 20 * ROW, [P, 4, N_TOK], f32r)
        xn = at("xn", o_xn, [P, KB, N_TOK])
        raw = at("raw", o_raw, [P, 2, SLAB_TILES, P])
        whi = at("whi", o_hi, [P, 2, SLAB_TILES, P], f32r)
        wlo = at("wlo", o_lo, [P, 2, SLAB_TILES, P], f32r)
        pj = at("pj", o_pj, [P, N_EVEN_BLK, N_TOK])
        relu = at("relu", o_pj + 24 * ROW, [P, 2, HALF])
        rsq = at("rsq", o_pj + 25 * ROW, [P, 2, HALF])
        rstd = at("rstd", o_pj + 26 * ROW, [P, 2, HALF])
        cst = at("cst", o_c, [P, C_END])
        gn = at("gn", o_s, [P, 2, 4, KB])
        gev = at("gev", o_s + 256, [P, H_A])
        god = at("god", o_s + 288, [P, 8])
        bgu = at("bgu", o_s + 320, [P, H_C])
        bsb = at("bsb", o_s + 352, [P, H_B])
        bsr = at("bsr", o_s + 384, [P, 32])
        bg = at("bg", o_s + 512, [H_A, 2])
        nbf = at("nbf", o_s + 544, [H_A, 1])
        one = at("one", o_s + 576, [P, 1])
        eps = at("eps", o_s + 608, [P, 1])
        ptab = at("ptab", o_s + 640, [1, P], i32)
        mst = at("mst", o_s + 1152, [H_A, DEC_B])
        grow = at("grow", o_s + 1184, [H_A, 2, N_TOK])
        assert sbuf0 + o_s + 1184 + 2 * ROW <= nc.sbuf_usable_end
        ident = cst[:, C_ID:C_ID + P]
        ones = cst[:, C_ONE:C_ONE + P]
        after = cst[:, C_U:C_U + P]
        strict = cst[:, C_SBM:C_SBM + P]

        ps = ctx.enter_context(nc.psum_tensor("ps", [P, 8, 512], f32))

        wg = at("wg", o_pj, [P, KB, 8])
        rows = at("rows", o_M, [H_A, 9, N_TOK])
        R_RST, R_LF, R_B, R_M, R_RM, R_W, R_A, R_WK, R_T = range(9)
        o = o_M + 9 * ROW
        gts = at("gts", o, [P, 5, 16]); o += 320
        ext = at("ext", o, [H_A, 3, DEC_B, 5]); o += 512
        gh = at("gh", o, [P, 5, 4]); o += 96
        wdh = at("wdh", o, [P, 12]); o += 64
        ghc = at("ghc", o, [P, 1]); o += 32
        den = at("den", o, [P, 5]); o += 32
        rec = at("rec", o, [P, 5]); o += 32
        ssq = at("ssq", o, [P, 5]); o += 32
        rs5 = at("rs5", o, [P, 5]); o += 32
        selh = at("selh", o, [H_A, P]); o += 512
        qkv = at("qkv", o, [P, 3, N_TOK]); o += 3 * ROW
        kw = at("kw", o, [P, 5, P]); o += 2560
        vx = at("vx", o, [P, 5, P + 1]); o += 2624
        dec = at("dec", o, [P, N_TOK]); o += ROW
        sT = at("sT", o, [P, N_TOK]); o += ROW
        Cs = at("Cs", o, [P, 5, P + 1]); o += 2624
        qm = at("qm", o, [P, 288]); o += 1152
        hx = at("hx", o, [P, 5, P + 1]); o += 2624
        hn = at("hn", o, [P, 5, P]); o += 2560
        kwm = at("kwm", o, [N_SAMP, DEC_B, P]); o += 4096
        so = at("so", o_s + 1184, [P, N_TOK])
        cfin = at("cfin", o, [P, H_A, P + 1]); o += 2080
        assert o <= o_xn
        c0 = at("c0", o_xn, [P, H_A, DEC_B, P + 1])

        o = o_M
        kbuf = at("kbuf", o, [P, 2, 4, 4, P]); o += 16384
        vbuf = at("vbuf", o, [P, 2, 4, 512]); o += 16384
        qbd = at("qbd", o, [P, 4, DEC_B, 8]); o += 1024
        zg = at("zg", o, [P, 2, P]); o += 1024
        lg = at("lg", o, [P, 2, P]); o += 1024
        sg = at("sg", o, [P, 2, P]); o += 1024
        ssg = at("ssg", o, [P, 2, P]); o += 1024
        acc = at("acc", o, [P, 32]); o += 128
        zn = at("zn", o, [N_SAMP, 256]); o += 1024
        ln_ = at("ln_", o, [N_SAMP, 256]); o += 1024
        spn = at("spn", o, [N_SAMP, 256]); o += 1024
        osn = at("osn", o, [P, 256]); o += 1024
        vnew = at("vnew", o, [N_SAMP, 4, P]); o += 2048
        assert o <= o_xn
        o = o_pj + 4 * ROW
        WZ = 1280
        WA = WZ + SEQ + N_META
        z = at("z", o, [P, WA]); o += 4 * WA
        lz = at("lz", o, [P, WA]); o += 4 * WA
        sp = at("sp", o, [P, WA]); o += 4 * WA
        qz = at("qz", o, [P, 2, N_TOK]); o += 2 * ROW
        assert o <= o_pj + 16 * ROW
        o = o_xn
        kP = at("kP", o, [P, N_TOK]); o += ROW
        vF = at("vF", o, [P, N_TOK]); o += ROW
        vP = at("vP", o, [P, 5, P]); o += 2560
        bh = at("bh", o, [P, 2]); o += 32
        assert o <= o_raw
        KOFF = [0, 512, 896, 1152]

        own = None
        NAMES = """scr_free mout xld cld out hi lo used pj_done pj_act pj_dve gate gate_ev up_done dn_done
            u_act u_hi u_lo d_dve n_sq n_ss n_rs n_xn n_hi n_lo n_h dve act rst rows1 rows2 gt gts_ok
            m_cp m_tr m_bc m_qk m_si m_kv m_qm m_D m_so m_S m_kvs m_in m_C m_it m_hn m_rs m_y m_yt m_end
            a_in a_q a_z a_l a_sp a_A a_t a_w a_v a_o b_pt kv0 kv1 kv_used b_z b_zs b_l b_sp b_A b_t b_w b_pv b_ev
            v_tr v_ev r_a r_e c0ld m_a m_sq d_q d_z d_sp d_A d_w d_o d_zs d_l d_t d_e a_x a_x2 a_e b_x wgl gd_ps gd_ok g_lg g_nb g_a g_l g_ex g_E g_el g_x g_p g_c grst h_cp h_tr h_kv h_kvs h_S h_t4 h_s0 h_rs h_y h_yt h_mix h_a h_sg h_o h_q h_b sst sfree
            """.split()
        S = {n: sem(n) for n in NAMES}

        def expv(act, out, in_, **k):
            return act.activation(out, in_, ACT.Exp, **k)

        RAW = [sem("raw0"), sem("raw1")]
        CREDIT = 16

        def load_pairs(sp_, first, last):
            with sp_.Fori(first // 2, last // 2) as i:
                for par in range(2):
                    sp_.wait_ge(S["lo"], i * 2 + (par + 1))
                    sp_.dma_start(raw[:, par], weights[bass.ds(i * 2 + par, 1), :, :, :]
                                  .rearrange("a p t c -> (a p) t c")).then_inc(RAW[par], 16)

        def split_hi(act, half_s, par):
            act.wait_ge(RAW[par], half_s * 16 + 16)
            act.activation(whi[:, par], raw[:, par], ACT.Copy).then_inc(S["hi"], 1)

        def split_lo(dve, half_s, par):
            dve.wait_ge(S["hi"], half_s * 2 + (par + 1))
            dve.tensor_tensor(wlo[:, par], raw[:, par], whi[:, par].bitcast(f32), ALU.subtract).then_inc(S["lo"], 1)

        def product(pe, out, par, t, hi, lo, first, last):
            pe.matmul(out, whi[:, par, t, :], hi, start=first, stop=False)
            pe.matmul(out, whi[:, par, t, :], lo, start=False, stop=False)
            return pe.matmul(out, wlo[:, par, t, :], hi, start=False, stop=last)

        NS = {"even": S_EVEN, "out0": S_OUT, "odd": S_ODD, "out1": S_OUT}
        PJ0 = {"even": 0, "out0": S_EVEN, "odd": S_EVEN + S_OUT, "out1": S_EVEN + S_OUT + S_ODD}
        COLS = [slice(0, HALF), slice(HALF, N_TOK)]

        def proj_pe(pe, name):
            s0, n0 = SLAB0[name], PJ0[name]
            with pe.Fori(0, NS[name] // 2) as i:
                for par in range(2):
                    pe.wait_ge(S["lo"], i * 2 + (s0 + par + 3))
                    for f in range(2):
                        for h in range(2):
                            bank = 4 * par + 2 * f + h
                            pe.wait_ge(S[("pj_act", "pj_dve")[h]], i * 4 + (2 * n0 + 2 * par + f + 1 + CREDIT - 4))
                            for k in range(KB):
                                mm = product(pe, ps[:, bank, 0:HALF], par, f * KB + k, xhi[:, k, COLS[h]],
                                             xlo[:, k, COLS[h]], k == 0, k == KB - 1)
                            mm.then_inc(S["pj_done"], 1)

        def proj_act(act, name):
            s0, n0 = SLAB0[name], PJ0[name]
            with act.Fori(0, NS[name] // 2) as i:
                for par in range(2):
                    act.wait_ge(S["pj_done"], i * 8 + (4 * (n0 + par) + CREDIT))
                    split_hi(act, i + (s0 + par + 1) // 2, 1 - par)
                    for f in range(2):
                        act.wait_ge(S["pj_done"], i * 8 + (4 * (n0 + par) + 2 * f + 1 + CREDIT))
                        act.activation(pj[:, bass.ds(i * 4 + (2 * par + f), 1), COLS[0]], ps[:, 4 * par + 2 * f, 0:HALF],
                                       ACT.Copy).then_inc(S["pj_act"], 1)

        def proj_dve(dve, name):
            s0, n0 = SLAB0[name], PJ0[name]
            with dve.Fori(0, NS[name] // 2) as i:
                for par in range(2):
                    split_lo(dve, i + (s0 + par + 1) // 2, 1 - par)
                    for f in range(2):
                        dve.wait_ge(S["pj_done"], i * 8 + (4 * (n0 + par) + 2 * f + 2 + CREDIT))
                        dve.tensor_copy(pj[:, bass.ds(i * 4 + (2 * par + f), 1), COLS[1]],
                                        ps[:, 4 * par + 2 * f + 1, 0:HALF]).then_inc(S["pj_dve"], 1)

        def pj_all(eng, name):
            n = 2 * (PJ0[name] + NS[name]) + CREDIT
            eng.wait_ge(S["pj_act"], n)
            eng.wait_ge(S["pj_dve"], n)

        def mlp_pe(pe, L):
            s0, d0, u0 = SLAB0[f"mlp{L}"], 128 * L + CREDIT, 64 * L
            with pe.Fori(0, MLP_GROUPS) as g:
                for par in range(2):
                    pe.wait_ge(S["lo"], g * 4 + (s0 + par + 3))
                    for f in range(2):
                        for h in range(2):
                            j = 4 * par + 2 * f + h
                            pe.wait_ge(S["d_dve"], g * 16 + (d0 - 8 + j + 1))
                            for k in range(KB):
                                mm = product(pe, ps[:, j, 0:HALF], par, f * KB + k, xhi[:, k, COLS[h]],
                                             xlo[:, k, COLS[h]], k == 0, k == KB - 1)
                            mm.then_inc(S["up_done"], 1)
                for par in range(2):
                    pe.wait_ge(S["lo"], g * 4 + (s0 + par + 5))
                    for h in range(2):
                        if par == 0:
                            pe.wait_ge(S["u_lo"], g * 8 + (u0 + 9 + h))
                        for d in range(4):
                            j = 4 * h + d
                            if par == 0:
                                pe.wait_ge(S["u_act"], g * 8 + (u0 + j + 1))
                            else:
                                pe.wait_ge(S["d_dve"], g * 16 + (d0 + j + 1))
                            for k in range(4):
                                mm = product(pe, ps[:, j, 0:HALF], par, d * 4 + k, dhi[:, k, COLS[h]],
                                             dlo[:, k, COLS[h]], k == 0, k == 3)
                            mm.then_inc(S["dn_done"], 1)

        def mlp_act(act, L):
            s0, d0, u0 = SLAB0[f"mlp{L}"], 128 * L + CREDIT, 64 * L

            def group(g, last=False):
                for par in range(2):
                    if par == 0:
                        act.wait_ge(S["dn_done"], g * 16 + d0)
                    else:
                        act.wait_ge(S["up_done"], g * 8 + (u0 + 4))
                    split_hi(act, g * 2 + (s0 + par + 1) // 2, 1 - par)
                    for f in range(2):
                        for h in range(2):
                            j = 4 * par + 2 * f + h
                            act.wait_ge(S["up_done"], g * 8 + (u0 + j + 1))
                            act.wait_ge(S["u_lo"], g * 8 + (u0 + j + 1))
                            act.activation(relu[:, h], ps[:, j, 0:HALF], ACT.Relu).then_inc(S["u_act"], 1)
                            act.wait_ge(S["u_act"], g * 8 + (u0 + j + 1))
                            act.activation(dhi[:, 2 * par + f, COLS[h]], relu[:, h], ACT.Square).then_inc(S["u_hi"], 1)
                act.wait_ge(S["up_done"], g * 8 + (u0 + 8))
                split_hi(act, g * 2 + (s0 + 2) // 2, 1)
                if not last:
                    act.wait_ge(S["dn_done"], g * 16 + (d0 + 8))
                    split_hi(act, g * 2 + (s0 + 4) // 2, 0)
            with act.Fori(0, MLP_GROUPS - L) as g:
                group(g)
            if L:
                group(MLP_GROUPS - 1, last=True)

        def mlp_dve(dve, L):
            s0, d0, u0 = SLAB0[f"mlp{L}"], 128 * L + CREDIT, 64 * L
            own.link(dve.memset(pj[:, 0:8, :], 0.0))

            def group(g, last=False):
                for par in range(2):
                    split_lo(dve, g * 2 + (s0 + par + 1) // 2, 1 - par)
                    for f in range(2):
                        for h in range(2):
                            j = 4 * par + 2 * f + h
                            dve.wait_ge(S["u_hi"], g * 8 + (u0 + j + 1))
                            own.link(dve.tensor_tensor(rsq[:, h], relu[:, h], relu[:, h], ALU.mult))
                            dve.tensor_tensor(dlo[:, 2 * par + f, COLS[h]], rsq[:, h],
                                              dhi[:, 2 * par + f, COLS[h]].bitcast(f32), ALU.subtract)\
                               .then_inc(S["u_lo"], 1)
                split_lo(dve, g * 2 + (s0 + 2) // 2, 1)
                for par in range(2):
                    if par == 1 and not last:
                        split_lo(dve, g * 2 + (s0 + 4) // 2, 0)
                    for h in range(2):
                        for d in range(4):
                            dve.wait_ge(S["dn_done"], g * 16 + (d0 + 8 * par + 4 * h + d + 1))
                            y = pj[:, 4 * par + d, COLS[h]]
                            dve.tensor_tensor(y, ps[:, 4 * h + d, 0:HALF], y, ALU.add).then_inc(S["d_dve"], 1)
            with dve.Fori(0, MLP_GROUPS - L) as g:
                own.start(g, 8)
                group(g)
                own.end(MLP_GROUPS - L)
            if L:
                group(MLP_GROUPS - 1, last=True)

        def norm_act(act, n, src, split=None):
            for h in range(2):
                m = 2 * n + h
                act.activation(xn[:, :, COLS[h]], src[:, :, COLS[h]], ACT.Square).then_inc(S["n_sq"], 1)
            for h in range(2):
                m = 2 * n + h
                act.wait_ge(S["n_ss"], m + 1)
                act.activation(rstd[:, h], ps[:, h, 0:HALF], ACT.Ln, bias=eps[:, 0:1], scale=1.0 / D)\
                   .then_inc(S["act"], 1)
                act.wait_ge(S["act"], m + 1)
                act.activation(rstd[:, h], rstd[:, h], ACT.Exp, scale=-0.5).then_inc(S["n_rs"], 1)
            if split is not None:
                for h in range(2):
                    act.wait_ge(S["n_xn"], 2 * split + h + 1)
                    act.activation(xhi[:, :, COLS[h]], xn[:, :, COLS[h]], ACT.Copy).then_inc(S["n_hi"], 1)

        def norm_pe(pe, n):
            for h in range(2):
                pe.wait_ge(S["n_sq"], 2 * n + h + 1)
                for k in range(KB):
                    mm = pe.matmul(ps[:, h, 0:HALF], ones, xn[:, k, COLS[h]], start=k == 0, stop=k == KB - 1)
                mm.then_inc(S["n_ss"], 1)

        def prenorm_dve(dve, n, L, g, q):
            for h in range(2):
                dve.wait_ge(S["n_rs"], 2 * n + h + 1)
                for k in range(KB):
                    ins = dve.scalar_tensor_tensor(xn[:, k, COLS[h]], hT[:, k, COLS[h]], gn[:, L, g, k:k + 1],
                                                   rstd[:, h], ALU.mult, ALU.mult)
                ins.then_inc(S["n_xn"], 1)
            split_x(dve, q)

        def split_x(dve, q):
            for h in range(2):
                dve.wait_ge(S["n_hi"], 2 * q + h + 1)
                dve.tensor_tensor(xlo[:, :, COLS[h]], xn[:, :, COLS[h]], xhi[:, :, COLS[h]].bitcast(f32), ALU.subtract)\
                   .then_inc(S["n_lo"], 1)

        def postnorm_dve(dve, n, L, g):
            for h in range(2):
                dve.wait_ge(S["n_rs"], 2 * n + h + 1)
                for k in range(KB):
                    ins = dve.scalar_tensor_tensor(xn[:, k, COLS[h]], pj[:, k, COLS[h]], gn[:, L, g, k:k + 1],
                                                   rstd[:, h], ALU.mult, ALU.mult)
                own.link(ins)
                dve.tensor_tensor(hT[:, :, COLS[h]], hT[:, :, COLS[h]], xn[:, :, COLS[h]], ALU.add).then_inc(S["n_h"], 1)

        def split_mix_act(act, q, parts):
            for src, dst in parts:
                act.activation(xhi[:, dst:dst + 4, :], pj[:, src:src + 4, :], ACT.Copy).then_inc(S["n_hi"], 1)

        def split_mix_dve(dve, q, parts):
            for j, (src, dst) in enumerate(parts):
                dve.wait_ge(S["n_hi"], 2 * q + j + 1)
                dve.tensor_tensor(xlo[:, dst:dst + 4, :], pj[:, src:src + 4, :], xhi[:, dst:dst + 4, :].bitcast(f32),
                                  ALU.subtract).then_inc(S["n_lo"], 1)

        def gates_pe(pe):
            pe.wait_ge(S["n_xn"], 2)
            pe.wait_ge(S["cld"], 16 * N_CONST)
            for q in range(2):
                for h in range(2):
                    for k in range(KB):
                        mm = pe.matmul(ps[0:H_A, 4 + 2 * q + h, 0:HALF], wg[:, k, 4 * q:4 * q + 4], xn[:, k, COLS[h]],
                                       start=k == 0, stop=k == KB - 1)
            mm.then_inc(S["gate"], 1)
            pe.wait_ge(S["gate_ev"], 4)

        def gates_act(act):
            act.wait_ge(S["gate"], 1)
            act.wait_ge(S["rows1"], 1)
            for h in range(2):
                act.activation(grow[:, 0, COLS[h]], ps[0:H_A, 4 + h, 0:HALF], ACT.Identity, bias=bg[:, 0:1])\
                   .then_inc(S["gate_ev"], 1)
                act.activation(grow[:, 1, COLS[h]], ps[0:H_A, 6 + h, 0:HALF], ACT.Identity, bias=nbf[:, 0:1], scale=-1.0)\
                   .then_inc(S["gate_ev"], 1)

        def rows_act(act):
            pj_all(act, "even")
            t = rows[:, R_T, :]
            for k, (src, fn, kw_) in enumerate(((grow[:, 1, :], ACT.Abs, {}), (t, ACT.Exp, {"scale": -1.0}),
                                                (t, ACT.Ln, {"bias": one[0:H_A, 0:1]}))):
                act.activation(t, src, fn, **kw_).then_inc(S["r_a"], 1)
                act.wait_ge(S["r_a"], k + 1)
            act.wait_ge(S["rows2"], 1)
            for r in (R_W, R_WK, R_T):
                act.activation(rows[:, r, :], rows[:, r, :], ACT.Exp, scale=-1.0 if r == R_T else 1.0)\
                   .then_inc(S["r_e"], 1)

        def rows_dve(dve):
            R = lambda k: rows[:, k, :]
            dve.wait_ge(S["r_a"], 3)
            dve.wait_ge(S["rst"], 16)
            own.link(dve.scalar_tensor_tensor(R(R_LF), grow[:, 1, :], 0.0, R(R_T), ALU.max, ALU.add))
            own.link(dve.tensor_scalar(R(R_LF), R(R_LF), -1.0, None, ALU.mult))
            own.link(dve.tensor_tensor_scan(R(R_B), R(R_RST), R(R_LF), 0.0, ALU.mult, ALU.add))
            gi = grow[:, 0, :]
            own.link(dve.tensor_tensor_scan(rows[:, R_M, META0:N_TOK], rows[:, R_LF, META0:N_TOK], gi[:, META0:N_TOK],
                                            0.0, ALU.add, ALU.max))
            own.link(dve.tensor_tensor_scan(rows[:, R_M, 0:SEQ], rows[:, R_LF, 0:SEQ], gi[:, 0:SEQ],
                                            rows[:, R_M, N_TOK - 1:N_TOK], ALU.add, ALU.max))
            dve.memset(ext[:, 0], NEG)
            own.link(dve.tensor_copy(ext[:, 1, :, 0:1], mst[:, :].rearrange("p (s o) -> p s o", o=1)))
            own.link(dve.tensor_copy(ext[:, 0, :, 1:5],
                                     rows[:, R_LF, SAMP0:META0].rearrange("p (s t) -> p s t", t=DEC_T)))
            own.link(dve.tensor_copy(ext[:, 1, :, 1:5], gi[:, SAMP0:META0].rearrange("p (s t) -> p s t", t=DEC_T)))
            own.link(dve.tensor_tensor_scan(ext[:, 2].rearrange("p s t -> p (s t)"), ext[:, 0].rearrange("p s t -> p (s t)"),
                                            ext[:, 1].rearrange("p s t -> p (s t)"), 0.0, ALU.add, ALU.max))
            own.link(dve.tensor_copy(rows[:, R_M, SAMP0:META0].rearrange("p (s t) -> p s t", t=DEC_T), ext[:, 2, :, 1:5]))
            own.link(dve.tensor_tensor(R(R_RM), R(R_B), R(R_M), ALU.subtract))
            own.link(dve.tensor_tensor(R(R_A), gi, R(R_B), ALU.subtract))
            own.link(dve.memset(rows[:, R_W, META0:N_TOK], 0.0))
            own.link(dve.tensor_copy(rows[:, R_W, 0:P], rows[:, R_M, N_TOK - 1:N_TOK].to_broadcast([H_A, P])))
            chunk = lambda r, a, b: rows[:, r, a:b].rearrange("p (c t) -> p c t", t=P)
            own.link(dve.tensor_copy(chunk(R_W, P, SEQ), chunk(R_M, 0, SEQ - P)[:, :, P - 1:P].to_broadcast([H_A, 3, P])))
            samp = lambda r: rows[:, r, SAMP0:META0].rearrange("p (s t) -> p s t", t=DEC_T)
            own.link(dve.tensor_copy(samp(R_W), ext[:, 2, :, 0:1].to_broadcast([H_A, DEC_B, DEC_T])))
            own.link(dve.tensor_tensor(R(R_W), R(R_W), R(R_RM), ALU.add))
            own.link(dve.tensor_copy(chunk(R_WK, 0, SEQ), chunk(R_RM, 0, SEQ)[:, :, P - 1:P].to_broadcast([H_A, 4, P])))
            own.link(dve.tensor_copy(samp(R_WK), samp(R_RM)[:, :, DEC_T - 1:DEC_T].to_broadcast([H_A, DEC_B, DEC_T])))
            own.link(dve.tensor_copy(rows[:, R_WK, META0:N_TOK], rows[:, R_RM, N_TOK - 1:N_TOK].to_broadcast([H_A, N_META])))
            own.link(dve.tensor_tensor(R(R_WK), R(R_WK), R(R_A), ALU.add))
            dve.tensor_copy(R(R_T), R(R_M)).then_inc(S["rows2"], 1)
            own.link(dve.memset(gts[:, :, :], 1.0))
            dve.wait_ge(S["gt"], 1)
            dve.tensor_copy(gts[:, 0:4, :], ps[:, 0, 0:64].rearrange("p (c q) -> p c q", q=16))
            own.link(dve.tensor_copy(gts[0:T4, 4, :], ps[0:T4, 0, 64:80]))
            own.link(dve.memset(hx[:, :, :], 1.0))
            own.link(dve.memset(hn[:, :, :], 0.0))
            own.link(dve.memset(qm[:, :], 0.0))
            own.link(dve.tensor_copy(mst[:, :], rows[:, R_M, SAMP0 + DEC_T - 1:META0:DEC_T]))
            dve.sem_inc(S["gts_ok"], 1)

        def rows_pe(pe):
            pe.wait_ge(S["r_e"], 3)
            for c in range(5):
                n = P if c < 4 else T4
                for q, r in enumerate((R_W, R_A, R_WK, R_T)):
                    mm = pe.transpose(ps[0:n, 0, 16 * c + 4 * q:16 * c + 4 * q + 4], rows[:, r, P * c:P * c + n],
                                      ident[0:H_A, 0:H_A])
            mm.then_inc(S["gt"], 1)

        W_, A_, WK_, EM_ = range(4)
        P1 = P + 1

        def mlstm_dve(dve):
            dve.wait_ge(S["c0ld"], 16)
            with dve.Fori(0, H_A) as i:
                own.start(i, 26)
                dve.tensor_copy(qkv[:, 0, :], pj[:, bass.ds(i + QA, 1), :].rearrange("p a n -> p (a n)"))
                dve.tensor_scalar(qkv[:, 1, :], pj[:, bass.ds(i + KA, 1), :].rearrange("p a n -> p (a n)"),
                                  float(P) ** -0.5, None, ALU.mult)
                dve.tensor_copy(qkv[:, 2, :], pj[:, bass.ds(i + VA, 1), :].rearrange("p a n -> p (a n)"))
                dve.tensor_copy(selh[:, :], cst[0:H_A, bass.ds(i * P + C_SEL, P)])
                dve.tensor_copy(ghc[:, :], gev[:, bass.ds(i, 1)])
                own.link(dve.tensor_copy(gh[:, :, :], gts[:, :, :].rearrange("p c (q h) -> p c q h", h=4)
                                         [:, :, :, bass.ds(i, 1)].rearrange("p c q h -> p c (q h)")))
                dve.tensor_copy(qm[:, :].rearrange("p (s c) -> p s c", c=36)[:, :, 0:4],
                                qkv[:, 0, SAMP0:META0].rearrange("p (s t) -> p s t", t=DEC_T)).then_inc(S["m_cp"], 1)
                dve.wait_ge(S["m_tr"], i + 1)
                dve.memset(vx[:, :, P:P1], 1.0)
                dve.tensor_copy(vx[:, 0:4, 0:P], ps[:, 1, :].rearrange("p (c n) -> p c n", n=P))
                dve.tensor_copy(vx[0:T4, 4, 0:P], ps[0:T4, 2, P:2 * P])
                dve.tensor_tensor(kw[:, 0:4, :], ps[:, 0, :].rearrange("p (c n) -> p c n", n=P),
                                  gh[:, 0:4, WK_:WK_ + 1].to_broadcast([P, 4, P]), ALU.mult)
                own.link(dve.tensor_scalar(kw[0:T4, 4, :], ps[0:T4, 2, 0:P], gh[0:T4, 4, WK_:WK_ + 1], None, ALU.mult))
                dve.tensor_tensor(kwm[:, :, :], kw[0:N_SAMP, 4:5, :].to_broadcast([N_SAMP, DEC_B, P]),
                                  cst[0:N_SAMP, C_SEQM:C_SEQM + DEC_B].rearrange("p (s o) -> p s o", o=1)
                                  .to_broadcast([N_SAMP, DEC_B, P]), ALU.mult).then_inc(S["m_kv"], 1)
                dve.wait_ge(S["m_bc"], i + 1)
                dve.wait_ge(S["m_D"], i + 1)
                own.link(dve.tensor_copy(wdh[:, :], ps[:, 4, 64:76]))
                dve.wait_ge(S["m_qk"], i + 1)
                dve.tensor_tensor(sT[:, 0:SEQ], ps[:, 5, :], dec[:, 0:SEQ], ALU.mult)
                dve.tensor_tensor(sT[0:T4, SEQ:N_TOK], ps[0:T4, 6, 0:T4], dec[0:T4, SEQ:N_TOK], ALU.mult)\
                   .then_inc(S["m_S"], 1)
                dve.wait_ge(S["m_kvs"], i + 1)
                own.link(dve.tensor_copy(Cs[:, 0, :], ps[:, 0, 0:P1]))
                for c in range(4):
                    kv = ps[:, 0, (c + 1) * P1:(c + 2) * P1] if c < 2 else ps[:, 1, (c - 2) * P1:(c - 1) * P1]
                    own.link(dve.scalar_tensor_tensor(Cs[:, c + 1, :], Cs[:, c, :], wdh[:, c:c + 1], kv, ALU.mult, ALU.add))
                dve.tensor_copy(cfin[:, bass.ds(i, 1), :], Cs[:, 4:5, :]).then_inc(S["m_C"], 1)
                dve.wait_ge(S["m_in"], i + 1)
                dve.tensor_copy(hx[0:T4, 4, :], ps[0:T4, 5, 0:P1])
                dve.tensor_copy(hx[:, 0:2, :], ps[:, 5, P1:3 * P1].rearrange("p (c n) -> p c n", n=P1))
                own.link(dve.tensor_copy(hx[:, 2:4, :], ps[:, 6, 0:2 * P1].rearrange("p (c n) -> p c n", n=P1)))
                dve.wait_ge(S["m_it"], i + 1)
                own.link(dve.scalar_tensor_tensor(hx[0:N_SAMP, 4, :], ps[0:N_SAMP, 7, 0:P1], gh[0:N_SAMP, 4, W_:W_ + 1],
                                                  hx[0:N_SAMP, 4, :], ALU.mult, ALU.add))
                for s in range(DEC_B):
                    kv = ps[:, 2 + s // 3, (s % 3) * P1:(s % 3 + 1) * P1]
                    st = c0[:, bass.ds(i, 1), s, :].rearrange("p a n -> p (a n)")
                    own.link(dve.scalar_tensor_tensor(st, st, wdh[:, 4 + s:5 + s], kv, ALU.mult, ALU.add))
                for c in range(4):
                    it = ps[:, 0, c * P1:(c + 1) * P1] if c < 3 else ps[:, 1, 0:P1]
                    own.link(dve.scalar_tensor_tensor(hx[:, c, :], it, gh[:, c, W_:W_ + 1], hx[:, c, :], ALU.mult, ALU.add))
                own.link(dve.scalar_tensor_tensor(den[:, :], hx[:, :, P], -1.0, gh[:, :, EM_], ALU.mult, ALU.max))
                own.link(dve.tensor_tensor(den[:, :], hx[:, :, P], den[:, :], ALU.max))
                own.link(dve.reciprocal(rec[:, :], den[:, :]))
                dve.tensor_tensor(hn[:, :, :], hx[:, :, 0:P],
                                  rec[:, :].rearrange("p (c o) -> p c o", o=1).to_broadcast([P, 5, P]), ALU.mult)\
                   .then_inc(S["m_hn"], 1)
                dve.wait_ge(S["m_rs"], i + 1)
                dve.tensor_tensor(hn[:, :, :], hn[:, :, :],
                                  rs5[:, :].rearrange("p (c o) -> p c o", o=1).to_broadcast([P, 5, P]), ALU.mult)\
                   .then_inc(S["m_y"], 1)
                dve.wait_ge(S["m_yt"], i + 1)
                dve.wait_ge(S["m_so"], i + 1)
                dve.scalar_tensor_tensor(pj[:, bass.ds(i, 1), 0:SEQ].rearrange("p a n -> p (a n)"), ps[:, 7, :],
                                         ghc[:, 0:1], so[:, 0:SEQ],
                                         ALU.mult, ALU.mult)
                own.link(dve.scalar_tensor_tensor(pj[:, bass.ds(i, 1), SEQ:N_TOK].rearrange("p a n -> p (a n)"), ps[:, 2, 0:T4],
                                                  ghc[:, 0:1], so[:, SEQ:N_TOK], ALU.mult, ALU.mult))
                own.end(H_A)

        def mlstm_act(act):
            with act.Fori(0, H_A) as i:
                act.wait_ge(S["m_cp"], i + 1)
                act.activation(so[:, :], pj[:, bass.ds(i + OA, 1), :].rearrange("p a n -> p (a n)"), ACT.Exp, scale=-1.0).then_inc(S["m_a"], 1)
                act.wait_ge(S["m_a"], i * 3 + 1)
                act.activation(so[:, :], so[:, :], ACT.Ln, bias=one[:, 0:1]).then_inc(S["m_a"], 1)
                act.wait_ge(S["m_a"], i * 3 + 2)
                act.activation(so[:, :], so[:, :], ACT.Exp, scale=-1.0).then_inc(S["m_so"], 1)
                act.wait_ge(S["m_bc"], i + 1)
                for c in range(4):
                    act.activation(dec[:, c * P:(c + 1) * P], ps[:, 3, c * P:(c + 1) * P], ACT.Exp, bias=gh[:, c, A_:A_ + 1])
                act.activation(dec[0:T4, SEQ:N_TOK], ps[0:T4, 4, 0:T4], ACT.Exp, bias=gh[0:T4, 4, A_:A_ + 1])\
                   .then_inc(S["m_D"], 1)
                act.wait_ge(S["m_hn"], i + 1)
                for c in range(5):
                    ins = act.activation(sT[:, 0:P], hn[:, c, :], ACT.Square, accum_out=ssq[:, c:c + 1])
                    ins.then_inc(S["m_sq"], 1)
                    act.wait_ge(S["m_sq"], i * 5 + (c + 1))
                act.activation(rs5[:, :], ssq[:, :], ACT.Ln, bias=eps[:, 0:1], scale=1.0 / P).then_inc(S["m_a"], 1)
                act.wait_ge(S["m_a"], i * 3 + 3)
                act.activation(rs5[:, :], rs5[:, :], ACT.Exp, scale=-0.5).then_inc(S["m_rs"], 1)

        def mlstm_pe(pe):
            with pe.Fori(0, H_A) as i:
                pe.wait_ge(S["m_cp"], i + 1)
                q, k, v = qkv[:, 0, :], qkv[:, 1, :], qkv[:, 2, :]
                tile = lambda a, c: a[:, P * c:P * c + (P if c < 4 else T4)]
                for c in range(4):
                    pe.transpose(ps[:, 0, c * P:(c + 1) * P], tile(k, c), ident)
                    pe.transpose(ps[:, 1, c * P:(c + 1) * P], tile(v, c), ident)
                pe.transpose(ps[0:T4, 2, 0:P], tile(k, 4), ident)
                pe.transpose(ps[0:T4, 2, P:2 * P], tile(v, 4), ident).then_inc(S["m_tr"], 1)
                pe.matmul(ps[:, 3, :], selh[:, :], rows[:, R_RM, 0:SEQ], start=True, stop=False)
                for c in range(4):
                    pe.matmul(ps[:, 3, c * P:(c + 1) * P], ident, cst[:, C_NEG:C_NEG + P], start=False, stop=c == 3)
                pe.matmul(ps[0:T4, 4, 0:T4], selh[:, 0:T4], rows[:, R_RM, SEQ:N_TOK], start=True, stop=False)
                pe.matmul(ps[0:T4, 4, 0:T4], ident[0:T4, 0:T4], cst[0:T4, C_NEG4:C_NEG4 + T4], start=False, stop=True)
                pe.matmul(ps[:, 4, 64:68], selh[:, :], rows[:, R_W, P - 1:SEQ:P], start=True, stop=True)
                pe.matmul(ps[:, 4, 68:76], selh[:, :], rows[:, R_W, SAMP0 + DEC_T - 1:META0:DEC_T], start=True, stop=True)\
                  .then_inc(S["m_bc"], 1)
                for c in range(4):
                    pe.matmul(ps[:, 5, c * P:(c + 1) * P], tile(k, c), tile(q, c), start=True, stop=True)
                pe.matmul(ps[0:T4, 6, 0:T4], tile(k, 4), tile(q, 4), start=True, stop=True).then_inc(S["m_qk"], 1)
                for s in range(DEC_B):
                    mm = pe.matmul(ps[0:N_SAMP, 7, 0:P1], qm[:, N_SAMP * s:N_SAMP * (s + 1)],
                                   c0[:, bass.ds(i, 1), s, :].rearrange("p a n -> p (a n)"), start=s == 0, stop=s == DEC_B - 1)
                mm.then_inc(S["m_si"], 1)
                pe.wait_ge(S["m_kv"], i + 1)
                pe.wait_ge(S["m_S"], i + 1)
                pe.matmul(ps[:, 0, 0:P1], kw[N_SAMP:T4, 4, :], vx[N_SAMP:T4, 4, :], start=True, stop=True)
                for c in range(4):
                    out = ps[:, 0, (c + 1) * P1:(c + 2) * P1] if c < 2 else ps[:, 1, (c - 2) * P1:(c - 1) * P1]
                    mm = pe.matmul(out, kw[:, c, :], vx[:, c, :], start=True, stop=True)
                mm.then_inc(S["m_kvs"], 1)
                pe.matmul(ps[0:T4, 5, 0:P1], sT[0:T4, SEQ:N_TOK], vx[0:T4, 4, :], start=True, stop=True)
                for c in range(4):
                    out = ps[:, 5, (c + 1) * P1:(c + 2) * P1] if c < 2 else ps[:, 6, (c - 2) * P1:(c - 1) * P1]
                    mm = pe.matmul(out, sT[:, c * P:(c + 1) * P], vx[:, c, :], start=True, stop=True)
                mm.then_inc(S["m_in"], 1)
                for s in range(DEC_B):
                    mm = pe.matmul(ps[:, 2 + s // 3, (s % 3) * P1:(s % 3 + 1) * P1], kwm[:, s, :], vx[0:N_SAMP, 4, :],
                                   start=True, stop=True)
                pe.wait_ge(S["m_C"], i + 1)
                for c in range(4):
                    out = ps[:, 0, c * P1:(c + 1) * P1] if c < 3 else ps[:, 1, 0:P1]
                    mm = pe.matmul(out, tile(q, c), Cs[:, c, :], start=True, stop=True)
                mm.then_inc(S["m_it"], 1)
                pe.wait_ge(S["m_y"], i + 1)
                for c in range(4):
                    pe.transpose(ps[:, 7, c * P:(c + 1) * P], hn[:, c, :], ident)
                pe.transpose(ps[:, 2, 0:T4], hn[0:T4, 4, :], ident[0:T4, 0:T4]).then_inc(S["m_yt"], 1)

        def new_pe(pe):
            pe.wait_ge(S["d_q"], 1)
            for p in range(4):
                pe.matmul(ps[0:N_SAMP, 5, 64 * p:64 * p + 64], pj[:, KBB + p, SAMP0:META0],
                          qbd[:, p, :, :].rearrange("p s c -> p (s c)"), start=True, stop=True)
                mm = pe.transpose(ps[0:N_SAMP, 6, P * p:P * p + P], pj[:, VB + p, SAMP0:META0], ident)
            mm.then_inc(S["d_z"], 1)
            pe.wait_ge(S["d_sp"], 1)
            pe.matmul(ps[0:N_SAMP, 5, 0:256], after[0:N_SAMP, 0:N_SAMP], spn[:, :], start=True, stop=True).then_inc(S["d_A"], 1)
            pe.wait_ge(S["d_w"], 1)
            for p in range(4):
                mm = pe.matmul(ps[:, 7, 64 * p:64 * p + 64], vnew[:, p, :], zn[:, 64 * p:64 * p + 64], start=True, stop=True)
            mm.then_inc(S["d_o"], 1)

        def softplus_act(act, src, dst, s, k0):
            act.activation(dst, src, ACT.Abs).then_inc(s, 1)
            act.wait_ge(s, k0 + 1)
            act.activation(dst, dst, ACT.Exp, scale=-1.0).then_inc(s, 1)
            act.wait_ge(s, k0 + 2)
            n = dst.shape[0]
            return act.activation(dst, dst, ACT.Ln, bias=one[0:n, 0:1])

        def new_act(act):
            act.wait_ge(S["d_zs"], 1)
            softplus_act(act, zn[:, :], ln_[:, :], S["a_x"], 0).then_inc(S["d_l"], 1)
            act.wait_ge(S["d_t"], 1)
            act.activation(zn[:, :], zn[:, :], ACT.Exp).then_inc(S["d_e"], 1)

        def new_dve(dve):
            own.link(dve.memset(qbd[:, :, :, :], 0.0))
            for r, c in ((0, 0), (64, 4)):
                ins = dve.tensor_copy(qbd[r:r + 64, :, :, c:c + 4],
                                      pj[r:r + 64, QB:QB + 4, SAMP0:META0].rearrange("p b (s t) -> p b s t", t=DEC_T))
                if r == 0:
                    own.link(ins)
            ins.then_inc(S["d_q"], 1)
            dve.wait_ge(S["d_z"], 1)
            dve.tensor_copy(vnew[:, :, :], ps[0:N_SAMP, 6, :].rearrange("p (b n) -> p b n", n=P))
            col = lambda a, p: a[:, 64 * p:64 * p + 64]
            v3 = lambda a: a.rearrange("p (s c) -> p s c", c=8)
            v4 = lambda a: a.rearrange("p (s h t) -> p s h t", h=2, t=DEC_T)
            for p in range(4):
                ins = dve.scalar_tensor_tensor(v3(col(zn, p)), v3(ps[0:N_SAMP, 5, 64 * p:64 * p + 64]), DH_B ** -0.5,
                                               bsr[0:N_SAMP, 8 * p:8 * p + 8].rearrange("p (o c) -> p o c", o=1)
                                               .to_broadcast([N_SAMP, DEC_B, 8]), ALU.mult, ALU.add)
            ins.then_inc(S["d_zs"], 1)
            dve.wait_ge(S["d_l"], 1)
            own.link(dve.scalar_tensor_tensor(spn[:, :], zn[:, :], 0.0, ln_[:, :], ALU.max, ALU.add))
            own.link(dve.scalar_tensor_tensor(zn[:, :], zn[:, :], 0.0, ln_[:, :], ALU.min, ALU.subtract))
            msk = cst[0:N_SAMP, C_NEWM:C_NEWM + N_SAMP].rearrange("p (s o t) -> p s o t", o=1, t=DEC_T)\
                .to_broadcast([N_SAMP, DEC_B, 2, DEC_T])
            for p in range(4):
                ins = dve.tensor_tensor(v4(col(spn, p)), v4(col(spn, p)), msk, ALU.mult)
            ins.then_inc(S["d_sp"], 1)
            dve.wait_ge(S["d_A"], 1)
            dve.tensor_tensor(zn[:, :], zn[:, :], ps[0:N_SAMP, 5, 0:256], ALU.subtract).then_inc(S["d_t"], 1)
            dve.wait_ge(S["d_e"], 1)
            for p in range(4):
                ins = dve.tensor_tensor(v4(col(zn, p)), v4(col(zn, p)), msk, ALU.mult)
            ins.then_inc(S["d_w"], 1)
            dve.wait_ge(S["d_o"], 1)
            own.link(dve.tensor_copy(osn[:, :], ps[:, 7, 0:256]))

        def load_pages(sp_):
            with sp_.Fori(0, DEC_B // 2) as i:
                for k in range(8):
                    sp_.wait_ge(S["kv_used"], i * 8 + (k + 1))
                    for a in range(4):
                        at_ = (k // 4) * N_PAGES + 4 * (3 - k % 4) + a
                        page = sp_.value_load(ptab[0:1, bass.ds(i * (2 * N_PAGES) + at_, 1)], min_val=0, max_val=N_POOL - 1)
                        sp_.dma_start(kbuf[:, k % 2, a, :, :].rearrange("p b n -> p (b n)"),
                                      k_cache[bass.ds(page, 1), :, :].rearrange("a p n -> (a p) n")).then_inc(KV[k % 2], 16)
                        sp_.dma_start(vbuf[:, k % 2, a, :],
                                      v_cache[bass.ds(page, 1), :, :].rearrange("a p n -> (a p) n")).then_inc(KV[k % 2], 16)

        KV = [S["kv0"], S["kv1"]]
        N_POOL = k_cache.shape[0]

        def qk_pe(pe, i, k):
            pe.wait_ge(KV[k % 2], i * 512 + 128 * (k // 2 + 1))
            if k >= 2:
                pe.wait_ge(S["b_t"], i * 8 + (k - 1))
            for a in range(4):
                for p in range(4):
                    mm = pe.matmul(ps[:, 5 + k % 2, 32 * a + 8 * p:32 * a + 8 * p + 8], kbuf[:, k % 2, a, p, :],
                                   qbd[:, p, bass.ds(i * 2 + k // 4, 1), :].rearrange("p s c -> p (s c)"), start=True, stop=True)
            mm.then_inc(S["b_z"], 1)

        def suffix_pe(pe, i, k):
            pe.wait_ge(S["b_sp"], i * 8 + (k + 1))
            pe.matmul(ps[:, 5 + k % 2, P:2 * P], after, sg[:, k % 2, :], start=True, stop=False)
            pe.matmul(ps[:, 5 + k % 2, P:2 * P], ones, ssg[:, k % 2, :], start=False, stop=True).then_inc(S["b_A"], 1)

        def pv_pe(pe, i, k):
            pe.wait_ge(S["b_w"], i * 8 + (k + 1))
            if k == 4:
                pe.wait_ge(S["b_ev"], i * 2 + 1)
            for a in range(4):
                for p in range(4):
                    mm = pe.matmul(ps[:, 7, 8 * p:8 * p + 8], vbuf[:, k % 2, a, P * p:P * p + P],
                                   lg[:, k % 2, 32 * a + 8 * p:32 * a + 8 * p + 8], start=(k % 4, a, p) == (0, 0, 0),
                                   stop=(k % 4, a, p) == (3, 3, 3), skip_group_check=True)
            mm.then_inc(S["kv_used"], 1)

        def page_act(act, i, k):
            act.wait_ge(S["b_zs"], i * 8 + (k + 1))
            softplus_act(act, zg[:, k % 2, :], lg[:, k % 2, :], S["b_x"], i * 16 + 2 * k).then_inc(S["b_l"], 1)

        def page_exp(act, i, k):
            act.wait_ge(S["b_t"], i * 8 + (k + 1))
            act.activation(lg[:, k % 2, :], lg[:, k % 2, :], ACT.Exp).then_inc(S["b_w"], 1)

        def page_dve(dve, i, k):
            q = k % 2
            if k % 4 == 0:
                own.link(dve.memset(acc[:, :], 0.0))
                own.link(dve.tensor_copy(acc[0:N_SAMP, :].rearrange("p (b c) -> p b c", c=8),
                                         spn[:, :].rearrange("p (b s c) -> p b s c", s=DEC_B, c=8)
                                         [:, :, bass.ds(i * 2 + k // 4, 1), :].rearrange("p b s c -> p b (s c)")))
            dve.wait_ge(S["b_z"], i * 8 + (k + 1))
            dve.scalar_tensor_tensor(zg[:, q, :].rearrange("p (a c) -> p a c", c=32),
                                     ps[:, 5 + q, 0:P].rearrange("p (a c) -> p a c", c=32), DH_B ** -0.5,
                                     bsr[:, :].rearrange("p (o c) -> p o c", o=1).to_broadcast([P, 4, 32]),
                                     ALU.mult, ALU.add).then_inc(S["b_zs"], 1)
            dve.wait_ge(S["b_l"], i * 8 + (k + 1))
            own.link(dve.scalar_tensor_tensor(sg[:, q, :], zg[:, q, :], 0.0, lg[:, q, :], ALU.max, ALU.add))
            dve.scalar_tensor_tensor(zg[:, q, :], zg[:, q, :], 0.0, lg[:, q, :], ALU.min, ALU.subtract)
            pg = lambda b, a: b[:, q, 32 * a:32 * a + 32]
            own.link(dve.tensor_copy(pg(ssg, 3), acc[:, :]))
            for a in (3, 2, 1):
                own.link(dve.tensor_tensor(pg(ssg, a - 1), pg(ssg, a), pg(sg, a), ALU.add))
            dve.tensor_tensor(acc[:, :], pg(ssg, 0), pg(sg, 0), ALU.add).then_inc(S["b_sp"], 1)
            dve.wait_ge(S["b_sp"], i * 8 + (k + 1))

        def page_sub(dve, i, k):
            q = k % 2
            dve.wait_ge(S["b_A"], i * 8 + (k + 1))
            dve.tensor_tensor(lg[:, q, :], zg[:, q, :], ps[:, 5 + q, P:2 * P], ALU.subtract).then_inc(S["b_t"], 1)

        def page_out(dve, i, k):
            dve.wait_ge(S["kv_used"], i * 8 + (k + 3))
            for r, c in ((0, 0), (64, 4)):
                ins = dve.tensor_tensor(pj[r:r + 64, QB:QB + 4, bass.ds(i * (2 * DEC_T) + (SAMP0 + DEC_T * (k // 4)), DEC_T)],
                                        ps[r:r + 64, 7, 0:32].rearrange("p (b c) -> p b c", c=8)[:, :, c:c + 4],
                                        osn[r:r + 64, :].rearrange("p (b s c) -> p b s c", s=DEC_B, c=8)
                                        [:, :, bass.ds(i * 2 + k // 4, 1), c:c + 4].rearrange("p b s c -> p b (s c)"), ALU.add)
            ins.then_inc(S["b_ev"], 1)

        WID = [SEQ - P * k for k in range(4)]
        ZB = [(0, 0), (1, 0), (2, 0), (2, 256)]
        META = slice(WZ, WZ + SEQ)
        METAQ = slice(WZ + SEQ, WA)

        def pair_dve(dve, i):
            blk = lambda b: pj[:, bass.ds(i + b, 1), :].rearrange("p a n -> p (a n)")
            dve.memset(qz[:, :, :], 0.0)
            dve.tensor_copy(bh[:, :], bsb[:, bass.ds(i * 2, 2)])
            own.link(dve.tensor_copy(kP[:, :], blk(KBB)))
            dve.tensor_copy(vF[:, :], blk(VB))
            for j in range(2):
                r = 64 * j
                ins = dve.tensor_copy(qz[r:r + 64, j, :], pj[r:r + 64, bass.ds(i + QB, 1), :].rearrange("p a n -> p (a n)"))
                if j == 0:
                    own.link(ins)
            ins.then_inc(S["a_in"], 1)
            dve.wait_ge(S["v_tr"], i + 1)
            dve.tensor_copy(vP[:, 0:4, :], ps[:, 4, :].rearrange("p (c n) -> p c n", n=P))
            dve.tensor_copy(vP[0:N_META, 4, :], ps[0:N_META, 2, 384:512]).then_inc(S["v_ev"], 1)

        def pz_pe(pe, i, j):
            if j == 0:
                pe.wait_ge(S["a_in"], i + 1)
                for c in range(4):
                    pe.transpose(ps[:, 4, P * c:P * c + P], vF[:, P * c:P * c + P], ident)
                pe.transpose(ps[0:N_META, 2, 384:512], vF[:, META0:N_TOK], ident).then_inc(S["v_tr"], 1)
                pe.wait_ge(S["v_ev"], i + 1)
            else:
                pe.wait_ge(S["a_t"], i * 2 + 1)
            for k in range(4):
                b, c = ZB[k]
                pe.matmul(ps[:, b, c:c + WID[k]], kP[:, P * k:P * k + P], qz[:, j, P * k:SEQ], start=True, stop=True)
            pe.matmul(ps[0:N_META, 3, 0:SEQ], kP[:, META0:N_TOK], qz[:, j, 0:SEQ], start=True, stop=True)
            pe.matmul(ps[0:N_META, 1, 384:400], kP[:, META0:N_TOK], qz[:, j, META0:N_TOK], start=True, stop=True)\
              .then_inc(S["a_z"], 1)

        def pz_act(act, i, j):
            act.wait_ge(S["a_z"], i * 2 + (j + 1))
            if j == 1:
                act.wait_ge(S["a_w"], i * 2 + 1)
            c = DH_B ** -0.5
            for dst, src in ((z[:, 0:512], ps[:, 0, :]), (z[:, 512:896], ps[:, 1, 0:384]), (z[:, 896:WZ], ps[:, 2, 0:384])):
                ins = act.activation(dst, src, ACT.Identity, scale=c, bias=bh[:, j:j + 1])
            for dst, src in ((z[0:N_META, META], ps[0:N_META, 3, :]), (z[0:N_META, METAQ], ps[0:N_META, 1, 384:400])):
                ins = act.activation(dst, src, ACT.Identity, scale=c, bias=bh[0:N_META, j:j + 1])
            ins.then_inc(S["a_x2"], 1)
            act.wait_ge(S["a_x2"], i * 10 + (5 * j + 1))
            softplus_act(act, z[:, 0:WZ], lz[:, 0:WZ], S["a_x2"], i * 10 + (5 * j + 1))
            softplus_act(act, z[0:N_META, WZ:WA], lz[0:N_META, WZ:WA], S["a_x2"], i * 10 + (5 * j + 3)).then_inc(S["a_l"], 1)

        FULL = [(slice(0, P), slice(0, WZ)), (slice(0, N_META), slice(WZ, WA))]

        def diag_mask(dve, buf):
            for k in range(4):
                dve.tensor_tensor(buf[:, KOFF[k]:KOFF[k] + P], buf[:, KOFF[k]:KOFF[k] + P], strict, ALU.mult)
            return dve.tensor_tensor(buf[0:N_META, METAQ], buf[0:N_META, METAQ], strict[0:N_META, 0:N_META], ALU.mult)

        def psp_dve(dve, i, j):
            dve.wait_ge(S["a_l"], i * 2 + (j + 1))
            for r, c in FULL:
                own.link(dve.scalar_tensor_tensor(sp[r, c], z[r, c], 0.0, lz[r, c], ALU.max, ALU.add))
                own.link(dve.scalar_tensor_tensor(z[r, c], z[r, c], 0.0, lz[r, c], ALU.min, ALU.subtract))
            diag_mask(dve, sp).then_inc(S["a_sp"], 1)

        def suffixes_pe(pe, i, j):
            pe.wait_ge(S["a_sp"], i * 2 + (j + 1))
            for k in range(4):
                b, c = ZB[k]
                pe.matmul(ps[:, b, c:c + WID[k]], after, sp[:, KOFF[k]:KOFF[k] + WID[k]], start=True, stop=k == 3)
                for l in range(k + 1, 4):
                    o_ = P * (l - k)
                    pe.matmul(ps[:, b, c + o_:c + WID[k]], ones, sp[:, KOFF[l]:KOFF[l] + WID[l]], start=False, stop=l == 3)
            pe.matmul(ps[0:N_META, 3, 0:SEQ], after[0:N_META, 0:N_META], sp[0:N_META, META], start=True, stop=False)
            for l in range(4):
                pe.matmul(ps[0:N_META, 3, P * l:SEQ], ones[:, 0:N_META], sp[:, KOFF[l]:KOFF[l] + WID[l]],
                          start=False, stop=l == 3)
            pe.matmul(ps[0:N_META, 1, 384:400], after[0:N_META, 0:N_META], sp[0:N_META, METAQ], start=True, stop=True)\
              .then_inc(S["a_A"], 1)

        def psub_dve(dve, i, j):
            dve.wait_ge(S["a_A"], i * 2 + (j + 1))
            for dst, src in (((slice(0, P), slice(0, 512)), ps[:, 0, :]), ((slice(0, P), slice(512, 896)), ps[:, 1, 0:384]),
                             ((slice(0, P), slice(896, WZ)), ps[:, 2, 0:384]), ((slice(0, N_META), META), ps[0:N_META, 3, :]),
                             ((slice(0, N_META), METAQ), ps[0:N_META, 1, 384:400])):
                ins = dve.tensor_tensor(lz[dst], z[dst], src, ALU.subtract)
            ins.then_inc(S["a_t"], 1)

        def pexp_act(act, i, j):
            act.wait_ge(S["a_t"], i * 2 + (j + 1))
            for r, c in FULL:
                ins = act.activation(lz[r, c], lz[r, c], ACT.Exp)
            ins.then_inc(S["a_e"], 1)

        def pmask_dve(dve, i, j):
            dve.wait_ge(S["a_e"], i * 2 + (j + 1))
            diag_mask(dve, lz).then_inc(S["a_w"], 1)

        def pv_prompt_pe(pe, i, j):
            pe.wait_ge(S["a_w"], i * 2 + (j + 1))
            if j == 1:
                pe.wait_ge(S["a_o"], i * 2 + 1)
            pe.matmul(ps[:, 4, :], vP[0:N_META, 4, :], lz[0:N_META, META], start=True, stop=False)
            for k in range(4):
                pe.matmul(ps[:, 4, P * k:SEQ], vP[:, k, :], lz[:, KOFF[k]:KOFF[k] + WID[k]], start=False, stop=k == 3)
            pe.matmul(ps[:, 2, 384:400], vP[0:N_META, 4, :], lz[0:N_META, METAQ], start=True, stop=True).then_inc(S["a_v"], 1)

        def pout_dve(dve, i, j):
            dve.wait_ge(S["a_v"], i * 2 + (j + 1))
            r = slice(64 * j, 64 * j + 64)
            blk = pj[r, bass.ds(i + QB, 1), :].rearrange("p a n -> p (a n)")
            dve.tensor_scalar(blk[:, 0:SEQ], ps[r, 4, :], 1.0, None, ALU.mult)
            dve.tensor_scalar(blk[:, META0:N_TOK], ps[r, 2, 384:400], 1.0, None, ALU.mult).then_inc(S["a_o"], 1)

        def attn_pe(pe):
            with pe.Fori(0, 4) as i:
                for k in range(8):
                    qk_pe(pe, i, k)
                    if k:
                        pv_pe(pe, i, k - 1)
                    j = k // 4
                    if k % 4 == 0:
                        pz_pe(pe, i, j)
                    if k % 4 == 2:
                        suffixes_pe(pe, i, j)
                    suffix_pe(pe, i, k)
                    if k % 4 == 3:
                        pv_prompt_pe(pe, i, j)
                pv_pe(pe, i, 7)

        def attn_act(act):
            with act.Fori(0, 4) as i:
                for k in range(8):
                    j = k // 4
                    if k:
                        page_exp(act, i, k - 1)
                    page_act(act, i, k)
                    if k % 4 == 0:
                        pz_act(act, i, j)
                    if k % 4 == 2:
                        pexp_act(act, i, j)
                page_exp(act, i, 7)

        def attn_dve(dve):
            with dve.Fori(0, 4) as i:
                own.start(i, 54)
                for k in range(8):
                    j = k // 4
                    if k == 0:
                        pair_dve(dve, i)
                    if k:
                        page_sub(dve, i, k - 1)
                    page_dve(dve, i, k)
                    if k == 4:
                        page_out(dve, i, 3)
                    if k % 4 == 1:
                        psp_dve(dve, i, j)
                    if k % 4 == 2:
                        psub_dve(dve, i, j)
                    if k % 4 == 3:
                        pmask_dve(dve, i, j)
                        pout_dve(dve, i, j)
                page_sub(dve, i, 7)
                page_out(dve, i, 7)
                own.end(4)

        LEVELS = [64, 32, 16, 8, 4, 2, 1, 0]
        X = [at("X0", o_M, [P, H_C, N_TOK]), at("X1", o_M + 4 * ROW, [P, H_C, N_TOK])]
        E = at("E", o_M + 8 * ROW, [P, H_C, N_TOK])
        cum = at("cum", o_M + 12 * ROW, [P, H_C, N_TOK])
        o = o_M + 16 * ROW
        AT = at("AT", o, [P, 5, H_C, P]); o += 5 * H_C * P * 4
        sfin = at("sfin", o, [P, H_C, DV_C])
        gmk = at("gmk", o, [P, 8, P], i32); o += 4096
        gm4 = at("gm4", o, [T4, 5, T4], i32); o += 960
        el = at("el", o, [P, H_C, 13]); o += 224
        nbg = at("nbg", o, [P, H_C]); o += 32
        assert o <= o_xn
        o = o_M + 8 * ROW
        ATh = at("ATh", o, [P, 5, P]); o += 2560
        KT = at("KT", o, [P, 5, P]); o += 2560
        VT = at("VT", o, [P, 5, DV_C]); o += 5120
        Ss = at("Ss", o, [P, 5, DV_C]); o += 5120
        gqm = at("gqm", o, [P, 416]); o += 1664
        elh = at("elh", o, [P, 13]); o += 64
        gos = at("gos", o, [P, 2]); o += 32
        gsq = at("gsq", o, [P, 5]); o += 32
        grs = at("grs", o, [P, 5]); o += 32
        assert o <= o_M + 16 * ROW
        o = o_pj
        gq = at("gq", o, [P, N_TOK]); o += ROW
        gk = at("gk", o, [P, N_TOK]); o += ROW
        gv = at("gv", o, [P, 2, N_TOK]); o += 2 * ROW
        sr = at("sr", o, [P, 2, N_TOK]); o += 2 * ROW
        gkm = at("gkm", o, [N_SAMP, DEC_B, P]); o += 4096
        assert o <= o_pj + 8 * ROW
        on = at("on", o_pj + 24 * ROW, [P, 5, DV_C])
        rst = at("rst", o_pj + 24 * ROW, [P, N_TOK])
        wgd = at("wgd", o_pj + 27 * ROW, [P, KB, 16])
        wgu = at("wgu", o_s + 1184, [16, H_C * P])
        gd = at("gd", o_s + 1184 + 2048, [16, N_TOK])
        s0b = at("s0b", o_xn, [P, 2, DEC_B, DV_C])
        TAU = 16.0
        flat = lambda a: a.rearrange("p h t -> p (h t)")
        UNITS = [(l, c) for l in range(8) for c in range(5) if c < 4 or LEVELS[l] <= 8]

        def gdown_pe(pe):
            pe.wait_ge(S["n_xn"], 6)
            pe.wait_ge(S["wgl"], 32)
            for h in range(2):
                for k in range(KB):
                    mm = pe.matmul(ps[0:16, 4 + h, 0:HALF], wgd[:, k, :], xn[:, k, COLS[h]], start=k == 0, stop=k == KB - 1)
            mm.then_inc(S["gd_ps"], 1)
            pe.wait_ge(S["gd_ok"], 2)

        def gdown_act(act):
            act.wait_ge(S["gd_ps"], 1)
            for h in range(2):
                act.activation(gd[:, COLS[h]], ps[0:16, 4 + h, 0:HALF], ACT.Copy).then_inc(S["gd_ok"], 1)

        def lgate_pe(pe):
            pj_all(pe, "odd")
            for h in range(H_C):
                for k in range(2):
                    mm = pe.matmul(ps[:, 2 * h + k, 0:HALF], wgu[:, P * h:P * h + P], gd[:, COLS[k]], start=True, stop=True)
            mm.then_inc(S["g_lg"], 1)

        def lgate_act(act):
            pj_all(act, "odd")
            act.wait_ge(S["g_lg"], 1)
            act.wait_ge(S["g_nb"], 1)
            for h in range(H_C):
                for k in range(2):
                    ins = act.activation(cum[:, h, COLS[k]], ps[:, 2 * h + k, 0:HALF], ACT.Identity, scale=-1.0,
                                         bias=nbg[:, h:h + 1])
            ins.then_inc(S["g_a"], 1)
            act.wait_ge(S["g_a"], 1)
            softplus_act(act, flat(cum[:, :, :]), flat(E[:, :, :]), S["g_a"], 1).then_inc(S["g_l"], 1)
            for l, w in enumerate(LEVELS[:-1]):
                act.wait_ge(S["g_ex"], l + 1)
                e = E[:, :, 0:SEQ] if w > 8 else E[:, :, :]
                act.activation(e, e, ACT.Exp, scale=1.0 / TAU).then_inc(S["g_E"], 1)
            act.wait_ge(S["g_x"], 7)
            act.activation(E[:, :, :], cum[:, :, :], ACT.Exp, scale=-1.0 / TAU).then_inc(S["g_E"], 1)
            act.wait_ge(S["g_ex"], 8)
            act.activation(E[:, :, :], E[:, :, :], ACT.Exp, scale=1.0 / TAU).then_inc(S["g_E"], 1)
            for a, b, c in ((0, 4, cum[:, :, P - 1:SEQ:P]), (4, 12, cum[:, :, SAMP0 + DEC_T - 1:META0:DEC_T]),
                            (12, 13, cum[:, :, N_TOK - 1:N_TOK])):
                act.activation(el[:, :, a:b], c, ACT.Exp, scale=-1.0 / TAU).then_inc(S["g_el"], 1)

        def level_dve(dve, l):
            w = LEVELS[l]
            if w > 8:
                v = lambda a: a[:, :, 0:SEQ].rearrange("p h (b c) -> p h b c", c=2 * w)
                lo, hi, ref = (slice(0, w), slice(w, 2 * w), slice(w - 1, w))
                sl = lambda a, r: v(a)[:, :, :, r]
                shape = [P, H_C, SEQ // (2 * w), w]
            else:
                v = lambda a: flat(a).rearrange("p (b c) -> p b c", c=2 * w)
                lo, hi, ref = (slice(0, w), slice(w, 2 * w), slice(w - 1, w))
                sl = lambda a, r: v(a)[:, :, r]
                shape = [P, H_C * N_TOK // (2 * w), w]
            x = X[l % 2]
            q, k = pj[:, QC:QC + 4, :], pj[:, KC:KC + 4, :]
            if l:
                dve.wait_ge(S["g_x"], l)
            r = sl(cum[:, :, :], ref).to_broadcast(shape)
            dve.tensor_tensor(sl(E[:, :, :], lo), sl(cum[:, :, :], lo), r, ALU.subtract)
            dve.tensor_tensor(sl(E[:, :, :], hi), r, sl(cum[:, :, :], hi), ALU.subtract).then_inc(S["g_ex"], 1)
            dve.wait_ge(S["g_E"], l + 1)
            if l >= 2:
                dve.wait_ge(S["g_p"], UNITS.index((l - 1, 0)))
            dve.tensor_tensor(sl(x[:, :, :], lo), sl(k, lo), sl(E[:, :, :], lo), ALU.mult)
            dve.tensor_tensor(sl(x[:, :, :], hi), sl(q, hi), sl(E[:, :, :], hi), ALU.mult).then_inc(S["g_x"], 1)

        def level_pick(dve, l):
            if l:
                dve.wait_ge(S["g_c"], UNITS.index((l, 0)))
            for c in range(5):
                if (l, c) not in UNITS:
                    continue
                u = UNITS.index((l, c))
                dve.wait_ge(S["g_p"], u + 1)
                if c < 4:
                    dve.copy_predicated(AT[:, c, :, :], gmk[:, l:l + 1, :].to_broadcast([P, H_C, P]),
                                        ps[:, u % 8, :].rearrange("p (h n) -> p h n", n=P)).then_inc(S["g_c"], 1)
                else:
                    dve.copy_predicated(AT[0:T4, 4, :, 0:T4], gm4[:, l - 3:l - 2, :].to_broadcast([T4, H_C, T4]),
                                        ps[0:T4, u % 8, 0:H_C * T4].rearrange("p (h n) -> p h n", n=T4)).then_inc(S["g_c"], 1)

        def levels_pe(pe):
            for u, (l, c) in enumerate(UNITS):
                if c == 0 and l < 7:
                    pe.wait_ge(S["g_x"], l + 1)
                if c == 0 and l == 0:
                    pe.wait_ge(S["g_l"], 1)
                if u >= 8:
                    pe.wait_ge(S["g_c"], u - 7)
                cols = slice(P * c, P * c + (P if c < 4 else T4))
                n = P if c < 4 else T4
                for h in range(H_C):
                    k, q = (X[l % 2][:, h, cols],) * 2 if l < 7 else (pj[:, KC + h, cols], pj[:, QC + h, cols])
                    mm = pe.matmul(ps[0:n, u % 8, h * n:h * n + n], k, q, start=True, stop=True)
                mm.then_inc(S["g_p"], 1)

        def gla_pre_dve(dve):
            dve.tensor_scalar(nbg[:, :], bgu[:, :], -1.0, None, ALU.mult).then_inc(S["g_nb"], 1)
            pj_all(dve, "odd")
            own.link(dve.memset(AT[:, :, :, :], 0.0))
            dve.tensor_scalar(pj[:, QC:QC + 4, :], pj[:, QC:QC + 4, :], float(P) ** -0.5, None, ALU.mult)
            dve.wait_ge(S["g_l"], 1)
            own.link(dve.scalar_tensor_tensor(flat(E[:, :, :]), flat(cum[:, :, :]), 0.0, flat(E[:, :, :]), ALU.max, ALU.add))
            dve.wait_ge(S["grst"], 48)
            for h in range(H_C):
                own.link(dve.tensor_tensor_scan(cum[:, h, :], rst[:, :], E[:, h, :], 0.0, ALU.mult, ALU.add))
            for l in range(7):
                level_dve(dve, l)
                if l:
                    level_pick(dve, l - 1)
            level_pick(dve, 6)
            dve.wait_ge(S["g_E"], 8)
            level_pick(dve, 7)
            own.link(dve.tensor_tensor(X[0][:, :, :], pj[:, QC:QC + 4, :], E[:, :, :], ALU.mult))
            ch = lambda a: a[:, :, 0:SEQ].rearrange("p h (c t) -> p h c t", t=P)
            sm = lambda a: a[:, :, SAMP0:META0].rearrange("p h (s t) -> p h s t", t=DEC_T)
            dve.tensor_tensor(ch(E), ch(cum), ch(cum)[:, :, :, P - 1:P].to_broadcast([P, H_C, 4, P]), ALU.subtract)
            dve.tensor_tensor(sm(E), sm(cum), sm(cum)[:, :, :, DEC_T - 1:DEC_T].to_broadcast([P, H_C, DEC_B, DEC_T]), ALU.subtract)
            dve.tensor_tensor(E[:, :, META0:N_TOK], cum[:, :, META0:N_TOK],
                              cum[:, :, N_TOK - 1:N_TOK].to_broadcast([P, H_C, N_META]), ALU.subtract).then_inc(S["g_ex"], 1)
            dve.wait_ge(S["g_E"], 9)
            own.link(dve.tensor_tensor(X[1][:, :, :], pj[:, KC:KC + 4, :], E[:, :, :], ALU.mult))
            dve.wait_ge(S["g_el"], 3)
            own.link(dve.memset(gqm[:, :], 0.0))
            own.link(dve.memset(gsq[:, :], 1.0))
            dve.memset(on[:, :, :], 0.0)

        def gla_dve(dve):
            with dve.Fori(0, H_C // 2) as i:
                own.start(i, 20)
                for j in range(2):
                    n = i * 2 + (j + 1)
                    hd = i * 2 + j
                    one_ = lambda a: a.rearrange("p a n -> p (a n)")
                    dve.tensor_scalar(gq[:, :], one_(X[0][:, bass.ds(hd, 1), :]), 1.0, None, ALU.mult)
                    dve.tensor_copy(gk[:, :], one_(X[1][:, bass.ds(hd, 1), :]))
                    dve.tensor_copy(ATh[:, :, :], AT[:, :, bass.ds(hd, 1), :].rearrange("p c h n -> p c (h n)"))
                    dve.tensor_copy(gv[:, :, :], pj[:, bass.ds(i * 4 + (VC + 2 * j), 2), :])
                    dve.tensor_copy(elh[:, :], one_(el[:, bass.ds(hd, 1), :]))
                    own.link(dve.tensor_copy(gos[:, :], god[:, bass.ds(i * 4 + 2 * j, 2)]))
                    dve.tensor_copy(gqm[:, :].rearrange("p (s c) -> p s c", c=52)[:, :, 0:4],
                                    gq[:, SAMP0:META0].rearrange("p (s t) -> p s t", t=DEC_T)).then_inc(S["h_cp"], 1)
                    dve.wait_ge(S["h_tr"], n)
                    dve.tensor_copy(KT[:, 0:4, :], ps[:, 0, :].rearrange("p (c n) -> p c n", n=P))
                    own.link(dve.tensor_copy(KT[0:T4, 4, :], ps[0:T4, 1, 0:P]))
                    dve.tensor_copy(VT[:, 0:2, :], ps[:, 2, :].rearrange("p (c n) -> p c n", n=DV_C))
                    dve.tensor_copy(VT[:, 2:4, :], ps[:, 3, :].rearrange("p (c n) -> p c n", n=DV_C))
                    dve.tensor_copy(VT[0:T4, 4, :], ps[0:T4, 1, P:P + DV_C])
                    dve.tensor_tensor(gkm[:, :, :], KT[0:N_SAMP, 4:5, :].to_broadcast([N_SAMP, DEC_B, P]),
                                      cst[0:N_SAMP, C_SEQM:C_SEQM + DEC_B].rearrange("p (s o) -> p s o", o=1)
                                      .to_broadcast([N_SAMP, DEC_B, P]), ALU.mult).then_inc(S["h_kv"], 1)
                    dve.wait_ge(S["h_kvs"], n)
                    own.link(dve.tensor_copy(Ss[:, 0, :], ps[:, 4, 0:DV_C]))
                    for c in range(4):
                        b, o_ = divmod(c + 1, 2)
                        own.link(dve.scalar_tensor_tensor(Ss[:, c + 1, :], Ss[:, c, :], elh[:, c:c + 1],
                                                          ps[:, 4 + b, o_ * DV_C:(o_ + 1) * DV_C], ALU.mult, ALU.add))
                    dve.tensor_copy(sfin[:, bass.ds(hd, 1), :], Ss[:, 4:5, :]).then_inc(S["h_S"], 1)
                    dve.wait_ge(S["h_t4"], n)
                    for s in range(DEC_B):
                        b, o_ = SKV[s]
                        ins = dve.scalar_tensor_tensor(s0b[:, j, s, :], s0b[:, j, s, :], elh[:, 4 + s:5 + s],
                                                       ps[:, b, o_:o_ + DV_C], ALU.mult, ALU.add)
                    ins.then_inc(S["h_s0"], 1)
                    dve.wait_ge(S["h_rs"], n)
                    for c in range(4):
                        ins = dve.tensor_scalar(on[:, c, :], ps[:, 4 + c // 2, (c % 2) * DV_C:(c % 2 + 1) * DV_C],
                                                grs[:, c:c + 1], None, ALU.mult)
                    dve.tensor_scalar(on[0:T4, 4, :], ps[0:T4, 1, 0:DV_C], grs[0:T4, 4:5], None, ALU.mult)\
                       .then_inc(S["h_y"], 1)
                    dve.wait_ge(S["h_sg"], n)
                    own.link(dve.tensor_tensor(sr[:, :, :], sr[:, :, :], pj[:, bass.ds(i * 4 + (RC + 2 * j), 2), :], ALU.mult))
                    dve.wait_ge(S["h_yt"], n)
                    for b in range(2):
                        blk = one_(pj[:, bass.ds(i * 4 + (VC + 2 * j + b), 1), :])
                        own.link(dve.scalar_tensor_tensor(blk[:, 0:SEQ], ps[:, 6 + b, :], gos[:, b:b + 1], sr[:, b, 0:SEQ],
                                                 ALU.mult, ALU.mult))
                        ins = dve.scalar_tensor_tensor(blk[:, SEQ:N_TOK], ps[:, 0, T4 * b:T4 * b + T4], gos[:, b:b + 1],
                                                       sr[:, b, SEQ:N_TOK], ALU.mult, ALU.mult)
                    ins.then_inc(S["h_mix"], 1)
                    dve.wait_ge(S["h_mix"], n)
                own.end(H_C // 2)

        SKV = [(6, 256), (7, 0), (7, 256), (0, 0), (0, 256), (2, 0), (2, 256), (3, 0)]

        def gla_act(act):
            with act.Fori(0, H_C // 2) as i:
                for j in range(2):
                    n = i * 2 + (j + 1)
                    act.wait_ge(S["h_cp"], n)
                    rr = pj[:, bass.ds(i * 4 + (RC + 2 * j), 2), :]
                    act.activation(sr[:, :, :], rr, ACT.Exp, scale=-1.0).then_inc(S["h_a"], 1)
                    act.wait_ge(S["h_a"], i * 4 + (2 * j + 1))
                    act.activation(sr[:, :, :], sr[:, :, :], ACT.Ln, bias=one[:, 0:1]).then_inc(S["h_a"], 1)
                    act.wait_ge(S["h_a"], i * 4 + (2 * j + 2))
                    act.activation(sr[:, :, :], sr[:, :, :], ACT.Exp, scale=-1.0).then_inc(S["h_sg"], 1)
                    act.wait_ge(S["h_o"], n)
                    for c in range(5):
                        src = ps[:, 4 + c // 2, (c % 2) * DV_C:(c % 2 + 1) * DV_C] if c < 4 else ps[0:T4, 1, 0:DV_C]
                        m = P if c < 4 else T4
                        act.activation(on[0:m, c, :], src, ACT.Square, accum_out=gsq[0:m, c:c + 1]).then_inc(S["h_q"], 1)
                    act.wait_ge(S["h_q"], i * 10 + (5 * j + 5))
                    act.activation(grs[:, :], gsq[:, :], ACT.Ln, bias=eps[:, 0:1], scale=1.0 / DV_C).then_inc(S["h_b"], 1)
                    act.wait_ge(S["h_b"], n)
                    act.activation(grs[:, :], grs[:, :], ACT.Exp, scale=-0.5).then_inc(S["h_rs"], 1)

        def gla_pe(pe):
            with pe.Fori(0, H_C // 2) as i:
                for j in range(2):
                    n = i * 2 + (j + 1)
                    tile = lambda a, c: a[:, P * c:P * c + (P if c < 4 else T4)]
                    pe.wait_ge(S["h_cp"], n)
                    pe.wait_ge(SLD[j], i * 16 + 16)
                    for c in range(4):
                        pe.transpose(ps[:, 0, c * P:(c + 1) * P], tile(gk, c), ident)
                        for b in range(2):
                            pe.transpose(ps[:, 2 + c // 2, (c % 2) * DV_C + b * P:(c % 2) * DV_C + (b + 1) * P],
                                         tile(gv[:, b], c), ident)
                    pe.transpose(ps[0:T4, 1, 0:P], tile(gk, 4), ident)
                    for b in range(2):
                        mm = pe.transpose(ps[0:T4, 1, P + b * P:2 * P + b * P], tile(gv[:, b], 4), ident)
                    mm.then_inc(S["h_tr"], 1)
                    pe.wait_ge(S["h_kv"], n)
                    for s in range(DEC_B):
                        b, o_ = SKV[s]
                        pe.matmul(ps[:, b, o_:o_ + DV_C], gkm[:, s, :], VT[0:N_SAMP, 4, :], start=True, stop=True)
                    pe.matmul(ps[:, 4, 0:DV_C], KT[N_SAMP:T4, 4, :], VT[N_SAMP:T4, 4, :], start=True, stop=True)
                    for c in range(4):
                        b, o_ = divmod(c + 1, 2)
                        mm = pe.matmul(ps[:, 4 + b, o_ * DV_C:(o_ + 1) * DV_C], KT[:, c, :], VT[:, c, :], start=True, stop=True)
                    mm.then_inc(S["h_kvs"], 1)
                    pe.matmul(ps[0:T4, 1, 0:DV_C], ATh[0:T4, 4, 0:T4], VT[0:T4, 4, :], start=True, stop=False)
                    for s in range(DEC_B):
                        mm = pe.matmul(ps[0:T4, 1, 0:DV_C], gqm[:, T4 * s:T4 * s + T4], s0b[:, j, s, :], start=False,
                                       stop=s == DEC_B - 1)
                    mm.then_inc(S["h_t4"], 1)
                    pe.wait_ge(S["h_S"], n)
                    for c in range(4):
                        out = ps[:, 4 + c // 2, (c % 2) * DV_C:(c % 2 + 1) * DV_C]
                        pe.matmul(out, ATh[:, c, :], VT[:, c, :], start=True, stop=False)
                        mm = pe.matmul(out, tile(gq, c), Ss[:, c, :], start=False, stop=True)
                    mm.then_inc(S["h_o"], 1)
                    pe.wait_ge(S["h_y"], n)
                    for b in range(2):
                        for c in range(4):
                            pe.transpose(ps[:, 6 + b, c * P:(c + 1) * P], on[:, c, b * P:(b + 1) * P], ident)
                    for b in range(2):
                        mm = pe.transpose(ps[:, 0, T4 * b:T4 * b + T4], on[0:T4, 4, b * P:(b + 1) * P], ident[0:T4, 0:T4])
                    mm.then_inc(S["h_yt"], 1)

        SLD = [sem("sld0"), sem("sld1")]

        N_CONST, N_OUT = 11, 3
        block = ctx.enter_context(nc.Block())

        @block.sync
        def _(sp_):
            for half in range(2):
                sp_.dma_start(hT[:, 4 * half:4 * half + 4, :], x[:, 4 * half:4 * half + 4, :]).then_inc(S["xld"], 16)
            for dst, src in ((cst[:, :], const), (gn[:, :, :, :], gains), (gev[:, :], g_even), (god[:, :], g_odd),
                             (bgu[:, :], b_gup), (bsb[:, :], b_sb), (bsr[:, :], b_sbrow), (bg[:, :], b_gate),
                             (ptab[:, :], pages), (mst[:, :], m_in), (wg[:, :, :], w_gate)):
                sp_.dma_start(dst, src).then_inc(S["cld"], 16)
            load_pairs(sp_, 0, SLAB0["out0"] + 2)
            sp_.wait_ge(S["cld"], 16 * N_CONST)
            sp_.wait_ge(S["scr_free"], 1)
            load_pages(sp_)
            load_pairs(sp_, SLAB0["out0"] + 2, N_SLABS)
            sp_.wait_ge(S["out"], 16 * N_OUT)

        @block.gpsimd
        def _(pool):
            pool.wait_ge(S["pj_done"], 4 * S_EVEN + CREDIT)
            pool.dma_start(rows[:, R_RST, :], reset[0:H_A, :]).then_inc(S["rst"], 16)
            pool.dma_start(c0[:, :, :, :], c_in).then_inc(S["c0ld"], 16)
            pool.wait_ge(S["pj_act"], 2 * S_EVEN + CREDIT)
            pool.wait_ge(S["pj_dve"], 2 * S_EVEN + CREDIT)
            for b in range(2):
                pool.dma_start(kv_out[:, 4 * b:4 * b + 4, :], pj[:, KBB + 4 * b:KBB + 4 * b + 4, :]).then_inc(S["out"], 16)
            pool.wait_ge(S["gts_ok"], 1)
            pool.dma_start(m_prompt, rows[:, R_M, SEQ - 1:SEQ]).then_inc(S["mout"], 16)
            pool.dma_start(m_sample, mst[:, :]).then_inc(S["mout"], 16)
            pool.wait_ge(S["m_end"], 1)
            pool.dma_start(c_prompt, cfin[:, :, :]).then_inc(S["mout"], 16)
            pool.dma_start(c_sample, c0[:, :, :, :]).then_inc(S["mout"], 16)
            pool.wait_ge(S["mout"], 64)
            pool.sem_inc(S["scr_free"], 2)
            pool.wait_ge(S["n_h"], 2)
            pool.dma_start(wgd[:, :, :], w_gdn).then_inc(S["wgl"], 16)
            pool.dma_start(wgu[:, :], w_gup).then_inc(S["wgl"], 16)
            pool.wait_ge(S["pj_done"], 4 * (PJ0["odd"] + S_ODD) + CREDIT)
            pool.dma_start(rst[:, :], reset).then_inc(S["grst"], 16)
            pool.dma_start(gmk[:, :, :], masks).then_inc(S["grst"], 16)
            pool.dma_start(gm4[:, :, :], masks4).then_inc(S["grst"], 16)
            for j in range(2):
                pool.dma_start(s0b[:, j, :, :], gla_in[j]).then_inc(SLD[j], 16)
            for h in range(H_C):
                pool.wait_ge(S["h_s0"], h + 1)
                pool.dma_start(s_sample[h], s0b[:, h % 2, :, :]).then_inc(S["sst"], 16)
                pool.wait_ge(S["sst"], 16 * h + 16)
                if h + 2 < H_C:
                    pool.dma_start(s0b[:, h % 2, :, :], gla_in[h + 2]).then_inc(SLD[h % 2], 16)
            pool.dma_start(s_prompt.rearrange("h p n -> p h n"), sfin[:, :, :]).then_inc(S["sst"], 16)
            pool.wait_ge(S["sst"], 16 * (H_C + 1))
            pool.sem_inc(S["sfree"], 1)
            pool.wait_ge(S["n_h"], 8)
            pool.dma_start(y_out, hT[:, :, :]).then_inc(S["out"], 16)

        @block.tensor
        def _(pe):
            for name, n in (("lo", 2), ("pj_done", CREDIT), ("pj_act", CREDIT), ("pj_dve", CREDIT), ("dn_done", CREDIT),
                            ("d_dve", CREDIT), ("u_lo", 2), ("kv_used", 2)):
                pe.sem_inc(S[name], n)
            pe.wait_ge(S["cld"], 16 * N_CONST)
            norm_pe(pe, 0)
            gates_pe(pe)
            pe.wait_ge(S["n_lo"], 2)
            proj_pe(pe, "even")
            rows_pe(pe)
            mlstm_pe(pe)
            new_pe(pe)
            attn_pe(pe)
            pe.wait_ge(S["n_lo"], 4)
            proj_pe(pe, "out0")
            norm_pe(pe, 1)
            norm_pe(pe, 2)
            pe.wait_ge(S["n_lo"], 6)
            mlp_pe(pe, 0)
            norm_pe(pe, 3)
            norm_pe(pe, 4)
            gdown_pe(pe)
            pe.wait_ge(S["n_lo"], 8)
            proj_pe(pe, "odd")
            lgate_pe(pe)
            levels_pe(pe)
            gla_pe(pe)
            pe.wait_ge(S["n_lo"], 10)
            proj_pe(pe, "out1")
            norm_pe(pe, 5)
            norm_pe(pe, 6)
            pe.wait_ge(S["n_lo"], 12)
            mlp_pe(pe, 1)
            norm_pe(pe, 7)

        @block.scalar
        def _(act):
            act.wait_ge(S["xld"], 32)
            act.wait_ge(S["cld"], 16 * N_CONST)
            act.wait_ge(S["rows1"], 1)
            split_hi(act, 0, 0)
            norm_act(act, 0, hT, split=0)
            gates_act(act)
            proj_act(act, "even")
            rows_act(act)
            mlstm_act(act)
            new_act(act)
            attn_act(act)
            act.wait_ge(S["a_o"], 8)
            act.wait_ge(S["b_ev"], 8)
            split_mix_act(act, 1, ((0, 0), (QB, 4)))
            proj_act(act, "out0")
            pj_all(act, "out0")
            norm_act(act, 1, pj[:, 0:8, :])
            act.wait_ge(S["n_h"], 2)
            norm_act(act, 2, hT, split=1)
            mlp_act(act, 0)
            act.wait_ge(S["d_dve"], 128 + CREDIT)
            norm_act(act, 3, pj[:, 0:8, :])
            act.wait_ge(S["n_h"], 4)
            norm_act(act, 4, hT, split=2)
            gdown_act(act)
            proj_act(act, "odd")
            lgate_act(act)
            gla_act(act)
            act.wait_ge(S["h_mix"], 4)
            act.wait_ge(S["sfree"], 1)
            split_mix_act(act, 4, ((VC, 0), (VC + 4, 4)))
            proj_act(act, "out1")
            pj_all(act, "out1")
            norm_act(act, 5, pj[:, 0:8, :])
            act.wait_ge(S["n_h"], 6)
            norm_act(act, 6, hT, split=3)
            mlp_act(act, 1)
            act.wait_ge(S["d_dve"], 256 + CREDIT)
            norm_act(act, 7, pj[:, 0:8, :])

        @block.vector
        def _(dve):
            nonlocal own
            own = Own(dve, S["dve"])
            dve.memset(one[:, :], 1.0)
            dve.memset(eps[:, :], EPS)
            dve.wait_ge(S["cld"], 16 * N_CONST)
            dve.tensor_scalar(nbf[:, :], bg[:, 1:2], -1.0, None, ALU.mult).then_inc(S["rows1"], 1)
            split_lo(dve, 0, 0)
            prenorm_dve(dve, 0, 0, 0, 0)
            proj_dve(dve, "even")
            rows_dve(dve)
            mlstm_dve(dve)
            dve.sem_inc(S["m_end"], 1)
            dve.wait_ge(S["scr_free"], 2)
            new_dve(dve)
            attn_dve(dve)
            split_mix_dve(dve, 1, ((0, 0), (QB, 4)))
            proj_dve(dve, "out0")
            postnorm_dve(dve, 1, 0, 1)
            prenorm_dve(dve, 2, 0, 2, 2)
            mlp_dve(dve, 0)
            postnorm_dve(dve, 3, 0, 3)
            prenorm_dve(dve, 4, 1, 0, 3)
            proj_dve(dve, "odd")
            gla_pre_dve(dve)
            gla_dve(dve)
            split_mix_dve(dve, 4, ((VC, 0), (VC + 4, 4)))
            proj_dve(dve, "out1")
            postnorm_dve(dve, 5, 1, 1)
            prenorm_dve(dve, 6, 1, 2, 5)
            mlp_dve(dve, 1)
            postnorm_dve(dve, 7, 1, 3)


_INS = ["x", "weights", "w_gate", "w_gdn", "w_gup", "k_cache", "v_cache", "pages", "c_in", "gla_in", "m_in", "gains",
        "g_even", "g_odd", "b_gate", "b_gup", "b_sb", "b_sbrow", "const", "reset", "masks", "masks4"]
_OUTS = [(P, KB, N_TOK), (P, 8, N_TOK), (P, H_A, P + 1), (P, H_A, DEC_B, P + 1), (H_A, 1), (H_A, DEC_B),
         (H_C, P, DV_C), (H_C, P, DEC_B, DV_C)]


def lay_out(i):
    np_ = lambda a: np.ascontiguousarray(a)
    feat = lambda a: np_(a.reshape(a.shape[0], -1, P).transpose(2, 1, 0))
    col = lambda a: np_(a.reshape(-1, P).T)

    def slabs(w):
        n = w.shape[1]
        return w.reshape(KB, P, n // 256, 2, P).transpose(2, 1, 3, 0, 4).reshape(n // 256, P, SLAB_TILES, P)

    def mlp(up, down):
        u = slabs(up).reshape(MLP_GROUPS, 2, P, SLAB_TILES, P)
        d = down.reshape(MLP_GROUPS, 4, P, 2, 4, P).transpose(0, 3, 2, 4, 1, 5).reshape(MLP_GROUPS, 2, P, SLAB_TILES, P)
        return np.concatenate([u, d], axis=1).reshape(-1, P, SLAB_TILES, P)

    we, wo = i["w_in_even"][0], i["w_in_odd"][0]
    ga = 4 * H_A * P
    tok = np.concatenate([i["x_prompt"][0], i["x_sample"].reshape(N_SAMP, D), i["meta_tokens"]])
    stream = np.concatenate([slabs(np.concatenate([we[:, :ga], we[:, ga + 2 * H_A:]], axis=1)), slabs(i["w_out_even"][0]),
                             mlp(i["w_up"][0], i["w_down"][0]), slabs(wo[:, :3072]), slabs(i["w_out_odd"][0]),
                             mlp(i["w_up"][1], i["w_down"][1])])
    n_pool = i["cache_sb_k"].shape[1]
    return {
        "x": feat(tok),
        "weights": np_(stream),
        "w_gate": np_(we[:, ga:ga + 2 * H_A].reshape(KB, P, 2 * H_A).transpose(1, 0, 2)),
        "w_gdn": np_(wo[:, 3072:].reshape(KB, P, 16).transpose(1, 0, 2)),
        "w_gup": np_(i["w_gate_up_odd"][0]),
        "k_cache": np_(i["cache_sb_k"][0].reshape(n_pool, P, 4, P).transpose(0, 3, 2, 1).reshape(n_pool, P, 512)),
        "v_cache": np_(i["cache_sb_v"][0].reshape(n_pool, P, 512)),
        "pages": np_(i["page_table"].reshape(1, -1)),
        "c_in": np_(np.concatenate([i["state_mlstm_c"][0], i["state_mlstm_n"][0][..., None]], axis=-1).transpose(2, 1, 0, 3)),
        "gla_in": np_(i["state_gla_s"][0].transpose(1, 2, 0, 3)),
        "m_in": np_(i["state_mlstm_m"][0].T),
        "gains": np_(i["norm_gains"].reshape(2, 4, KB, P).transpose(3, 0, 1, 2)),
        "g_even": col(i["g_head_even"][0]),
        "g_odd": col(i["g_head_odd"][0]),
        "b_gate": np_(i["b_gate_even"][0].reshape(2, H_A).T),
        "b_gup": col(i["b_gate_up_odd"][0]),
        "b_sb": np_(np.broadcast_to(i["b_sb_even"][0], (P, H_B))),
        "b_sbrow": np_(np.broadcast_to(np.repeat(i["b_sb_even"][0], DEC_T), (P, 32))),
        "const": constants(),
        "reset": reset_row(),
        "masks": level_masks(P, np.zeros(P, int), (64, 32, 16, 8, 4, 2, 1, 0)),
        "masks4": level_masks(T4, (np.arange(T4) < N_SAMP).astype(int), (8, 4, 2, 1, 0)),
    }


def kernel(**inputs):
    import concourse.bacc as _bacc
    from concourse.bass_utils import run_bass_kernel_spmd as _run

    laid = lay_out({k: np.asarray(v) for k, v in inputs.items()})
    nc = _bacc.Bacc("TRN2", target_bir_lowering=False, num_devices=1)
    arrays, args = {}, []
    for name in _INS:
        arrays[f"in_{name}_dram"] = laid[name]
        args.append(nc.dram_tensor(f"in_{name}_dram", laid[name].shape, mybir.dt.from_np(laid[name].dtype),
                                   kind="ExternalInput").ap())
    for i, shape in enumerate(_OUTS):
        args.append(nc.dram_tensor(f"out_{i}_dram", shape, mybir.dt.float32, kind="ExternalOutput").ap())
    build(nc, *args)
    r = _run(nc, [arrays], core_ids=[0])
    y, kv, cp, cs, mp, ms, sp, ss = (r.results[0][f"out_{i}_dram"] for i in range(len(_OUTS)))
    rows = lambda a: a.transpose(2, 1, 0).reshape(N_TOK, -1)
    y, k, v = rows(y), rows(kv[:, 0:4]), rows(kv[:, 4:8])
    prompt = lambda a: np.concatenate([a[META0:], a[:SEQ]]).reshape(1, 1, N_META + SEQ, H_B, DH_B)
    samp = lambda a: a[SAMP0:META0].reshape(1, DEC_B, DEC_T, H_B, DH_B)
    cp, cs = cp.transpose(1, 0, 2), cs.transpose(2, 1, 0, 3)
    out = (y[:SEQ].reshape(1, SEQ, D), y[SAMP0:META0].reshape(DEC_B, DEC_T, D), prompt(k), prompt(v),
           cp[None, None, :, :, :P], cp[None, None, :, :, P], mp.reshape(1, 1, H_A), sp[None, None],
           samp(k), samp(v), cs[None, :, :, :, :P], cs[None, :, :, :, P], ms.T[None], ss.transpose(2, 0, 1, 3)[None])
    return tuple(np.ascontiguousarray(o) for o in out)
```

```python
from contextlib import ExitStack

import numpy as np

import concourse.bass as bass
from concourse import mybir

D = 1024
P = 128
KB = D // P
SEQ, N_META, DEC_B, DEC_T = 512, 16, 8, 4
N_SAMP = DEC_B * DEC_T
N_TOK = SEQ + N_SAMP + N_META
HALF = N_TOK // 2
N_TILE = SEQ // P
SAMP0, META0 = SEQ, SEQ + N_SAMP
T4 = N_SAMP + N_META
H_A, H_B, H_C = 4, 8, 4
DH_B = 64
DV_C = 256
N_PAGES = 16
D_FF = 4 * D
EPS = 1e-6
N_EVEN_BLK = 28
QA, KA, VA, OA, QB, KBB, VB = range(0, 28, 4)
N_ODD_BLK = 24
QC, KC, VC, RC = 0, 4, 8, 16
SLAB_TILES = 16
SLAB = SLAB_TILES * P
MLP_GROUPS = D_FF // 512
S_EVEN, S_OUT, S_MLP, S_ODD = 14, 4, 4 * MLP_GROUPS, 12
SLAB0 = {"even": 0, "out0": 14, "mlp0": 18, "odd": 50, "out1": 62, "mlp1": 66}
N_SLABS = 98
NEG = -1e30

C_ID, C_ONE, C_U, C_NEG, C_NEG4, C_SBM, C_SEL, C_SEQM = 0, 128, 256, 384, 512, 560, 688, 1200
C_NEWM = 1208
C_HEAD, C_QRY = C_NEWM + 32, C_NEWM + 40
C_END = C_QRY + DEC_T


def constants():
    c = np.zeros((P, C_END), np.float32)
    i = np.arange(P)
    c[:, C_ID:C_ID + P] = i[:, None] == i[None, :]
    c[:, C_ONE:C_ONE + P] = 1
    c[:, C_U:C_U + P] = i[:, None] > i[None, :]
    c[:, C_NEG:C_NEG + P] = np.where(i[:, None] <= i[None, :], 0, NEG)
    grp = np.where(i[:T4] < N_SAMP, i[:T4] // DEC_T, DEC_B)
    same = (grp[:, None] == grp[None, :]) & (i[:T4, None] <= i[None, :T4])
    c[:T4, C_NEG4:C_NEG4 + T4] = np.where(same, 0, NEG)
    c[:, C_SBM:C_SBM + P] = i[:, None] < i[None, :]
    for h in range(H_A):
        c[h, C_SEL + h * P:C_SEL + (h + 1) * P] = 1
    c[:N_SAMP, C_SEQM:C_SEQM + DEC_B] = (i[:N_SAMP, None] // DEC_T) == np.arange(DEC_B)[None, :]
    c[:N_SAMP, C_NEWM:C_NEWM + N_SAMP] = same[:N_SAMP, :N_SAMP] & (i[:N_SAMP, None] < i[None, :N_SAMP])
    c[:N_SAMP, C_HEAD:C_HEAD + H_B] = (i[:N_SAMP, None] // DEC_T) == np.arange(H_B)[None, :]
    c[:N_SAMP, C_QRY:C_QRY + DEC_T] = (i[:N_SAMP, None] % DEC_T) == np.arange(DEC_T)[None, :]
    return c


def reset_row():
    r = np.ones((P, N_TOK), np.float32)
    r[:, 0:SEQ:P] = 0
    r[:, SAMP0:META0:DEC_T] = 0
    r[:, META0] = 0
    return r


def level_masks(n, decode, levels):
    i = np.arange(n)
    out = np.zeros((n, len(levels), n), np.int32)
    for a, w in enumerate(levels):
        m = i[:, None] == i[None, :]
        if w:
            m = (i[:, None] // (2 * w) == i[None, :] // (2 * w)) & (i[:, None] % (2 * w) < w) & (i[None, :] % (2 * w) >= w)
            if 2 * w > DEC_T:
                m &= (decode[:, None] == 0) & (decode[None, :] == 0)
        out[:, a, :] = m
    return out


class Own:

    def __init__(self, eng, sem):
        self.eng, self.sem, self.n, self.loop, self.per = eng, sem, 0, 0, 0

    def link(self, ins):
        self.n += 1
        ins.then_inc(self.sem, 1)
        self.eng.wait_ge(self.sem, self.loop + self.n)

    def start(self, i, per):
        self.loop, self.per, self.n0 = i * per, per, self.n

    def end(self, trips):
        assert self.n - self.n0 == self.per, f"steps per iteration: {self.n - self.n0}"
        self.n, self.loop = self.n0 + trips * self.per, 0



def build(nc, x, weights, w_gate, w_gdn, w_gup, k_cache, v_cache, pages, c_in, gla_in, m_in, gains, g_even, g_odd,
          b_gate, b_gup, b_sb, b_sbrow, b_sbcol, const, reset, masks, masks4,
          y_out, kv_out, c_prompt, c_sample, m_prompt, m_sample, s_prompt, s_sample):
    f32, f32r, i32 = mybir.dt.float32, mybir.dt.float32r, mybir.dt.int32
    ALU, ACT = mybir.AluOpType, mybir.ActivationFunctionType
    ctx = ExitStack()
    with ctx:
        sbuf0 = (nc.sbuf_base + 63) // 64 * 64

        def at(name, off, shape, dt=f32):
            return nc.alloc_sbuf_tensor_at(name, shape, dt, offset=sbuf0 + off)

        def sem(name):
            return ctx.enter_context(nc.semaphore(name))

        ROW = N_TOK * 4
        o_hT = 0
        o_M = o_hT + KB * ROW
        o_xn = o_M + 24 * ROW
        o_raw = o_xn + KB * ROW
        o_hi = o_raw + 2 * SLAB * 4
        o_lo = o_hi + 2 * SLAB * 4
        o_pj = o_lo + 2 * SLAB * 4
        o_c = o_pj + N_EVEN_BLK * ROW
        o_s = o_c + (C_END * 4 + 31) // 32 * 32
        hT = at("hT", o_hT, [P, KB, N_TOK])
        xhi = at("xhi", o_M, [P, KB, N_TOK], f32r)
        xlo = at("xlo", o_M + KB * ROW, [P, KB, N_TOK], f32r)
        dhi = at("dhi", o_M + 16 * ROW, [P, 4, N_TOK], f32r)
        dlo = at("dlo", o_M + 20 * ROW, [P, 4, N_TOK], f32r)
        xn = at("xn", o_xn, [P, KB, N_TOK])
        raw = at("raw", o_raw, [P, 2, SLAB_TILES, P])
        whi = at("whi", o_hi, [P, 2, SLAB_TILES, P], f32r)
        wlo = at("wlo", o_lo, [P, 2, SLAB_TILES, P], f32r)
        pj = at("pj", o_pj, [P, N_EVEN_BLK, N_TOK])
        relu = at("relu", o_pj + 24 * ROW, [P, 2, HALF])
        rsq = at("rsq", o_pj + 25 * ROW, [P, 2, HALF])
        rstd = at("rstd", o_pj + 26 * ROW, [P, 2, HALF])
        cst = at("cst", o_c, [P, C_END])
        gn = at("gn", o_s, [P, 2, 4, KB])
        gev = at("gev", o_s + 256, [P, H_A])
        god = at("god", o_s + 288, [P, 8])
        bgu = at("bgu", o_s + 320, [P, H_C])
        bsb = at("bsb", o_s + 352, [P, H_B])
        bsr = at("bsr", o_s + 384, [P, 32])
        bg = at("bg", o_s + 512, [H_A, 2])
        nbf = at("nbf", o_s + 544, [H_A, 1])
        one_eps = at("one_eps", o_s + 576, [P, 2])
        one, eps = one_eps[:, 0:1], one_eps[:, 1:2]
        bcol = at("bcol", o_s + 608, [P, 1])
        ptab = at("ptab", o_s + 640, [1, P], i32)
        mst = at("mst", o_s + 1152, [H_A, DEC_B])
        grow = at("grow", o_s + 1184, [H_A, 2, N_TOK])
        assert sbuf0 + o_s + 1184 + 2 * ROW <= nc.sbuf_usable_end
        ident = cst[:, C_ID:C_ID + P]
        ones = cst[:, C_ONE:C_ONE + P]
        after = cst[:, C_U:C_U + P]
        strict = cst[:, C_SBM:C_SBM + P]

        ps = ctx.enter_context(nc.psum_tensor("ps", [P, 8, 512], f32))

        wg = at("wg", o_pj, [P, KB, 8])
        rows = at("rows", o_M, [H_A, 9, N_TOK])
        R_RST, R_LF, R_B, R_M, R_RM, R_W, R_A, R_WK, R_T = range(9)
        o = o_M + 9 * ROW
        gts = at("gts", o, [P, 5, 16]); o += 320
        ext = at("ext", o, [H_A, 3, DEC_B, 5]); o += 512
        gh = at("gh", o, [P, 5, 4]); o += 96
        wdh = at("wdh", o, [P, 12]); o += 64
        ghc = at("ghc", o, [P, 1]); o += 32
        den = at("den", o, [P, 5]); o += 32
        rec = at("rec", o, [P, 5]); o += 32
        ssq = at("ssq", o, [P, 5]); o += 32
        rs5 = at("rs5", o, [P, 5]); o += 32
        selh = at("selh", o, [H_A, P]); o += 512
        qkv = at("qkv", o, [P, 3, N_TOK]); o += 3 * ROW
        kw = at("kw", o, [P, 5, P]); o += 2560
        vx = at("vx", o, [P, 5, P + 1]); o += 2624
        dec = at("dec", o, [P, N_TOK]); o += ROW
        sT = at("sT", o, [P, N_TOK]); o += ROW
        Cs = at("Cs", o, [P, 5, P + 1]); o += 2624
        qm = at("qm", o, [P, 288]); o += 1152
        hx = at("hx", o, [P, 5, P + 1]); o += 2624
        hn = at("hn", o, [P, 5, P]); o += 2560
        kwm = at("kwm", o, [N_SAMP, DEC_B, P]); o += 4096
        so = at("so", o_s + 1184, [P, N_TOK])
        cfin = at("cfin", o, [P, H_A, P + 1]); o += 2080
        assert o <= o_xn
        c0 = at("c0", o_xn, [P, H_A, DEC_B, P + 1])

        PG = N_PAGES // 4
        GB = PG * 4 * P * 4
        ROWN = 4 * DEC_B
        kbuf = [at(f"kbuf{g}", (o_hi + GB, o_lo + GB, o_M, o_M + GB)[g], [P, PG, 4, P]) for g in range(4)]
        vbuf = [at(f"vbuf{g}", o_M + (2 + g) * GB, [P, PG, 4 * P]) for g in range(4)]
        o = o_M + 6 * GB
        qbd = at("qbd", o, [P, 4, DEC_B, 8]); o += 1024
        zn = at("zn", o, [N_SAMP, 256]); o += 1024
        ln_ = at("ln_", o, [N_SAMP, 256]); o += 1024
        spn = at("spn", o, [N_SAMP, 256]); o += 1024
        assert o <= o_xn
        o = o_raw
        zg = at("zg", o, [P, N_PAGES, ROWN]); o += 2048
        lg = at("lg", o, [P, 2, N_PAGES, ROWN]); o += 4096
        osn = at("osn", o, [P, 256]); o += 1024
        qs = at("qs", o, [P, 4, 40]); o += 640
        assert o <= o_raw + SLAB * 4
        o = o_pj + 4 * ROW
        WZ = 1280
        WA = WZ + SEQ + N_META
        z = at("z", o, [P, WA]); o += 4 * WA
        lz = at("lz", o, [P, WA]); o += 4 * WA
        sp = at("sp", o, [P, WA]); o += 4 * WA
        qz = at("qz", o, [P, 2, N_TOK]); o += 2 * ROW
        assert o <= o_pj + 16 * ROW
        o = o_xn
        kP = at("kP", o, [P, N_TOK]); o += ROW
        vF = at("vF", o, [P, N_TOK]); o += ROW
        vP = at("vP", o, [P, 5, P]); o += 2560
        vnew = at("vnew", o, [N_SAMP, 4, P])
        outm = at("outm", o, [ROWN, 4 * P]); o += 2048
        zr = at("zr", o, [P, PG * P]); o += 2048
        sg = at("sg", o, [P, ROWN, 1 + N_PAGES]); o += 2176
        ssg = at("ssg", o, [P, ROWN, 1 + N_PAGES]); o += 2176
        smk = at("smk", o, [P, ROWN, 1 + N_PAGES]); o += 2176
        bh = at("bh", o, [P, 2]); o += 32
        assert o <= o_raw
        KOFF = [0, 512, 896, 1152]

        own = None
        NAMES = """scr_free mout xld cld out hi lo used pj_done pj_act pj_dve gate gate_ev up_done dn_done
            u_act u_hi u_lo d_dve n_sq n_ss n_rs n_xn n_hi n_lo n_h dve act rst rows1 rows2 gt gts_ok
            m_cp m_tr m_bc m_qk m_si m_kv m_qm m_D m_so m_S m_kvs m_in m_C m_it m_hn m_rs m_y m_yt m_end
            a_in a_q a_z a_l a_sp a_A a_t a_w a_v a_o b_pt k_used v_used b_z b_zr b_q b_om b_o b_l b_sp b_A b_t b_w b_pv b_ev
            v_tr v_ev r_a r_e c0ld m_a m_sq d_q d_z d_sp d_A d_w d_o d_zs d_l d_t d_e a_x a_x2 a_e b_x wgl gd_ps gd_ok g_lg g_nb g_a g_l g_ex g_E g_el g_x g_p g_c grst h_cp h_tr h_kv h_kvs h_S h_t4 h_s0 h_rs h_y h_yt h_mix h_a h_sg h_o h_q h_b sst sfree
            """.split()
        S = {n: sem(n) for n in NAMES}

        def expv(act, out, in_, **k):
            return act.activation(out, in_, ACT.Exp, **k)

        RAW = [sem("raw0"), sem("raw1")]
        CREDIT = 16

        def load_pairs(sp_, first, last):
            with sp_.Fori(first // 2, last // 2) as i:
                for par in range(2):
                    sp_.wait_ge(S["lo"], i * 2 + (par + 1))
                    sp_.dma_start(raw[:, par], weights[bass.ds(i * 2 + par, 1), :, :, :]
                                  .rearrange("a p t c -> (a p) t c")).then_inc(RAW[par], 16)

        def split_hi(act, half_s, par):
            act.wait_ge(RAW[par], half_s * 16 + 16)
            act.activation(whi[:, par], raw[:, par], ACT.Copy).then_inc(S["hi"], 1)

        def split_lo(dve, half_s, par):
            dve.wait_ge(S["hi"], half_s * 2 + (par + 1))
            dve.tensor_tensor(wlo[:, par], raw[:, par], whi[:, par].bitcast(f32), ALU.subtract).then_inc(S["lo"], 1)

        def product(pe, out, par, t, hi, lo, first, last):
            pe.matmul(out, whi[:, par, t, :], hi, start=first, stop=False)
            pe.matmul(out, whi[:, par, t, :], lo, start=False, stop=False)
            return pe.matmul(out, wlo[:, par, t, :], hi, start=False, stop=last)

        NS = {"even": S_EVEN, "out0": S_OUT, "odd": S_ODD, "out1": S_OUT}
        PJ0 = {"even": 0, "out0": S_EVEN, "odd": S_EVEN + S_OUT, "out1": S_EVEN + S_OUT + S_ODD}
        COLS = [slice(0, HALF), slice(HALF, N_TOK)]

        def proj_pe(pe, name):
            s0, n0 = SLAB0[name], PJ0[name]
            with pe.Fori(0, NS[name] // 2) as i:
                for par in range(2):
                    pe.wait_ge(S["lo"], i * 2 + (s0 + par + 3))
                    for f in range(2):
                        for h in range(2):
                            bank = 4 * par + 2 * f + h
                            pe.wait_ge(S[("pj_act", "pj_dve")[h]], i * 4 + (2 * n0 + 2 * par + f + 1 + CREDIT - 4))
                            for k in range(KB):
                                mm = product(pe, ps[:, bank, 0:HALF], par, f * KB + k, xhi[:, k, COLS[h]],
                                             xlo[:, k, COLS[h]], k == 0, k == KB - 1)
                            mm.then_inc(S["pj_done"], 1)

        def proj_act(act, name):
            s0, n0 = SLAB0[name], PJ0[name]
            with act.Fori(0, NS[name] // 2) as i:
                for par in range(2):
                    act.wait_ge(S["pj_done"], i * 8 + (4 * (n0 + par) + CREDIT))
                    split_hi(act, i + (s0 + par + 1) // 2, 1 - par)
                    for f in range(2):
                        act.wait_ge(S["pj_done"], i * 8 + (4 * (n0 + par) + 2 * f + 1 + CREDIT))
                        act.activation(pj[:, bass.ds(i * 4 + (2 * par + f), 1), COLS[0]], ps[:, 4 * par + 2 * f, 0:HALF],
                                       ACT.Copy).then_inc(S["pj_act"], 1)

        def proj_dve(dve, name):
            s0, n0 = SLAB0[name], PJ0[name]
            with dve.Fori(0, NS[name] // 2) as i:
                for par in range(2):
                    split_lo(dve, i + (s0 + par + 1) // 2, 1 - par)
                    for f in range(2):
                        dve.wait_ge(S["pj_done"], i * 8 + (4 * (n0 + par) + 2 * f + 2 + CREDIT))
                        dve.tensor_copy(pj[:, bass.ds(i * 4 + (2 * par + f), 1), COLS[1]],
                                        ps[:, 4 * par + 2 * f + 1, 0:HALF]).then_inc(S["pj_dve"], 1)

        def pj_all(eng, name):
            n = 2 * (PJ0[name] + NS[name]) + CREDIT
            eng.wait_ge(S["pj_act"], n)
            eng.wait_ge(S["pj_dve"], n)

        def mlp_pe(pe, L):
            s0, d0, u0 = SLAB0[f"mlp{L}"], 128 * L + CREDIT, 64 * L
            with pe.Fori(0, MLP_GROUPS) as g:
                for par in range(2):
                    pe.wait_ge(S["lo"], g * 4 + (s0 + par + 3))
                    for f in range(2):
                        for h in range(2):
                            j = 4 * par + 2 * f + h
                            pe.wait_ge(S["d_dve"], g * 16 + (d0 - 8 + j + 1))
                            for k in range(KB):
                                mm = product(pe, ps[:, j, 0:HALF], par, f * KB + k, xhi[:, k, COLS[h]],
                                             xlo[:, k, COLS[h]], k == 0, k == KB - 1)
                            mm.then_inc(S["up_done"], 1)
                for par in range(2):
                    pe.wait_ge(S["lo"], g * 4 + (s0 + par + 5))
                    for h in range(2):
                        if par == 0:
                            pe.wait_ge(S["u_lo"], g * 8 + (u0 + 9 + h))
                        for d in range(4):
                            j = 4 * h + d
                            if par == 0:
                                pe.wait_ge(S["u_act"], g * 8 + (u0 + j + 1))
                            else:
                                pe.wait_ge(S["d_dve"], g * 16 + (d0 + j + 1))
                            for k in range(4):
                                mm = product(pe, ps[:, j, 0:HALF], par, d * 4 + k, dhi[:, k, COLS[h]],
                                             dlo[:, k, COLS[h]], k == 0, k == 3)
                            mm.then_inc(S["dn_done"], 1)

        def mlp_act(act, L):
            s0, d0, u0 = SLAB0[f"mlp{L}"], 128 * L + CREDIT, 64 * L

            def group(g, last=False):
                for par in range(2):
                    if par == 0:
                        act.wait_ge(S["dn_done"], g * 16 + d0)
                    else:
                        act.wait_ge(S["up_done"], g * 8 + (u0 + 4))
                    split_hi(act, g * 2 + (s0 + par + 1) // 2, 1 - par)
                    for f in range(2):
                        for h in range(2):
                            j = 4 * par + 2 * f + h
                            act.wait_ge(S["up_done"], g * 8 + (u0 + j + 1))
                            act.wait_ge(S["u_lo"], g * 8 + (u0 + j + 1))
                            act.activation(relu[:, h], ps[:, j, 0:HALF], ACT.Relu).then_inc(S["u_act"], 1)
                            act.wait_ge(S["u_act"], g * 8 + (u0 + j + 1))
                            act.activation(dhi[:, 2 * par + f, COLS[h]], relu[:, h], ACT.Square).then_inc(S["u_hi"], 1)
                act.wait_ge(S["up_done"], g * 8 + (u0 + 8))
                split_hi(act, g * 2 + (s0 + 2) // 2, 1)
                if not last:
                    act.wait_ge(S["dn_done"], g * 16 + (d0 + 8))
                    split_hi(act, g * 2 + (s0 + 4) // 2, 0)
            with act.Fori(0, MLP_GROUPS - L) as g:
                group(g)
            if L:
                group(MLP_GROUPS - 1, last=True)

        def mlp_dve(dve, L):
            s0, d0, u0 = SLAB0[f"mlp{L}"], 128 * L + CREDIT, 64 * L
            own.link(dve.memset(pj[:, 0:8, :], 0.0))

            def group(g, last=False):
                for par in range(2):
                    split_lo(dve, g * 2 + (s0 + par + 1) // 2, 1 - par)
                    for f in range(2):
                        for h in range(2):
                            j = 4 * par + 2 * f + h
                            dve.wait_ge(S["u_hi"], g * 8 + (u0 + j + 1))
                            own.link(dve.tensor_tensor(rsq[:, h], relu[:, h], relu[:, h], ALU.mult))
                            dve.tensor_tensor(dlo[:, 2 * par + f, COLS[h]], rsq[:, h],
                                              dhi[:, 2 * par + f, COLS[h]].bitcast(f32), ALU.subtract)\
                               .then_inc(S["u_lo"], 1)
                split_lo(dve, g * 2 + (s0 + 2) // 2, 1)
                for par in range(2):
                    if par == 1 and not last:
                        split_lo(dve, g * 2 + (s0 + 4) // 2, 0)
                    for h in range(2):
                        for d in range(4):
                            dve.wait_ge(S["dn_done"], g * 16 + (d0 + 8 * par + 4 * h + d + 1))
                            y = pj[:, 4 * par + d, COLS[h]]
                            dve.tensor_tensor(y, ps[:, 4 * h + d, 0:HALF], y, ALU.add).then_inc(S["d_dve"], 1)
            with dve.Fori(0, MLP_GROUPS - L) as g:
                own.start(g, 8)
                group(g)
                own.end(MLP_GROUPS - L)
            if L:
                group(MLP_GROUPS - 1, last=True)

        def norm_act(act, n, src, split=None):
            for h in range(2):
                m = 2 * n + h
                act.activation(xn[:, :, COLS[h]], src[:, :, COLS[h]], ACT.Square).then_inc(S["n_sq"], 1)
            for h in range(2):
                m = 2 * n + h
                act.wait_ge(S["n_ss"], m + 1)
                act.activation(rstd[:, h], ps[:, h, 0:HALF], ACT.Ln, bias=eps[:, 0:1], scale=1.0 / D)\
                   .then_inc(S["act"], 1)
                act.wait_ge(S["act"], m + 1)
                act.activation(rstd[:, h], rstd[:, h], ACT.Exp, scale=-0.5).then_inc(S["n_rs"], 1)
            if split is not None:
                for h in range(2):
                    act.wait_ge(S["n_xn"], 2 * split + h + 1)
                    act.activation(xhi[:, :, COLS[h]], xn[:, :, COLS[h]], ACT.Copy).then_inc(S["n_hi"], 1)

        def norm_pe(pe, n):
            for h in range(2):
                pe.wait_ge(S["n_sq"], 2 * n + h + 1)
                for k in range(KB):
                    mm = pe.matmul(ps[:, h, 0:HALF], ones, xn[:, k, COLS[h]], start=k == 0, stop=k == KB - 1)
                mm.then_inc(S["n_ss"], 1)

        def prenorm_dve(dve, n, L, g, q):
            for h in range(2):
                dve.wait_ge(S["n_rs"], 2 * n + h + 1)
                for k in range(KB):
                    ins = dve.scalar_tensor_tensor(xn[:, k, COLS[h]], hT[:, k, COLS[h]], gn[:, L, g, k:k + 1],
                                                   rstd[:, h], ALU.mult, ALU.mult)
                ins.then_inc(S["n_xn"], 1)
            split_x(dve, q)

        def split_x(dve, q):
            for h in range(2):
                dve.wait_ge(S["n_hi"], 2 * q + h + 1)
                dve.tensor_tensor(xlo[:, :, COLS[h]], xn[:, :, COLS[h]], xhi[:, :, COLS[h]].bitcast(f32), ALU.subtract)\
                   .then_inc(S["n_lo"], 1)

        def postnorm_dve(dve, n, L, g):
            for h in range(2):
                dve.wait_ge(S["n_rs"], 2 * n + h + 1)
                for k in range(KB):
                    ins = dve.scalar_tensor_tensor(xn[:, k, COLS[h]], pj[:, k, COLS[h]], gn[:, L, g, k:k + 1],
                                                   rstd[:, h], ALU.mult, ALU.mult)
                own.link(ins)
                dve.tensor_tensor(hT[:, :, COLS[h]], hT[:, :, COLS[h]], xn[:, :, COLS[h]], ALU.add).then_inc(S["n_h"], 1)

        def split_mix_act(act, q, parts):
            for src, dst in parts:
                act.activation(xhi[:, dst:dst + 4, :], pj[:, src:src + 4, :], ACT.Copy).then_inc(S["n_hi"], 1)

        def split_mix_dve(dve, q, parts):
            for j, (src, dst) in enumerate(parts):
                dve.wait_ge(S["n_hi"], 2 * q + j + 1)
                dve.tensor_tensor(xlo[:, dst:dst + 4, :], pj[:, src:src + 4, :], xhi[:, dst:dst + 4, :].bitcast(f32),
                                  ALU.subtract).then_inc(S["n_lo"], 1)

        def gates_pe(pe):
            pe.wait_ge(S["n_xn"], 2)
            pe.wait_ge(S["cld"], 16 * N_CONST)
            for q in range(2):
                for h in range(2):
                    for k in range(KB):
                        mm = pe.matmul(ps[0:H_A, 4 + 2 * q + h, 0:HALF], wg[:, k, 4 * q:4 * q + 4], xn[:, k, COLS[h]],
                                       start=k == 0, stop=k == KB - 1)
            mm.then_inc(S["gate"], 1)
            pe.wait_ge(S["gate_ev"], 4)

        def gates_act(act):
            act.wait_ge(S["gate"], 1)
            act.wait_ge(S["rows1"], 1)
            for h in range(2):
                act.activation(grow[:, 0, COLS[h]], ps[0:H_A, 4 + h, 0:HALF], ACT.Identity, bias=bg[:, 0:1])\
                   .then_inc(S["gate_ev"], 1)
                act.activation(grow[:, 1, COLS[h]], ps[0:H_A, 6 + h, 0:HALF], ACT.Identity, bias=nbf[:, 0:1], scale=-1.0)\
                   .then_inc(S["gate_ev"], 1)

        def rows_act(act):
            pj_all(act, "even")
            t = rows[:, R_T, :]
            for k, (src, fn, kw_) in enumerate(((grow[:, 1, :], ACT.Abs, {}), (t, ACT.Exp, {"scale": -1.0}),
                                                (t, ACT.Ln, {"bias": one[0:H_A, 0:1]}))):
                act.activation(t, src, fn, **kw_).then_inc(S["r_a"], 1)
                act.wait_ge(S["r_a"], k + 1)
            act.wait_ge(S["rows2"], 1)
            for r in (R_W, R_WK, R_T):
                act.activation(rows[:, r, :], rows[:, r, :], ACT.Exp, scale=-1.0 if r == R_T else 1.0)\
                   .then_inc(S["r_e"], 1)

        def rows_dve(dve):
            R = lambda k: rows[:, k, :]
            dve.wait_ge(S["r_a"], 3)
            dve.wait_ge(S["rst"], 16)
            own.link(dve.scalar_tensor_tensor(R(R_LF), grow[:, 1, :], 0.0, R(R_T), ALU.max, ALU.add))
            own.link(dve.tensor_scalar(R(R_LF), R(R_LF), -1.0, None, ALU.mult))
            own.link(dve.tensor_tensor_scan(R(R_B), R(R_RST), R(R_LF), 0.0, ALU.mult, ALU.add))
            gi = grow[:, 0, :]
            own.link(dve.tensor_tensor_scan(rows[:, R_M, META0:N_TOK], rows[:, R_LF, META0:N_TOK], gi[:, META0:N_TOK],
                                            0.0, ALU.add, ALU.max))
            own.link(dve.tensor_tensor_scan(rows[:, R_M, 0:SEQ], rows[:, R_LF, 0:SEQ], gi[:, 0:SEQ],
                                            rows[:, R_M, N_TOK - 1:N_TOK], ALU.add, ALU.max))
            dve.memset(ext[:, 0], NEG)
            own.link(dve.tensor_copy(ext[:, 1, :, 0:1], mst[:, :].rearrange("p (s o) -> p s o", o=1)))
            own.link(dve.tensor_copy(ext[:, 0, :, 1:5],
                                     rows[:, R_LF, SAMP0:META0].rearrange("p (s t) -> p s t", t=DEC_T)))
            own.link(dve.tensor_copy(ext[:, 1, :, 1:5], gi[:, SAMP0:META0].rearrange("p (s t) -> p s t", t=DEC_T)))
            own.link(dve.tensor_tensor_scan(ext[:, 2].rearrange("p s t -> p (s t)"), ext[:, 0].rearrange("p s t -> p (s t)"),
                                            ext[:, 1].rearrange("p s t -> p (s t)"), 0.0, ALU.add, ALU.max))
            own.link(dve.tensor_copy(rows[:, R_M, SAMP0:META0].rearrange("p (s t) -> p s t", t=DEC_T), ext[:, 2, :, 1:5]))
            own.link(dve.tensor_tensor(R(R_RM), R(R_B), R(R_M), ALU.subtract))
            own.link(dve.tensor_tensor(R(R_A), gi, R(R_B), ALU.subtract))
            own.link(dve.memset(rows[:, R_W, META0:N_TOK], 0.0))
            own.link(dve.tensor_copy(rows[:, R_W, 0:P], rows[:, R_M, N_TOK - 1:N_TOK].to_broadcast([H_A, P])))
            chunk = lambda r, a, b: rows[:, r, a:b].rearrange("p (c t) -> p c t", t=P)
            own.link(dve.tensor_copy(chunk(R_W, P, SEQ), chunk(R_M, 0, SEQ - P)[:, :, P - 1:P].to_broadcast([H_A, 3, P])))
            samp = lambda r: rows[:, r, SAMP0:META0].rearrange("p (s t) -> p s t", t=DEC_T)
            own.link(dve.tensor_copy(samp(R_W), ext[:, 2, :, 0:1].to_broadcast([H_A, DEC_B, DEC_T])))
            own.link(dve.tensor_tensor(R(R_W), R(R_W), R(R_RM), ALU.add))
            own.link(dve.tensor_copy(chunk(R_WK, 0, SEQ), chunk(R_RM, 0, SEQ)[:, :, P - 1:P].to_broadcast([H_A, 4, P])))
            own.link(dve.tensor_copy(samp(R_WK), samp(R_RM)[:, :, DEC_T - 1:DEC_T].to_broadcast([H_A, DEC_B, DEC_T])))
            own.link(dve.tensor_copy(rows[:, R_WK, META0:N_TOK], rows[:, R_RM, N_TOK - 1:N_TOK].to_broadcast([H_A, N_META])))
            own.link(dve.tensor_tensor(R(R_WK), R(R_WK), R(R_A), ALU.add))
            dve.tensor_copy(R(R_T), R(R_M)).then_inc(S["rows2"], 1)
            own.link(dve.memset(gts[:, :, :], 1.0))
            dve.wait_ge(S["gt"], 1)
            dve.tensor_copy(gts[:, 0:4, :], ps[:, 0, 0:64].rearrange("p (c q) -> p c q", q=16))
            own.link(dve.tensor_copy(gts[0:T4, 4, :], ps[0:T4, 0, 64:80]))
            own.link(dve.memset(hx[:, :, :], 1.0))
            own.link(dve.memset(hn[:, :, :], 0.0))
            own.link(dve.memset(qm[:, :], 0.0))
            own.link(dve.tensor_copy(mst[:, :], rows[:, R_M, SAMP0 + DEC_T - 1:META0:DEC_T]))
            dve.sem_inc(S["gts_ok"], 1)

        def rows_pe(pe):
            pe.wait_ge(S["r_e"], 3)
            for c in range(5):
                n = P if c < 4 else T4
                for q, r in enumerate((R_W, R_A, R_WK, R_T)):
                    mm = pe.transpose(ps[0:n, 0, 16 * c + 4 * q:16 * c + 4 * q + 4], rows[:, r, P * c:P * c + n],
                                      ident[0:H_A, 0:H_A])
            mm.then_inc(S["gt"], 1)

        W_, A_, WK_, EM_ = range(4)
        P1 = P + 1

        def mlstm_dve(dve):
            dve.wait_ge(S["c0ld"], 16)
            with dve.Fori(0, H_A) as i:
                own.start(i, 26)
                dve.tensor_copy(qkv[:, 0, :], pj[:, bass.ds(i + QA, 1), :].rearrange("p a n -> p (a n)"))
                dve.tensor_scalar(qkv[:, 1, :], pj[:, bass.ds(i + KA, 1), :].rearrange("p a n -> p (a n)"),
                                  float(P) ** -0.5, None, ALU.mult)
                dve.tensor_copy(qkv[:, 2, :], pj[:, bass.ds(i + VA, 1), :].rearrange("p a n -> p (a n)"))
                dve.tensor_copy(selh[:, :], cst[0:H_A, bass.ds(i * P + C_SEL, P)])
                dve.tensor_copy(ghc[:, :], gev[:, bass.ds(i, 1)])
                own.link(dve.tensor_copy(gh[:, :, :], gts[:, :, :].rearrange("p c (q h) -> p c q h", h=4)
                                         [:, :, :, bass.ds(i, 1)].rearrange("p c q h -> p c (q h)")))
                dve.tensor_copy(qm[:, :].rearrange("p (s c) -> p s c", c=36)[:, :, 0:4],
                                qkv[:, 0, SAMP0:META0].rearrange("p (s t) -> p s t", t=DEC_T)).then_inc(S["m_cp"], 1)
                dve.wait_ge(S["m_tr"], i + 1)
                dve.memset(vx[:, :, P:P1], 1.0)
                dve.tensor_copy(vx[:, 0:4, 0:P], ps[:, 1, :].rearrange("p (c n) -> p c n", n=P))
                dve.tensor_copy(vx[0:T4, 4, 0:P], ps[0:T4, 2, P:2 * P])
                dve.tensor_tensor(kw[:, 0:4, :], ps[:, 0, :].rearrange("p (c n) -> p c n", n=P),
                                  gh[:, 0:4, WK_:WK_ + 1].to_broadcast([P, 4, P]), ALU.mult)
                own.link(dve.tensor_scalar(kw[0:T4, 4, :], ps[0:T4, 2, 0:P], gh[0:T4, 4, WK_:WK_ + 1], None, ALU.mult))
                dve.tensor_tensor(kwm[:, :, :], kw[0:N_SAMP, 4:5, :].to_broadcast([N_SAMP, DEC_B, P]),
                                  cst[0:N_SAMP, C_SEQM:C_SEQM + DEC_B].rearrange("p (s o) -> p s o", o=1)
                                  .to_broadcast([N_SAMP, DEC_B, P]), ALU.mult).then_inc(S["m_kv"], 1)
                dve.wait_ge(S["m_bc"], i + 1)
                dve.wait_ge(S["m_D"], i + 1)
                own.link(dve.tensor_copy(wdh[:, :], ps[:, 4, 64:76]))
                dve.wait_ge(S["m_qk"], i + 1)
                dve.tensor_tensor(sT[:, 0:SEQ], ps[:, 5, :], dec[:, 0:SEQ], ALU.mult)
                dve.tensor_tensor(sT[0:T4, SEQ:N_TOK], ps[0:T4, 6, 0:T4], dec[0:T4, SEQ:N_TOK], ALU.mult)\
                   .then_inc(S["m_S"], 1)
                dve.wait_ge(S["m_kvs"], i + 1)
                own.link(dve.tensor_copy(Cs[:, 0, :], ps[:, 0, 0:P1]))
                for c in range(4):
                    kv = ps[:, 0, (c + 1) * P1:(c + 2) * P1] if c < 2 else ps[:, 1, (c - 2) * P1:(c - 1) * P1]
                    own.link(dve.scalar_tensor_tensor(Cs[:, c + 1, :], Cs[:, c, :], wdh[:, c:c + 1], kv, ALU.mult, ALU.add))
                dve.tensor_copy(cfin[:, bass.ds(i, 1), :], Cs[:, 4:5, :]).then_inc(S["m_C"], 1)
                dve.wait_ge(S["m_in"], i + 1)
                dve.tensor_copy(hx[0:T4, 4, :], ps[0:T4, 5, 0:P1])
                dve.tensor_copy(hx[:, 0:2, :], ps[:, 5, P1:3 * P1].rearrange("p (c n) -> p c n", n=P1))
                own.link(dve.tensor_copy(hx[:, 2:4, :], ps[:, 6, 0:2 * P1].rearrange("p (c n) -> p c n", n=P1)))
                dve.wait_ge(S["m_it"], i + 1)
                own.link(dve.scalar_tensor_tensor(hx[0:N_SAMP, 4, :], ps[0:N_SAMP, 7, 0:P1], gh[0:N_SAMP, 4, W_:W_ + 1],
                                                  hx[0:N_SAMP, 4, :], ALU.mult, ALU.add))
                for s in range(DEC_B):
                    kv = ps[:, 2 + s // 3, (s % 3) * P1:(s % 3 + 1) * P1]
                    st = c0[:, bass.ds(i, 1), s, :].rearrange("p a n -> p (a n)")
                    own.link(dve.scalar_tensor_tensor(st, st, wdh[:, 4 + s:5 + s], kv, ALU.mult, ALU.add))
                for c in range(4):
                    it = ps[:, 0, c * P1:(c + 1) * P1] if c < 3 else ps[:, 1, 0:P1]
                    own.link(dve.scalar_tensor_tensor(hx[:, c, :], it, gh[:, c, W_:W_ + 1], hx[:, c, :], ALU.mult, ALU.add))
                own.link(dve.scalar_tensor_tensor(den[:, :], hx[:, :, P], -1.0, gh[:, :, EM_], ALU.mult, ALU.max))
                own.link(dve.tensor_tensor(den[:, :], hx[:, :, P], den[:, :], ALU.max))
                own.link(dve.reciprocal(rec[:, :], den[:, :]))
                dve.tensor_tensor(hn[:, :, :], hx[:, :, 0:P],
                                  rec[:, :].rearrange("p (c o) -> p c o", o=1).to_broadcast([P, 5, P]), ALU.mult)\
                   .then_inc(S["m_hn"], 1)
                dve.wait_ge(S["m_rs"], i + 1)
                dve.tensor_tensor(hn[:, :, :], hn[:, :, :],
                                  rs5[:, :].rearrange("p (c o) -> p c o", o=1).to_broadcast([P, 5, P]), ALU.mult)\
                   .then_inc(S["m_y"], 1)
                dve.wait_ge(S["m_yt"], i + 1)
                dve.wait_ge(S["m_so"], i + 1)
                dve.scalar_tensor_tensor(pj[:, bass.ds(i, 1), 0:SEQ].rearrange("p a n -> p (a n)"), ps[:, 7, :],
                                         ghc[:, 0:1], so[:, 0:SEQ],
                                         ALU.mult, ALU.mult)
                own.link(dve.scalar_tensor_tensor(pj[:, bass.ds(i, 1), SEQ:N_TOK].rearrange("p a n -> p (a n)"), ps[:, 2, 0:T4],
                                                  ghc[:, 0:1], so[:, SEQ:N_TOK], ALU.mult, ALU.mult))
                own.end(H_A)

        def mlstm_act(act):
            with act.Fori(0, H_A) as i:
                act.wait_ge(S["m_cp"], i + 1)
                act.activation(so[:, :], pj[:, bass.ds(i + OA, 1), :].rearrange("p a n -> p (a n)"), ACT.Exp, scale=-1.0).then_inc(S["m_a"], 1)
                act.wait_ge(S["m_a"], i * 3 + 1)
                act.activation(so[:, :], so[:, :], ACT.Ln, bias=one[:, 0:1]).then_inc(S["m_a"], 1)
                act.wait_ge(S["m_a"], i * 3 + 2)
                act.activation(so[:, :], so[:, :], ACT.Exp, scale=-1.0).then_inc(S["m_so"], 1)
                act.wait_ge(S["m_bc"], i + 1)
                for c in range(4):
                    act.activation(dec[:, c * P:(c + 1) * P], ps[:, 3, c * P:(c + 1) * P], ACT.Exp, bias=gh[:, c, A_:A_ + 1])
                act.activation(dec[0:T4, SEQ:N_TOK], ps[0:T4, 4, 0:T4], ACT.Exp, bias=gh[0:T4, 4, A_:A_ + 1])\
                   .then_inc(S["m_D"], 1)
                act.wait_ge(S["m_hn"], i + 1)
                for c in range(5):
                    ins = act.activation(sT[:, 0:P], hn[:, c, :], ACT.Square, accum_out=ssq[:, c:c + 1])
                    ins.then_inc(S["m_sq"], 1)
                    act.wait_ge(S["m_sq"], i * 5 + (c + 1))
                act.activation(rs5[:, :], ssq[:, :], ACT.Ln, bias=eps[:, 0:1], scale=1.0 / P).then_inc(S["m_a"], 1)
                act.wait_ge(S["m_a"], i * 3 + 3)
                act.activation(rs5[:, :], rs5[:, :], ACT.Exp, scale=-0.5).then_inc(S["m_rs"], 1)

        def mlstm_pe(pe):
            with pe.Fori(0, H_A) as i:
                pe.wait_ge(S["m_cp"], i + 1)
                q, k, v = qkv[:, 0, :], qkv[:, 1, :], qkv[:, 2, :]
                tile = lambda a, c: a[:, P * c:P * c + (P if c < 4 else T4)]
                for c in range(4):
                    pe.transpose(ps[:, 0, c * P:(c + 1) * P], tile(k, c), ident)
                    pe.transpose(ps[:, 1, c * P:(c + 1) * P], tile(v, c), ident)
                pe.transpose(ps[0:T4, 2, 0:P], tile(k, 4), ident)
                pe.transpose(ps[0:T4, 2, P:2 * P], tile(v, 4), ident).then_inc(S["m_tr"], 1)
                pe.matmul(ps[:, 3, :], selh[:, :], rows[:, R_RM, 0:SEQ], start=True, stop=False)
                for c in range(4):
                    pe.matmul(ps[:, 3, c * P:(c + 1) * P], ident, cst[:, C_NEG:C_NEG + P], start=False, stop=c == 3)
                pe.matmul(ps[0:T4, 4, 0:T4], selh[:, 0:T4], rows[:, R_RM, SEQ:N_TOK], start=True, stop=False)
                pe.matmul(ps[0:T4, 4, 0:T4], ident[0:T4, 0:T4], cst[0:T4, C_NEG4:C_NEG4 + T4], start=False, stop=True)
                pe.matmul(ps[:, 4, 64:68], selh[:, :], rows[:, R_W, P - 1:SEQ:P], start=True, stop=True)
                pe.matmul(ps[:, 4, 68:76], selh[:, :], rows[:, R_W, SAMP0 + DEC_T - 1:META0:DEC_T], start=True, stop=True)\
                  .then_inc(S["m_bc"], 1)
                for c in range(4):
                    pe.matmul(ps[:, 5, c * P:(c + 1) * P], tile(k, c), tile(q, c), start=True, stop=True)
                pe.matmul(ps[0:T4, 6, 0:T4], tile(k, 4), tile(q, 4), start=True, stop=True).then_inc(S["m_qk"], 1)
                for s in range(DEC_B):
                    mm = pe.matmul(ps[0:N_SAMP, 7, 0:P1], qm[:, N_SAMP * s:N_SAMP * (s + 1)],
                                   c0[:, bass.ds(i, 1), s, :].rearrange("p a n -> p (a n)"), start=s == 0, stop=s == DEC_B - 1)
                mm.then_inc(S["m_si"], 1)
                pe.wait_ge(S["m_kv"], i + 1)
                pe.wait_ge(S["m_S"], i + 1)
                pe.matmul(ps[:, 0, 0:P1], kw[N_SAMP:T4, 4, :], vx[N_SAMP:T4, 4, :], start=True, stop=True)
                for c in range(4):
                    out = ps[:, 0, (c + 1) * P1:(c + 2) * P1] if c < 2 else ps[:, 1, (c - 2) * P1:(c - 1) * P1]
                    mm = pe.matmul(out, kw[:, c, :], vx[:, c, :], start=True, stop=True)
                mm.then_inc(S["m_kvs"], 1)
                pe.matmul(ps[0:T4, 5, 0:P1], sT[0:T4, SEQ:N_TOK], vx[0:T4, 4, :], start=True, stop=True)
                for c in range(4):
                    out = ps[:, 5, (c + 1) * P1:(c + 2) * P1] if c < 2 else ps[:, 6, (c - 2) * P1:(c - 1) * P1]
                    mm = pe.matmul(out, sT[:, c * P:(c + 1) * P], vx[:, c, :], start=True, stop=True)
                mm.then_inc(S["m_in"], 1)
                for s in range(DEC_B):
                    mm = pe.matmul(ps[:, 2 + s // 3, (s % 3) * P1:(s % 3 + 1) * P1], kwm[:, s, :], vx[0:N_SAMP, 4, :],
                                   start=True, stop=True)
                pe.wait_ge(S["m_C"], i + 1)
                for c in range(4):
                    out = ps[:, 0, c * P1:(c + 1) * P1] if c < 3 else ps[:, 1, 0:P1]
                    mm = pe.matmul(out, tile(q, c), Cs[:, c, :], start=True, stop=True)
                mm.then_inc(S["m_it"], 1)
                pe.wait_ge(S["m_y"], i + 1)
                for c in range(4):
                    pe.transpose(ps[:, 7, c * P:(c + 1) * P], hn[:, c, :], ident)
                pe.transpose(ps[:, 2, 0:T4], hn[0:T4, 4, :], ident[0:T4, 0:T4]).then_inc(S["m_yt"], 1)

        def new_pe(pe):
            pe.wait_ge(S["d_q"], 1)
            for p in range(4):
                pe.matmul(ps[0:N_SAMP, 5, 64 * p:64 * p + 64], pj[:, KBB + p, SAMP0:META0],
                          qbd[:, p, :, :].rearrange("p s c -> p (s c)"), start=True, stop=True)
                mm = pe.transpose(ps[0:N_SAMP, 6, P * p:P * p + P], pj[:, VB + p, SAMP0:META0], ident)
            mm.then_inc(S["d_z"], 1)
            pe.wait_ge(S["d_sp"], 1)
            pe.matmul(ps[0:N_SAMP, 5, 0:256], after[0:N_SAMP, 0:N_SAMP], spn[:, :], start=True, stop=True).then_inc(S["d_A"], 1)
            pe.wait_ge(S["d_w"], 1)
            for p in range(4):
                mm = pe.matmul(ps[:, 7, 64 * p:64 * p + 64], vnew[:, p, :], zn[:, 64 * p:64 * p + 64], start=True, stop=True)
            mm.then_inc(S["d_o"], 1)

        def softplus_act(act, src, dst, s, k0):
            act.activation(dst, src, ACT.Abs).then_inc(s, 1)
            act.wait_ge(s, k0 + 1)
            act.activation(dst, dst, ACT.Exp, scale=-1.0).then_inc(s, 1)
            act.wait_ge(s, k0 + 2)
            n = dst.shape[0]
            return act.activation(dst, dst, ACT.Ln, bias=one[0:n, 0:1])

        def new_act(act):
            act.wait_ge(S["d_zs"], 1)
            softplus_act(act, zn[:, :], ln_[:, :], S["a_x"], 0).then_inc(S["d_l"], 1)
            act.wait_ge(S["d_t"], 1)
            act.activation(zn[:, :], zn[:, :], ACT.Exp).then_inc(S["d_e"], 1)

        def new_dve(dve):
            own.link(dve.memset(qbd[:, :, :, :], 0.0))
            for r, c in ((0, 0), (64, 4)):
                ins = dve.tensor_copy(qbd[r:r + 64, :, :, c:c + 4],
                                      pj[r:r + 64, QB:QB + 4, SAMP0:META0].rearrange("p b (s t) -> p b s t", t=DEC_T))
                if r == 0:
                    own.link(ins)
            ins.then_inc(S["d_q"], 1)
            dve.wait_ge(S["d_z"], 1)
            dve.tensor_copy(vnew[:, :, :], ps[0:N_SAMP, 6, :].rearrange("p (b n) -> p b n", n=P))
            col = lambda a, p: a[:, 64 * p:64 * p + 64]
            v3 = lambda a: a.rearrange("p (s c) -> p s c", c=8)
            v4 = lambda a: a.rearrange("p (s h t) -> p s h t", h=2, t=DEC_T)
            for p in range(4):
                ins = dve.scalar_tensor_tensor(v3(col(zn, p)), v3(ps[0:N_SAMP, 5, 64 * p:64 * p + 64]), DH_B ** -0.5,
                                               bsr[0:N_SAMP, 8 * p:8 * p + 8].rearrange("p (o c) -> p o c", o=1)
                                               .to_broadcast([N_SAMP, DEC_B, 8]), ALU.mult, ALU.add)
            ins.then_inc(S["d_zs"], 1)
            dve.wait_ge(S["d_l"], 1)
            own.link(dve.scalar_tensor_tensor(spn[:, :], zn[:, :], 0.0, ln_[:, :], ALU.max, ALU.add))
            own.link(dve.scalar_tensor_tensor(zn[:, :], zn[:, :], 0.0, ln_[:, :], ALU.min, ALU.subtract))
            msk = cst[0:N_SAMP, C_NEWM:C_NEWM + N_SAMP].rearrange("p (s o t) -> p s o t", o=1, t=DEC_T)\
                .to_broadcast([N_SAMP, DEC_B, 2, DEC_T])
            for p in range(4):
                ins = dve.tensor_tensor(v4(col(spn, p)), v4(col(spn, p)), msk, ALU.mult)
            ins.then_inc(S["d_sp"], 1)
            dve.wait_ge(S["d_A"], 1)
            dve.tensor_tensor(zn[:, :], zn[:, :], ps[0:N_SAMP, 5, 0:256], ALU.subtract).then_inc(S["d_t"], 1)
            dve.wait_ge(S["d_e"], 1)
            for p in range(4):
                ins = dve.tensor_tensor(v4(col(zn, p)), v4(col(zn, p)), msk, ALU.mult)
            ins.then_inc(S["d_w"], 1)
            dve.wait_ge(S["d_o"], 1)
            own.link(dve.tensor_copy(osn[:, :], ps[:, 7, 0:256]))

        KLD = [sem(f"kld{g}") for g in range(4)]
        VLD = [sem(f"vld{g}") for g in range(4)]
        N_POOL = k_cache.shape[0]

        def load_group(sp_, cache, buf, ready, used, i, u, g):
            for a in range(PG):
                at_ = u * N_PAGES + N_PAGES - 1 - (4 * a + g)
                page = sp_.value_load(ptab[0:1, bass.ds(i * (2 * N_PAGES) + at_, 1)], min_val=0, max_val=N_POOL - 1)
                if a == 0:
                    sp_.wait_ge(S[used], i * 8 + (4 * u + g + 1))
                sp_.dma_start(buf[g][:, a].rearrange("p b n -> p (b n)") if buf is kbuf else buf[g][:, a],
                              cache[bass.ds(page, 1), :, :].rearrange("a p n -> (a p) n")).then_inc(ready[g], 16)

        def load_k(sp_, i, u, g):
            load_group(sp_, k_cache, kbuf, KLD, "k_used", i, u, g)

        def load_v(sp_, i, u, g):
            load_group(sp_, v_cache, vbuf, VLD, "v_used", i, u, g)

        def load_step(sp_, i, u, last=False):
            for half in range(2):
                for g in (2 * half, 2 * half + 1):
                    if not last:
                        load_k(sp_, i, u + 1, g)
                for g in (2 * half, 2 * half + 1):
                    load_v(sp_, i, u, g)

        def qs_dve(dve, i, u):
            dve.tensor_copy(qs[:, :, 0:8], qbd[:, :, bass.ds(i * 2 + u, 1), :].rearrange("p b s c -> p b (s c)"))\
               .then_inc(S["b_q"], 1)

        def qk_pe(pe, i, u):
            pe.wait_ge(S["b_q"], i * 2 + (u + 1))
            for g in range(4):
                pe.wait_ge(KLD[g], i * 128 + 64 * (u + 1))
                for p in range(4):
                    mm = pe.matmul(ps[ROWN * g:ROWN * (g + 1), 5, :], qs[:, :, :].rearrange("p b c -> p (b c)")
                                   [:, ROWN * p:ROWN * (p + 1)], kbuf[g][:, :, p, :],
                                   start=p == 0, stop=p == 3)
                mm.then_inc(S["k_used"], 1)

        def tr_pe(pe, i, u):
            pe.wait_ge(S["b_zr"], i * 2 + (u + 1))
            for a in range(PG):
                mm = pe.transpose(ps[:, 6, P * a:P * a + P], zr[:, P * a:P * a + P], ident)
            mm.then_inc(S["b_z"], 1)

        def suffix_pe(pe, i, u):
            pe.wait_ge(S["b_sp"], i * 2 + (u + 1))
            out = ps[:, 6, :].rearrange("p (c a) -> p c a", a=N_PAGES)
            pe.matmul(out, after, sg[:, :, 1:1 + N_PAGES], start=True, stop=False)
            pe.matmul(out, ones, ssg[:, :, 0:N_PAGES], start=False, stop=True).then_inc(S["b_A"], 1)

        def pv_pe(pe, i, u, half):
            if half == 0:
                pe.wait_ge(S["b_w"], i * 2 + (u + 1))
                pe.wait_ge(S["b_ev"], i * 2 + (u + 1))
            for g in (2 * half, 2 * half + 1):
                pe.wait_ge(VLD[g], i * 128 + 64 * (u + 1))
                for a in range(PG):
                    mm = pe.matmul(ps[0:ROWN, 7, :], lg[:, u % 2, 4 * a + g, :], vbuf[g][:, a, :],
                                   start=(g, a) == (0, 0), stop=(g, a) == (3, PG - 1))
                mm.then_inc(S["v_used"], 1)

        def out_pe(pe, i, u):
            pe.wait_ge(S["b_om"], i * 2 + (u + 1))
            for p in range(4):
                mm = pe.matmul(ps[:, 7, DEC_T * p:DEC_T * (p + 1)], outm[:, P * p:P * p + P],
                               cst[0:ROWN, C_QRY:C_QRY + DEC_T], start=True, stop=True)
            mm.then_inc(S["b_o"], 1)

        def page_z_act(act, i, u):
            act.wait_ge(S["k_used"], i * 8 + (4 * u + 8))
            act.activation(zr[:, :], ps[:, 5, :], ACT.Identity, bias=bcol[:, 0:1], scale=DH_B ** -0.5)\
               .then_inc(S["b_zr"], 1)

        def page_act(act, i, u):
            act.wait_ge(S["b_z"], i * 2 + (u + 1))
            if u:
                act.wait_ge(S["v_used"], i * 8 + 4 * u)
            softplus_act(act, ps[:, 6, :].rearrange("p (a c) -> p a c", c=ROWN), lg[:, u % 2], S["b_x"],
                         i * 4 + 2 * u).then_inc(S["b_l"], 1)

        def page_exp(act, i, u):
            act.wait_ge(S["b_t"], i * 2 + (u + 1))
            act.activation(lg[:, u % 2], lg[:, u % 2], ACT.Exp).then_inc(S["b_w"], 1)

        def page_z_dve(dve, i, u):
            dve.tensor_copy(sg[0:N_SAMP, :, 0:1].rearrange("p (b c) o -> p b (c o)", c=8),
                            spn[:, :].rearrange("p (b s c) -> p b s c", s=DEC_B, c=8)
                            [:, :, bass.ds(i * 2 + u, 1), :].rearrange("p b s c -> p b (s c)"))
            dve.wait_ge(S["b_l"], i * 2 + (u + 1))
            zt = ps[:, 6, :].rearrange("p (a c) -> p a c", c=ROWN)
            dve.scalar_tensor_tensor(zg[:, :, :], zt, 0.0, lg[:, u % 2], ALU.min, ALU.subtract)
            own.link(dve.scalar_tensor_tensor(sg[:, :, 1:].rearrange("p c a -> p a c"), zt, 0.0, lg[:, u % 2],
                                              ALU.max, ALU.add))
            f2 = lambda a: a[:, :, :].rearrange("p c a -> p (c a)")
            dve.tensor_tensor_scan(f2(ssg), f2(smk), f2(sg), 0.0, ALU.mult, ALU.add).then_inc(S["b_sp"], 1)

        def page_sub(dve, i, u):
            dve.wait_ge(S["b_A"], i * 2 + (u + 1))
            dve.tensor_tensor(lg[:, u % 2], zg[:, :, :], ps[:, 6, :].rearrange("p (c a) -> p a c", a=N_PAGES), ALU.subtract)\
               .then_inc(S["b_t"], 1)

        def own_heads_dve(dve, i, u):
            dve.wait_ge(S["v_used"], i * 8 + (4 * u + 8))
            dve.tensor_tensor(outm[:, :].rearrange("p (h d) -> p h d", d=DH_B), ps[0:ROWN, 7, :]
                              .rearrange("p (h d) -> p h d", d=DH_B),
                              cst[0:ROWN, C_HEAD:C_HEAD + H_B].rearrange("p (h o) -> p h o", o=1)
                              .to_broadcast([ROWN, H_B, DH_B]), ALU.mult).then_inc(S["b_om"], 1)

        def page_out(dve, i, u):
            dve.wait_ge(S["b_o"], i * 2 + (u + 1))
            for r, c in ((0, 0), (64, 4)):
                ins = dve.tensor_tensor(pj[r:r + 64, QB:QB + 4, bass.ds(i * (2 * DEC_T) + (SAMP0 + DEC_T * u), DEC_T)],
                                        ps[r:r + 64, 7, 0:16].rearrange("p (b c) -> p b c", c=DEC_T),
                                        osn[r:r + 64, :].rearrange("p (b s c) -> p b s c", s=DEC_B, c=8)
                                        [:, :, bass.ds(i * 2 + u, 1), c:c + 4].rearrange("p b s c -> p b (s c)"), ALU.add)
            ins.then_inc(S["b_ev"], 1)

        WID = [SEQ - P * k for k in range(4)]
        ZB = [(0, 0), (1, 0), (2, 0), (2, 256)]
        META = slice(WZ, WZ + SEQ)
        METAQ = slice(WZ + SEQ, WA)

        def pair_dve(dve, i):
            blk = lambda b: pj[:, bass.ds(i + b, 1), :].rearrange("p a n -> p (a n)")
            dve.memset(qz[:, :, :], 0.0)
            dve.tensor_copy(bh[:, :], bsb[:, bass.ds(i * 2, 2)])
            own.link(dve.tensor_copy(kP[:, :], blk(KBB)))
            dve.tensor_copy(vF[:, :], blk(VB))
            for j in range(2):
                r = 64 * j
                ins = dve.tensor_copy(qz[r:r + 64, j, :], pj[r:r + 64, bass.ds(i + QB, 1), :].rearrange("p a n -> p (a n)"))
                if j == 0:
                    own.link(ins)
            ins.then_inc(S["a_in"], 1)
            dve.wait_ge(S["v_tr"], i + 1)
            dve.tensor_copy(vP[:, 0:4, :], ps[:, 4, :].rearrange("p (c n) -> p c n", n=P))
            dve.tensor_copy(vP[0:N_META, 4, :], ps[0:N_META, 2, 384:512]).then_inc(S["v_ev"], 1)

        def pz_pe(pe, i, j):
            if j == 0:
                pe.wait_ge(S["a_in"], i + 1)
                for c in range(4):
                    pe.transpose(ps[:, 4, P * c:P * c + P], vF[:, P * c:P * c + P], ident)
                pe.transpose(ps[0:N_META, 2, 384:512], vF[:, META0:N_TOK], ident).then_inc(S["v_tr"], 1)
                pe.wait_ge(S["v_ev"], i + 1)
            else:
                pe.wait_ge(S["a_o"], i * 2 + 1)
            for k in range(4):
                b, c = ZB[k]
                pe.matmul(ps[:, b, c:c + WID[k]], kP[:, P * k:P * k + P], qz[:, j, P * k:SEQ], start=True, stop=True)
            pe.matmul(ps[0:N_META, 3, 0:SEQ], kP[:, META0:N_TOK], qz[:, j, 0:SEQ], start=True, stop=True)
            pe.matmul(ps[0:N_META, 1, 384:400], kP[:, META0:N_TOK], qz[:, j, META0:N_TOK], start=True, stop=True)\
              .then_inc(S["a_z"], 1)

        def pz_act(act, i, j):
            act.wait_ge(S["a_z"], i * 2 + (j + 1))
            if j == 1:
                act.wait_ge(S["a_w"], i * 2 + 1)
            c = DH_B ** -0.5
            for dst, src in ((z[:, 0:512], ps[:, 0, :]), (z[:, 512:896], ps[:, 1, 0:384]), (z[:, 896:WZ], ps[:, 2, 0:384])):
                ins = act.activation(dst, src, ACT.Identity, scale=c, bias=bh[:, j:j + 1])
            for dst, src in ((z[0:N_META, META], ps[0:N_META, 3, :]), (z[0:N_META, METAQ], ps[0:N_META, 1, 384:400])):
                ins = act.activation(dst, src, ACT.Identity, scale=c, bias=bh[0:N_META, j:j + 1])
            ins.then_inc(S["a_x2"], 1)

        def psoft_act(act, i, j):
            act.wait_ge(S["a_x2"], i * 10 + (5 * j + 1))
            softplus_act(act, z[:, 0:WZ], lz[:, 0:WZ], S["a_x2"], i * 10 + (5 * j + 1))
            softplus_act(act, z[0:N_META, WZ:WA], lz[0:N_META, WZ:WA], S["a_x2"], i * 10 + (5 * j + 3)).then_inc(S["a_l"], 1)

        FULL = [(slice(0, P), slice(0, WZ)), (slice(0, N_META), slice(WZ, WA))]

        def diag_mask(dve, buf):
            for k in range(4):
                dve.tensor_tensor(buf[:, KOFF[k]:KOFF[k] + P], buf[:, KOFF[k]:KOFF[k] + P], strict, ALU.mult)
            return dve.tensor_tensor(buf[0:N_META, METAQ], buf[0:N_META, METAQ], strict[0:N_META, 0:N_META], ALU.mult)

        def psp_dve(dve, i, j):
            dve.wait_ge(S["a_l"], i * 2 + (j + 1))
            for r, c in FULL:
                own.link(dve.scalar_tensor_tensor(sp[r, c], z[r, c], 0.0, lz[r, c], ALU.max, ALU.add))
                own.link(dve.scalar_tensor_tensor(z[r, c], z[r, c], 0.0, lz[r, c], ALU.min, ALU.subtract))
            diag_mask(dve, sp).then_inc(S["a_sp"], 1)

        def suffixes_pe(pe, i, j):
            pe.wait_ge(S["a_sp"], i * 2 + (j + 1))
            for k in range(4):
                b, c = ZB[k]
                pe.matmul(ps[:, b, c:c + WID[k]], after, sp[:, KOFF[k]:KOFF[k] + WID[k]], start=True, stop=k == 3)
                for l in range(k + 1, 4):
                    o_ = P * (l - k)
                    pe.matmul(ps[:, b, c + o_:c + WID[k]], ones, sp[:, KOFF[l]:KOFF[l] + WID[l]], start=False, stop=l == 3)
            pe.matmul(ps[0:N_META, 3, 0:SEQ], after[0:N_META, 0:N_META], sp[0:N_META, META], start=True, stop=False)
            for l in range(4):
                pe.matmul(ps[0:N_META, 3, P * l:SEQ], ones[:, 0:N_META], sp[:, KOFF[l]:KOFF[l] + WID[l]],
                          start=False, stop=l == 3)
            pe.matmul(ps[0:N_META, 1, 384:400], after[0:N_META, 0:N_META], sp[0:N_META, METAQ], start=True, stop=True)\
              .then_inc(S["a_A"], 1)

        def psub_dve(dve, i, j):
            dve.wait_ge(S["a_A"], i * 2 + (j + 1))
            for dst, src in (((slice(0, P), slice(0, 512)), ps[:, 0, :]), ((slice(0, P), slice(512, 896)), ps[:, 1, 0:384]),
                             ((slice(0, P), slice(896, WZ)), ps[:, 2, 0:384]), ((slice(0, N_META), META), ps[0:N_META, 3, :]),
                             ((slice(0, N_META), METAQ), ps[0:N_META, 1, 384:400])):
                ins = dve.tensor_tensor(lz[dst], z[dst], src, ALU.subtract)
            ins.then_inc(S["a_t"], 1)

        def pexp_act(act, i, j):
            act.wait_ge(S["a_t"], i * 2 + (j + 1))
            for r, c in FULL:
                ins = act.activation(lz[r, c], lz[r, c], ACT.Exp)
            ins.then_inc(S["a_e"], 1)

        def pmask_dve(dve, i, j):
            dve.wait_ge(S["a_e"], i * 2 + (j + 1))
            diag_mask(dve, lz).then_inc(S["a_w"], 1)

        def pv_prompt_pe(pe, i, j):
            pe.wait_ge(S["a_w"], i * 2 + (j + 1))
            if j == 1:
                pe.wait_ge(S["a_o"], i * 2 + 1)
            pe.matmul(ps[:, 4, :], vP[0:N_META, 4, :], lz[0:N_META, META], start=True, stop=False)
            for k in range(4):
                pe.matmul(ps[:, 4, P * k:SEQ], vP[:, k, :], lz[:, KOFF[k]:KOFF[k] + WID[k]], start=False, stop=k == 3)
            pe.matmul(ps[:, 2, 384:400], vP[0:N_META, 4, :], lz[0:N_META, METAQ], start=True, stop=True).then_inc(S["a_v"], 1)

        def pout_dve(dve, i, j):
            dve.wait_ge(S["a_v"], i * 2 + (j + 1))
            r = slice(64 * j, 64 * j + 64)
            blk = pj[r, bass.ds(i + QB, 1), :].rearrange("p a n -> p (a n)")
            dve.tensor_scalar(blk[:, 0:SEQ], ps[r, 4, :], 1.0, None, ALU.mult)
            dve.tensor_scalar(blk[:, META0:N_TOK], ps[r, 2, 384:400], 1.0, None, ALU.mult).then_inc(S["a_o"], 1)

        def turns(eng, step, own_steps=None):
            with eng.Fori(0, 3) as i:
                if own_steps:
                    own.start(i, own_steps)
                for u in range(2):
                    step(i, u, False)
                if own_steps:
                    own.end(3)
            for u in range(2):
                step(3, u, u == 1)

        def load_pages(sp_):
            turns(sp_, lambda i, u, last: load_step(sp_, i, u, last))

        def attn_pe(pe):
            def step(i, u, last):
                pz_pe(pe, i, u)
                suffix_pe(pe, i, u)
                if not last:
                    qk_pe(pe, i, u + 1)
                pv_pe(pe, i, u, 0)
                if not last:
                    tr_pe(pe, i, u + 1)
                suffixes_pe(pe, i, u)
                pv_pe(pe, i, u, 1)
                pv_prompt_pe(pe, i, u)
                out_pe(pe, i, u)
            qk_pe(pe, 0, 0)
            tr_pe(pe, 0, 0)
            turns(pe, step)

        def attn_act(act):
            def step(i, u, last):
                pz_act(act, i, u)
                page_exp(act, i, u)
                psoft_act(act, i, u)
                if not last:
                    page_z_act(act, i, u + 1)
                    page_act(act, i, u + 1)
                pexp_act(act, i, u)
            page_z_act(act, 0, 0)
            page_act(act, 0, 0)
            turns(act, step)

        def attn_dve(dve):
            def step(i, u, last):
                if u == 0:
                    pair_dve(dve, i)
                if not last:
                    qs_dve(dve, i, u + 1)
                page_sub(dve, i, u)
                psp_dve(dve, i, u)
                if not last:
                    page_z_dve(dve, i, u + 1)
                psub_dve(dve, i, u)
                pmask_dve(dve, i, u)
                own_heads_dve(dve, i, u)
                pout_dve(dve, i, u)
                page_out(dve, i, u)
            own.link(dve.memset(qs[:, :, :], 0.0))
            qs_dve(dve, 0, 0)
            dve.memset(sg[:, :, 0:1], 0.0)
            own.link(dve.memset(smk[:, :, :], 1.0))
            own.link(dve.memset(smk[:, :, 0:1], 0.0))
            page_z_dve(dve, 0, 0)
            turns(dve, step, 12)

        LEVELS = [64, 32, 16, 8, 4, 2, 1, 0]
        X = [at("X0", o_M, [P, H_C, N_TOK]), at("X1", o_M + 4 * ROW, [P, H_C, N_TOK])]
        E = at("E", o_M + 8 * ROW, [P, H_C, N_TOK])
        cum = at("cum", o_M + 12 * ROW, [P, H_C, N_TOK])
        o = o_M + 16 * ROW
        AT = at("AT", o, [P, 5, H_C, P]); o += 5 * H_C * P * 4
        sfin = at("sfin", o, [P, H_C, DV_C])
        gmk = at("gmk", o, [P, 8, P], i32); o += 4096
        gm4 = at("gm4", o, [T4, 5, T4], i32); o += 960
        el = at("el", o, [P, H_C, 13]); o += 224
        nbg = at("nbg", o, [P, H_C]); o += 32
        assert o <= o_xn
        o = o_M + 8 * ROW
        ATh = at("ATh", o, [P, 5, P]); o += 2560
        KT = at("KT", o, [P, 5, P]); o += 2560
        VT = at("VT", o, [P, 5, DV_C]); o += 5120
        Ss = at("Ss", o, [P, 5, DV_C]); o += 5120
        gqm = at("gqm", o, [P, 416]); o += 1664
        elh = at("elh", o, [P, 13]); o += 64
        gos = at("gos", o, [P, 2]); o += 32
        gsq = at("gsq", o, [P, 5]); o += 32
        grs = at("grs", o, [P, 5]); o += 32
        assert o <= o_M + 16 * ROW
        o = o_pj
        gq = at("gq", o, [P, N_TOK]); o += ROW
        gk = at("gk", o, [P, N_TOK]); o += ROW
        gv = at("gv", o, [P, 2, N_TOK]); o += 2 * ROW
        sr = at("sr", o, [P, 2, N_TOK]); o += 2 * ROW
        gkm = at("gkm", o, [N_SAMP, DEC_B, P]); o += 4096
        assert o <= o_pj + 8 * ROW
        on = at("on", o_pj + 24 * ROW, [P, 5, DV_C])
        rst = at("rst", o_pj + 24 * ROW, [P, N_TOK])
        wgd = at("wgd", o_pj + 27 * ROW, [P, KB, 16])
        wgu = at("wgu", o_s + 1184, [16, H_C * P])
        gd = at("gd", o_s + 1184 + 2048, [16, N_TOK])
        s0b = at("s0b", o_xn, [P, 2, DEC_B, DV_C])
        TAU = 16.0
        flat = lambda a: a.rearrange("p h t -> p (h t)")
        UNITS = [(l, c) for l in range(8) for c in range(5) if c < 4 or LEVELS[l] <= 8]

        def gdown_pe(pe):
            pe.wait_ge(S["n_xn"], 6)
            pe.wait_ge(S["wgl"], 32)
            for h in range(2):
                for k in range(KB):
                    mm = pe.matmul(ps[0:16, 4 + h, 0:HALF], wgd[:, k, :], xn[:, k, COLS[h]], start=k == 0, stop=k == KB - 1)
            mm.then_inc(S["gd_ps"], 1)
            pe.wait_ge(S["gd_ok"], 2)

        def gdown_act(act):
            act.wait_ge(S["gd_ps"], 1)
            for h in range(2):
                act.activation(gd[:, COLS[h]], ps[0:16, 4 + h, 0:HALF], ACT.Copy).then_inc(S["gd_ok"], 1)

        def lgate_pe(pe):
            pj_all(pe, "odd")
            for h in range(H_C):
                for k in range(2):
                    mm = pe.matmul(ps[:, 2 * h + k, 0:HALF], wgu[:, P * h:P * h + P], gd[:, COLS[k]], start=True, stop=True)
            mm.then_inc(S["g_lg"], 1)

        def lgate_act(act):
            pj_all(act, "odd")
            act.wait_ge(S["g_lg"], 1)
            act.wait_ge(S["g_nb"], 1)
            for h in range(H_C):
                for k in range(2):
                    ins = act.activation(cum[:, h, COLS[k]], ps[:, 2 * h + k, 0:HALF], ACT.Identity, scale=-1.0,
                                         bias=nbg[:, h:h + 1])
            ins.then_inc(S["g_a"], 1)
            act.wait_ge(S["g_a"], 1)
            softplus_act(act, flat(cum[:, :, :]), flat(E[:, :, :]), S["g_a"], 1).then_inc(S["g_l"], 1)
            for l, w in enumerate(LEVELS[:-1]):
                act.wait_ge(S["g_ex"], l + 1)
                e = E[:, :, 0:SEQ] if w > 8 else E[:, :, :]
                act.activation(e, e, ACT.Exp, scale=1.0 / TAU).then_inc(S["g_E"], 1)
            act.wait_ge(S["g_x"], 7)
            act.activation(E[:, :, :], cum[:, :, :], ACT.Exp, scale=-1.0 / TAU).then_inc(S["g_E"], 1)
            act.wait_ge(S["g_ex"], 8)
            act.activation(E[:, :, :], E[:, :, :], ACT.Exp, scale=1.0 / TAU).then_inc(S["g_E"], 1)
            for a, b, c in ((0, 4, cum[:, :, P - 1:SEQ:P]), (4, 12, cum[:, :, SAMP0 + DEC_T - 1:META0:DEC_T]),
                            (12, 13, cum[:, :, N_TOK - 1:N_TOK])):
                act.activation(el[:, :, a:b], c, ACT.Exp, scale=-1.0 / TAU).then_inc(S["g_el"], 1)

        def level_dve(dve, l):
            w = LEVELS[l]
            if w > 8:
                v = lambda a: a[:, :, 0:SEQ].rearrange("p h (b c) -> p h b c", c=2 * w)
                lo, hi, ref = (slice(0, w), slice(w, 2 * w), slice(w - 1, w))
                sl = lambda a, r: v(a)[:, :, :, r]
                shape = [P, H_C, SEQ // (2 * w), w]
            else:
                v = lambda a: flat(a).rearrange("p (b c) -> p b c", c=2 * w)
                lo, hi, ref = (slice(0, w), slice(w, 2 * w), slice(w - 1, w))
                sl = lambda a, r: v(a)[:, :, r]
                shape = [P, H_C * N_TOK // (2 * w), w]
            x = X[l % 2]
            q, k = pj[:, QC:QC + 4, :], pj[:, KC:KC + 4, :]
            if l:
                dve.wait_ge(S["g_x"], l)
            r = sl(cum[:, :, :], ref).to_broadcast(shape)
            dve.tensor_tensor(sl(E[:, :, :], lo), sl(cum[:, :, :], lo), r, ALU.subtract)
            dve.tensor_tensor(sl(E[:, :, :], hi), r, sl(cum[:, :, :], hi), ALU.subtract).then_inc(S["g_ex"], 1)
            dve.wait_ge(S["g_E"], l + 1)
            if l >= 2:
                dve.wait_ge(S["g_p"], UNITS.index((l - 1, 0)))
            dve.tensor_tensor(sl(x[:, :, :], lo), sl(k, lo), sl(E[:, :, :], lo), ALU.mult)
            dve.tensor_tensor(sl(x[:, :, :], hi), sl(q, hi), sl(E[:, :, :], hi), ALU.mult).then_inc(S["g_x"], 1)

        def level_pick(dve, l):
            if l:
                dve.wait_ge(S["g_c"], UNITS.index((l, 0)))
            for c in range(5):
                if (l, c) not in UNITS:
                    continue
                u = UNITS.index((l, c))
                dve.wait_ge(S["g_p"], u + 1)
                if c < 4:
                    dve.copy_predicated(AT[:, c, :, :], gmk[:, l:l + 1, :].to_broadcast([P, H_C, P]),
                                        ps[:, u % 8, :].rearrange("p (h n) -> p h n", n=P)).then_inc(S["g_c"], 1)
                else:
                    dve.copy_predicated(AT[0:T4, 4, :, 0:T4], gm4[:, l - 3:l - 2, :].to_broadcast([T4, H_C, T4]),
                                        ps[0:T4, u % 8, 0:H_C * T4].rearrange("p (h n) -> p h n", n=T4)).then_inc(S["g_c"], 1)

        def levels_pe(pe):
            for u, (l, c) in enumerate(UNITS):
                if c == 0 and l < 7:
                    pe.wait_ge(S["g_x"], l + 1)
                if c == 0 and l == 0:
                    pe.wait_ge(S["g_l"], 1)
                if u >= 8:
                    pe.wait_ge(S["g_c"], u - 7)
                cols = slice(P * c, P * c + (P if c < 4 else T4))
                n = P if c < 4 else T4
                for h in range(H_C):
                    k, q = (X[l % 2][:, h, cols],) * 2 if l < 7 else (pj[:, KC + h, cols], pj[:, QC + h, cols])
                    mm = pe.matmul(ps[0:n, u % 8, h * n:h * n + n], k, q, start=True, stop=True)
                mm.then_inc(S["g_p"], 1)

        def gla_pre_dve(dve):
            dve.tensor_scalar(nbg[:, :], bgu[:, :], -1.0, None, ALU.mult).then_inc(S["g_nb"], 1)
            pj_all(dve, "odd")
            own.link(dve.memset(AT[:, :, :, :], 0.0))
            dve.tensor_scalar(pj[:, QC:QC + 4, :], pj[:, QC:QC + 4, :], float(P) ** -0.5, None, ALU.mult)
            dve.wait_ge(S["g_l"], 1)
            own.link(dve.scalar_tensor_tensor(flat(E[:, :, :]), flat(cum[:, :, :]), 0.0, flat(E[:, :, :]), ALU.max, ALU.add))
            dve.wait_ge(S["grst"], 48)
            for h in range(H_C):
                own.link(dve.tensor_tensor_scan(cum[:, h, :], rst[:, :], E[:, h, :], 0.0, ALU.mult, ALU.add))
            for l in range(7):
                level_dve(dve, l)
                if l:
                    level_pick(dve, l - 1)
            level_pick(dve, 6)
            dve.wait_ge(S["g_E"], 8)
            level_pick(dve, 7)
            own.link(dve.tensor_tensor(X[0][:, :, :], pj[:, QC:QC + 4, :], E[:, :, :], ALU.mult))
            ch = lambda a: a[:, :, 0:SEQ].rearrange("p h (c t) -> p h c t", t=P)
            sm = lambda a: a[:, :, SAMP0:META0].rearrange("p h (s t) -> p h s t", t=DEC_T)
            dve.tensor_tensor(ch(E), ch(cum), ch(cum)[:, :, :, P - 1:P].to_broadcast([P, H_C, 4, P]), ALU.subtract)
            dve.tensor_tensor(sm(E), sm(cum), sm(cum)[:, :, :, DEC_T - 1:DEC_T].to_broadcast([P, H_C, DEC_B, DEC_T]), ALU.subtract)
            dve.tensor_tensor(E[:, :, META0:N_TOK], cum[:, :, META0:N_TOK],
                              cum[:, :, N_TOK - 1:N_TOK].to_broadcast([P, H_C, N_META]), ALU.subtract).then_inc(S["g_ex"], 1)
            dve.wait_ge(S["g_E"], 9)
            own.link(dve.tensor_tensor(X[1][:, :, :], pj[:, KC:KC + 4, :], E[:, :, :], ALU.mult))
            dve.wait_ge(S["g_el"], 3)
            own.link(dve.memset(gqm[:, :], 0.0))
            own.link(dve.memset(gsq[:, :], 1.0))
            dve.memset(on[:, :, :], 0.0)

        def gla_dve(dve):
            with dve.Fori(0, H_C // 2) as i:
                own.start(i, 20)
                for j in range(2):
                    n = i * 2 + (j + 1)
                    hd = i * 2 + j
                    one_ = lambda a: a.rearrange("p a n -> p (a n)")
                    dve.tensor_scalar(gq[:, :], one_(X[0][:, bass.ds(hd, 1), :]), 1.0, None, ALU.mult)
                    dve.tensor_copy(gk[:, :], one_(X[1][:, bass.ds(hd, 1), :]))
                    dve.tensor_copy(ATh[:, :, :], AT[:, :, bass.ds(hd, 1), :].rearrange("p c h n -> p c (h n)"))
                    dve.tensor_copy(gv[:, :, :], pj[:, bass.ds(i * 4 + (VC + 2 * j), 2), :])
                    dve.tensor_copy(elh[:, :], one_(el[:, bass.ds(hd, 1), :]))
                    own.link(dve.tensor_copy(gos[:, :], god[:, bass.ds(i * 4 + 2 * j, 2)]))
                    dve.tensor_copy(gqm[:, :].rearrange("p (s c) -> p s c", c=52)[:, :, 0:4],
                                    gq[:, SAMP0:META0].rearrange("p (s t) -> p s t", t=DEC_T)).then_inc(S["h_cp"], 1)
                    dve.wait_ge(S["h_tr"], n)
                    dve.tensor_copy(KT[:, 0:4, :], ps[:, 0, :].rearrange("p (c n) -> p c n", n=P))
                    own.link(dve.tensor_copy(KT[0:T4, 4, :], ps[0:T4, 1, 0:P]))
                    dve.tensor_copy(VT[:, 0:2, :], ps[:, 2, :].rearrange("p (c n) -> p c n", n=DV_C))
                    dve.tensor_copy(VT[:, 2:4, :], ps[:, 3, :].rearrange("p (c n) -> p c n", n=DV_C))
                    dve.tensor_copy(VT[0:T4, 4, :], ps[0:T4, 1, P:P + DV_C])
                    dve.tensor_tensor(gkm[:, :, :], KT[0:N_SAMP, 4:5, :].to_broadcast([N_SAMP, DEC_B, P]),
                                      cst[0:N_SAMP, C_SEQM:C_SEQM + DEC_B].rearrange("p (s o) -> p s o", o=1)
                                      .to_broadcast([N_SAMP, DEC_B, P]), ALU.mult).then_inc(S["h_kv"], 1)
                    dve.wait_ge(S["h_kvs"], n)
                    own.link(dve.tensor_copy(Ss[:, 0, :], ps[:, 4, 0:DV_C]))
                    for c in range(4):
                        b, o_ = divmod(c + 1, 2)
                        own.link(dve.scalar_tensor_tensor(Ss[:, c + 1, :], Ss[:, c, :], elh[:, c:c + 1],
                                                          ps[:, 4 + b, o_ * DV_C:(o_ + 1) * DV_C], ALU.mult, ALU.add))
                    dve.tensor_copy(sfin[:, bass.ds(hd, 1), :], Ss[:, 4:5, :]).then_inc(S["h_S"], 1)
                    dve.wait_ge(S["h_t4"], n)
                    for s in range(DEC_B):
                        b, o_ = SKV[s]
                        ins = dve.scalar_tensor_tensor(s0b[:, j, s, :], s0b[:, j, s, :], elh[:, 4 + s:5 + s],
                                                       ps[:, b, o_:o_ + DV_C], ALU.mult, ALU.add)
                    ins.then_inc(S["h_s0"], 1)
                    dve.wait_ge(S["h_rs"], n)
                    for c in range(4):
                        ins = dve.tensor_scalar(on[:, c, :], ps[:, 4 + c // 2, (c % 2) * DV_C:(c % 2 + 1) * DV_C],
                                                grs[:, c:c + 1], None, ALU.mult)
                    dve.tensor_scalar(on[0:T4, 4, :], ps[0:T4, 1, 0:DV_C], grs[0:T4, 4:5], None, ALU.mult)\
                       .then_inc(S["h_y"], 1)
                    dve.wait_ge(S["h_sg"], n)
                    own.link(dve.tensor_tensor(sr[:, :, :], sr[:, :, :], pj[:, bass.ds(i * 4 + (RC + 2 * j), 2), :], ALU.mult))
                    dve.wait_ge(S["h_yt"], n)
                    for b in range(2):
                        blk = one_(pj[:, bass.ds(i * 4 + (VC + 2 * j + b), 1), :])
                        own.link(dve.scalar_tensor_tensor(blk[:, 0:SEQ], ps[:, 6 + b, :], gos[:, b:b + 1], sr[:, b, 0:SEQ],
                                                 ALU.mult, ALU.mult))
                        ins = dve.scalar_tensor_tensor(blk[:, SEQ:N_TOK], ps[:, 0, T4 * b:T4 * b + T4], gos[:, b:b + 1],
                                                       sr[:, b, SEQ:N_TOK], ALU.mult, ALU.mult)
                    ins.then_inc(S["h_mix"], 1)
                    dve.wait_ge(S["h_mix"], n)
                own.end(H_C // 2)

        SKV = [(6, 256), (7, 0), (7, 256), (0, 0), (0, 256), (2, 0), (2, 256), (3, 0)]

        def gla_act(act):
            with act.Fori(0, H_C // 2) as i:
                for j in range(2):
                    n = i * 2 + (j + 1)
                    act.wait_ge(S["h_cp"], n)
                    rr = pj[:, bass.ds(i * 4 + (RC + 2 * j), 2), :]
                    act.activation(sr[:, :, :], rr, ACT.Exp, scale=-1.0).then_inc(S["h_a"], 1)
                    act.wait_ge(S["h_a"], i * 4 + (2 * j + 1))
                    act.activation(sr[:, :, :], sr[:, :, :], ACT.Ln, bias=one[:, 0:1]).then_inc(S["h_a"], 1)
                    act.wait_ge(S["h_a"], i * 4 + (2 * j + 2))
                    act.activation(sr[:, :, :], sr[:, :, :], ACT.Exp, scale=-1.0).then_inc(S["h_sg"], 1)
                    act.wait_ge(S["h_o"], n)
                    for c in range(5):
                        src = ps[:, 4 + c // 2, (c % 2) * DV_C:(c % 2 + 1) * DV_C] if c < 4 else ps[0:T4, 1, 0:DV_C]
                        m = P if c < 4 else T4
                        act.activation(on[0:m, c, :], src, ACT.Square, accum_out=gsq[0:m, c:c + 1]).then_inc(S["h_q"], 1)
                    act.wait_ge(S["h_q"], i * 10 + (5 * j + 5))
                    act.activation(grs[:, :], gsq[:, :], ACT.Ln, bias=eps[:, 0:1], scale=1.0 / DV_C).then_inc(S["h_b"], 1)
                    act.wait_ge(S["h_b"], n)
                    act.activation(grs[:, :], grs[:, :], ACT.Exp, scale=-0.5).then_inc(S["h_rs"], 1)

        def gla_pe(pe):
            with pe.Fori(0, H_C // 2) as i:
                for j in range(2):
                    n = i * 2 + (j + 1)
                    tile = lambda a, c: a[:, P * c:P * c + (P if c < 4 else T4)]
                    pe.wait_ge(S["h_cp"], n)
                    pe.wait_ge(SLD[j], i * 16 + 16)
                    for c in range(4):
                        pe.transpose(ps[:, 0, c * P:(c + 1) * P], tile(gk, c), ident)
                        for b in range(2):
                            pe.transpose(ps[:, 2 + c // 2, (c % 2) * DV_C + b * P:(c % 2) * DV_C + (b + 1) * P],
                                         tile(gv[:, b], c), ident)
                    pe.transpose(ps[0:T4, 1, 0:P], tile(gk, 4), ident)
                    for b in range(2):
                        mm = pe.transpose(ps[0:T4, 1, P + b * P:2 * P + b * P], tile(gv[:, b], 4), ident)
                    mm.then_inc(S["h_tr"], 1)
                    pe.wait_ge(S["h_kv"], n)
                    for s in range(DEC_B):
                        b, o_ = SKV[s]
                        pe.matmul(ps[:, b, o_:o_ + DV_C], gkm[:, s, :], VT[0:N_SAMP, 4, :], start=True, stop=True)
                    pe.matmul(ps[:, 4, 0:DV_C], KT[N_SAMP:T4, 4, :], VT[N_SAMP:T4, 4, :], start=True, stop=True)
                    for c in range(4):
                        b, o_ = divmod(c + 1, 2)
                        mm = pe.matmul(ps[:, 4 + b, o_ * DV_C:(o_ + 1) * DV_C], KT[:, c, :], VT[:, c, :], start=True, stop=True)
                    mm.then_inc(S["h_kvs"], 1)
                    pe.matmul(ps[0:T4, 1, 0:DV_C], ATh[0:T4, 4, 0:T4], VT[0:T4, 4, :], start=True, stop=False)
                    for s in range(DEC_B):
                        mm = pe.matmul(ps[0:T4, 1, 0:DV_C], gqm[:, T4 * s:T4 * s + T4], s0b[:, j, s, :], start=False,
                                       stop=s == DEC_B - 1)
                    mm.then_inc(S["h_t4"], 1)
                    pe.wait_ge(S["h_S"], n)
                    for c in range(4):
                        out = ps[:, 4 + c // 2, (c % 2) * DV_C:(c % 2 + 1) * DV_C]
                        pe.matmul(out, ATh[:, c, :], VT[:, c, :], start=True, stop=False)
                        mm = pe.matmul(out, tile(gq, c), Ss[:, c, :], start=False, stop=True)
                    mm.then_inc(S["h_o"], 1)
                    pe.wait_ge(S["h_y"], n)
                    for b in range(2):
                        for c in range(4):
                            pe.transpose(ps[:, 6 + b, c * P:(c + 1) * P], on[:, c, b * P:(b + 1) * P], ident)
                    for b in range(2):
                        mm = pe.transpose(ps[:, 0, T4 * b:T4 * b + T4], on[0:T4, 4, b * P:(b + 1) * P], ident[0:T4, 0:T4])
                    mm.then_inc(S["h_yt"], 1)

        SLD = [sem("sld0"), sem("sld1")]

        N_CONST, N_OUT = 12, 3
        block = ctx.enter_context(nc.Block())

        @block.sync
        def _(sp_):
            for half in range(2):
                sp_.dma_start(hT[:, 4 * half:4 * half + 4, :], x[:, 4 * half:4 * half + 4, :]).then_inc(S["xld"], 16)
            for dst, src in ((cst[:, :], const), (gn[:, :, :, :], gains), (gev[:, :], g_even), (god[:, :], g_odd),
                             (bgu[:, :], b_gup), (bsb[:, :], b_sb), (bsr[:, :], b_sbrow), (bcol[:, :], b_sbcol), (bg[:, :], b_gate),
                             (ptab[:, :], pages), (mst[:, :], m_in), (wg[:, :, :], w_gate)):
                sp_.dma_start(dst, src).then_inc(S["cld"], 16)
            load_pairs(sp_, 0, SLAB0["out0"] + 2)
            sp_.wait_ge(S["cld"], 16 * N_CONST)
            sp_.wait_ge(S["pj_done"], 4 * S_EVEN + CREDIT)
            for g in range(4):
                if g == 2:
                    sp_.wait_ge(S["scr_free"], 1)
                load_k(sp_, 0, 0, g)
            load_pages(sp_)
            sp_.wait_ge(S["b_ev"], 9)
            load_pairs(sp_, SLAB0["out0"] + 2, N_SLABS)
            sp_.wait_ge(S["out"], 16 * N_OUT)

        @block.gpsimd
        def _(pool):
            pool.wait_ge(S["pj_done"], 4 * S_EVEN + CREDIT)
            pool.dma_start(rows[:, R_RST, :], reset[0:H_A, :]).then_inc(S["rst"], 16)
            pool.dma_start(c0[:, :, :, :], c_in).then_inc(S["c0ld"], 16)
            pool.wait_ge(S["pj_act"], 2 * S_EVEN + CREDIT)
            pool.wait_ge(S["pj_dve"], 2 * S_EVEN + CREDIT)
            for b in range(2):
                pool.dma_start(kv_out[:, 4 * b:4 * b + 4, :], pj[:, KBB + 4 * b:KBB + 4 * b + 4, :]).then_inc(S["out"], 16)
            pool.wait_ge(S["gts_ok"], 1)
            pool.dma_start(m_prompt, rows[:, R_M, SEQ - 1:SEQ]).then_inc(S["mout"], 16)
            pool.dma_start(m_sample, mst[:, :]).then_inc(S["mout"], 16)
            pool.wait_ge(S["m_end"], 1)
            pool.dma_start(c_prompt, cfin[:, :, :]).then_inc(S["mout"], 16)
            pool.dma_start(c_sample, c0[:, :, :, :]).then_inc(S["mout"], 16)
            pool.wait_ge(S["mout"], 64)
            pool.sem_inc(S["scr_free"], 2)
            pool.wait_ge(S["n_h"], 2)
            pool.dma_start(wgd[:, :, :], w_gdn).then_inc(S["wgl"], 16)
            pool.dma_start(wgu[:, :], w_gup).then_inc(S["wgl"], 16)
            pool.wait_ge(S["pj_done"], 4 * (PJ0["odd"] + S_ODD) + CREDIT)
            pool.dma_start(rst[:, :], reset).then_inc(S["grst"], 16)
            pool.dma_start(gmk[:, :, :], masks).then_inc(S["grst"], 16)
            pool.dma_start(gm4[:, :, :], masks4).then_inc(S["grst"], 16)
            for j in range(2):
                pool.dma_start(s0b[:, j, :, :], gla_in[j]).then_inc(SLD[j], 16)
            for h in range(H_C):
                pool.wait_ge(S["h_s0"], h + 1)
                pool.dma_start(s_sample[h], s0b[:, h % 2, :, :]).then_inc(S["sst"], 16)
                pool.wait_ge(S["sst"], 16 * h + 16)
                if h + 2 < H_C:
                    pool.dma_start(s0b[:, h % 2, :, :], gla_in[h + 2]).then_inc(SLD[h % 2], 16)
            pool.dma_start(s_prompt.rearrange("h p n -> p h n"), sfin[:, :, :]).then_inc(S["sst"], 16)
            pool.wait_ge(S["sst"], 16 * (H_C + 1))
            pool.sem_inc(S["sfree"], 1)
            pool.wait_ge(S["n_h"], 8)
            pool.dma_start(y_out, hT[:, :, :]).then_inc(S["out"], 16)

        @block.tensor
        def _(pe):
            for name, n in (("lo", 2), ("pj_done", CREDIT), ("pj_act", CREDIT), ("pj_dve", CREDIT), ("dn_done", CREDIT),
                            ("d_dve", CREDIT), ("u_lo", 2), ("k_used", 4), ("v_used", 4), ("b_ev", 1)):
                pe.sem_inc(S[name], n)
            pe.wait_ge(S["cld"], 16 * N_CONST)
            norm_pe(pe, 0)
            gates_pe(pe)
            pe.wait_ge(S["n_lo"], 2)
            proj_pe(pe, "even")
            rows_pe(pe)
            mlstm_pe(pe)
            new_pe(pe)
            attn_pe(pe)
            pe.wait_ge(S["n_lo"], 4)
            proj_pe(pe, "out0")
            norm_pe(pe, 1)
            norm_pe(pe, 2)
            pe.wait_ge(S["n_lo"], 6)
            mlp_pe(pe, 0)
            norm_pe(pe, 3)
            norm_pe(pe, 4)
            gdown_pe(pe)
            pe.wait_ge(S["n_lo"], 8)
            proj_pe(pe, "odd")
            lgate_pe(pe)
            levels_pe(pe)
            gla_pe(pe)
            pe.wait_ge(S["n_lo"], 10)
            proj_pe(pe, "out1")
            norm_pe(pe, 5)
            norm_pe(pe, 6)
            pe.wait_ge(S["n_lo"], 12)
            mlp_pe(pe, 1)
            norm_pe(pe, 7)

        @block.scalar
        def _(act):
            act.preload_act_table_set("natural_log_exp_and_others")
            act.wait_ge(S["xld"], 32)
            act.wait_ge(S["cld"], 16 * N_CONST)
            act.wait_ge(S["rows1"], 1)
            split_hi(act, 0, 0)
            norm_act(act, 0, hT, split=0)
            gates_act(act)
            proj_act(act, "even")
            rows_act(act)
            mlstm_act(act)
            new_act(act)
            attn_act(act)
            act.wait_ge(S["a_o"], 8)
            act.wait_ge(S["b_ev"], 9)
            split_mix_act(act, 1, ((0, 0), (QB, 4)))
            proj_act(act, "out0")
            pj_all(act, "out0")
            norm_act(act, 1, pj[:, 0:8, :])
            act.wait_ge(S["n_h"], 2)
            norm_act(act, 2, hT, split=1)
            mlp_act(act, 0)
            act.wait_ge(S["d_dve"], 128 + CREDIT)
            norm_act(act, 3, pj[:, 0:8, :])
            act.wait_ge(S["n_h"], 4)
            norm_act(act, 4, hT, split=2)
            gdown_act(act)
            proj_act(act, "odd")
            lgate_act(act)
            gla_act(act)
            act.wait_ge(S["h_mix"], 4)
            act.wait_ge(S["sfree"], 1)
            split_mix_act(act, 4, ((VC, 0), (VC + 4, 4)))
            proj_act(act, "out1")
            pj_all(act, "out1")
            norm_act(act, 5, pj[:, 0:8, :])
            act.wait_ge(S["n_h"], 6)
            norm_act(act, 6, hT, split=3)
            mlp_act(act, 1)
            act.wait_ge(S["d_dve"], 256 + CREDIT)
            norm_act(act, 7, pj[:, 0:8, :])

        @block.vector
        def _(dve):
            nonlocal own
            own = Own(dve, S["dve"])
            dve.memset(one[:, :], 1.0)
            dve.memset(eps[:, :], EPS)
            dve.wait_ge(S["cld"], 16 * N_CONST)
            dve.tensor_scalar(nbf[:, :], bg[:, 1:2], -1.0, None, ALU.mult).then_inc(S["rows1"], 1)
            split_lo(dve, 0, 0)
            prenorm_dve(dve, 0, 0, 0, 0)
            proj_dve(dve, "even")
            rows_dve(dve)
            mlstm_dve(dve)
            dve.sem_inc(S["m_end"], 1)
            dve.wait_ge(S["scr_free"], 2)
            new_dve(dve)
            attn_dve(dve)
            split_mix_dve(dve, 1, ((0, 0), (QB, 4)))
            proj_dve(dve, "out0")
            postnorm_dve(dve, 1, 0, 1)
            prenorm_dve(dve, 2, 0, 2, 2)
            mlp_dve(dve, 0)
            postnorm_dve(dve, 3, 0, 3)
            prenorm_dve(dve, 4, 1, 0, 3)
            proj_dve(dve, "odd")
            gla_pre_dve(dve)
            gla_dve(dve)
            split_mix_dve(dve, 4, ((VC, 0), (VC + 4, 4)))
            proj_dve(dve, "out1")
            postnorm_dve(dve, 5, 1, 1)
            prenorm_dve(dve, 6, 1, 2, 5)
            mlp_dve(dve, 1)
            postnorm_dve(dve, 7, 1, 3)


_INS = ["x", "weights", "w_gate", "w_gdn", "w_gup", "k_cache", "v_cache", "pages", "c_in", "gla_in", "m_in", "gains",
        "g_even", "g_odd", "b_gate", "b_gup", "b_sb", "b_sbrow", "b_sbcol",
        "const", "reset", "masks", "masks4"]
_OUTS = [(P, KB, N_TOK), (P, 8, N_TOK), (P, H_A, P + 1), (P, H_A, DEC_B, P + 1), (H_A, 1), (H_A, DEC_B),
         (H_C, P, DV_C), (H_C, P, DEC_B, DV_C)]


def lay_out(i):
    np_ = lambda a: np.ascontiguousarray(a)
    feat = lambda a: np_(a.reshape(a.shape[0], -1, P).transpose(2, 1, 0))
    col = lambda a: np_(a.reshape(-1, P).T)

    def slabs(w):
        n = w.shape[1]
        return w.reshape(KB, P, n // 256, 2, P).transpose(2, 1, 3, 0, 4).reshape(n // 256, P, SLAB_TILES, P)

    def mlp(up, down):
        u = slabs(up).reshape(MLP_GROUPS, 2, P, SLAB_TILES, P)
        d = down.reshape(MLP_GROUPS, 4, P, 2, 4, P).transpose(0, 3, 2, 4, 1, 5).reshape(MLP_GROUPS, 2, P, SLAB_TILES, P)
        return np.concatenate([u, d], axis=1).reshape(-1, P, SLAB_TILES, P)

    we, wo = i["w_in_even"][0], i["w_in_odd"][0]
    ga = 4 * H_A * P
    tok = np.concatenate([i["x_prompt"][0], i["x_sample"].reshape(N_SAMP, D), i["meta_tokens"]])
    stream = np.concatenate([slabs(np.concatenate([we[:, :ga], we[:, ga + 2 * H_A:]], axis=1)), slabs(i["w_out_even"][0]),
                             mlp(i["w_up"][0], i["w_down"][0]), slabs(wo[:, :3072]), slabs(i["w_out_odd"][0]),
                             mlp(i["w_up"][1], i["w_down"][1])])
    n_pool = i["cache_sb_k"].shape[1]
    return {
        "x": feat(tok),
        "weights": np_(stream),
        "w_gate": np_(we[:, ga:ga + 2 * H_A].reshape(KB, P, 2 * H_A).transpose(1, 0, 2)),
        "w_gdn": np_(wo[:, 3072:].reshape(KB, P, 16).transpose(1, 0, 2)),
        "w_gup": np_(i["w_gate_up_odd"][0]),
        "k_cache": np_(i["cache_sb_k"][0].reshape(n_pool, P, 4, P).transpose(0, 3, 2, 1).reshape(n_pool, P, 512)),
        "v_cache": np_(i["cache_sb_v"][0].reshape(n_pool, P, 512)),
        "pages": np_(i["page_table"].reshape(1, -1)),
        "c_in": np_(np.concatenate([i["state_mlstm_c"][0], i["state_mlstm_n"][0][..., None]], axis=-1).transpose(2, 1, 0, 3)),
        "gla_in": np_(i["state_gla_s"][0].transpose(1, 2, 0, 3)),
        "m_in": np_(i["state_mlstm_m"][0].T),
        "gains": np_(i["norm_gains"].reshape(2, 4, KB, P).transpose(3, 0, 1, 2)),
        "g_even": col(i["g_head_even"][0]),
        "g_odd": col(i["g_head_odd"][0]),
        "b_gate": np_(i["b_gate_even"][0].reshape(2, H_A).T),
        "b_gup": col(i["b_gate_up_odd"][0]),
        "b_sb": np_(np.broadcast_to(i["b_sb_even"][0], (P, H_B))),
        "b_sbrow": np_(np.broadcast_to(np.repeat(i["b_sb_even"][0], DEC_T), (P, 32))),
        "b_sbcol": np_(np.tile(np.repeat(i["b_sb_even"][0], DEC_T), 4)[:, None]),
        "const": constants(),
        "reset": reset_row(),
        "masks": level_masks(P, np.zeros(P, int), (64, 32, 16, 8, 4, 2, 1, 0)),
        "masks4": level_masks(T4, (np.arange(T4) < N_SAMP).astype(int), (8, 4, 2, 1, 0)),
    }


def kernel(**inputs):
    import concourse.bacc as _bacc
    from concourse.bass_utils import run_bass_kernel_spmd as _run

    laid = lay_out({k: np.asarray(v) for k, v in inputs.items()})
    nc = _bacc.Bacc("TRN2", target_bir_lowering=False, num_devices=1)
    arrays, args = {}, []
    for name in _INS:
        arrays[f"in_{name}_dram"] = laid[name]
        args.append(nc.dram_tensor(f"in_{name}_dram", laid[name].shape, mybir.dt.from_np(laid[name].dtype),
                                   kind="ExternalInput").ap())
    for i, shape in enumerate(_OUTS):
        args.append(nc.dram_tensor(f"out_{i}_dram", shape, mybir.dt.float32, kind="ExternalOutput").ap())
    build(nc, *args)
    r = _run(nc, [arrays], core_ids=[0])
    y, kv, cp, cs, mp, ms, sp, ss = (r.results[0][f"out_{i}_dram"] for i in range(len(_OUTS)))
    rows = lambda a: a.transpose(2, 1, 0).reshape(N_TOK, -1)
    y, k, v = rows(y), rows(kv[:, 0:4]), rows(kv[:, 4:8])
    prompt = lambda a: np.concatenate([a[META0:], a[:SEQ]]).reshape(1, 1, N_META + SEQ, H_B, DH_B)
    samp = lambda a: a[SAMP0:META0].reshape(1, DEC_B, DEC_T, H_B, DH_B)
    cp, cs = cp.transpose(1, 0, 2), cs.transpose(2, 1, 0, 3)
    out = (y[:SEQ].reshape(1, SEQ, D), y[SAMP0:META0].reshape(DEC_B, DEC_T, D), prompt(k), prompt(v),
           cp[None, None, :, :, :P], cp[None, None, :, :, P], mp.reshape(1, 1, H_A), sp[None, None],
           samp(k), samp(v), cs[None, :, :, :, :P], cs[None, :, :, :, P], ms.T[None], ss.transpose(2, 0, 1, 3)[None])
    return tuple(np.ascontiguousarray(o) for o in out)
```

```python
from contextlib import ExitStack

import numpy as np

import concourse.bass as bass
from concourse import mybir

D = 1024
P = 128
KB = D // P
SEQ, N_META, DEC_B, DEC_T = 512, 16, 8, 4
N_SAMP = DEC_B * DEC_T
N_TOK = SEQ + N_SAMP + N_META
HALF = N_TOK // 2
N_TILE = SEQ // P
SAMP0, META0 = SEQ, SEQ + N_SAMP
T4 = N_SAMP + N_META
H_A, H_B, H_C = 4, 8, 4
DH_B = 64
DV_C = 256
N_PAGES = 16
D_FF = 4 * D
EPS = 1e-6
N_EVEN_BLK = 28
QA, KA, VA, OA, QB, KBB, VB = range(0, 28, 4)
QC, KC, VC, RC = 0, 4, 8, 16
SLAB_TILES = 16
SLAB = SLAB_TILES * P
MLP_GROUPS = D_FF // 512
S_EVEN, S_OUT, S_MLP, S_ODD = 14, 4, 4 * MLP_GROUPS, 12
SLAB0 = {"even": 0, "out0": 14, "mlp0": 18, "odd": 50, "out1": 62, "mlp1": 66}
N_SLABS = 98
NEG = -1e30

C_ID, C_ONE, C_U, C_NEG, C_NEG4, C_SBM, C_SEL, C_SEQM = 0, 128, 256, 384, 512, 560, 688, 1200
C_NEWM = 1208
C_HEAD, C_QRY = C_NEWM + 32, C_NEWM + 40
C_END = C_QRY + DEC_T


def constants():
    c = np.zeros((P, C_END), np.float32)
    i = np.arange(P)
    c[:, C_ID:C_ID + P] = i[:, None] == i[None, :]
    c[:, C_ONE:C_ONE + P] = 1
    c[:, C_U:C_U + P] = i[:, None] > i[None, :]
    c[:, C_NEG:C_NEG + P] = np.where(i[:, None] <= i[None, :], 0, NEG)
    grp = np.where(i[:T4] < N_SAMP, i[:T4] // DEC_T, DEC_B)
    same = (grp[:, None] == grp[None, :]) & (i[:T4, None] <= i[None, :T4])
    c[:T4, C_NEG4:C_NEG4 + T4] = np.where(same, 0, NEG)
    c[:, C_SBM:C_SBM + P] = i[:, None] < i[None, :]
    for h in range(H_A):
        c[h, C_SEL + h * P:C_SEL + (h + 1) * P] = 1
    c[:N_SAMP, C_SEQM:C_SEQM + DEC_B] = (i[:N_SAMP, None] // DEC_T) == np.arange(DEC_B)[None, :]
    c[:N_SAMP, C_NEWM:C_NEWM + N_SAMP] = same[:N_SAMP, :N_SAMP] & (i[:N_SAMP, None] < i[None, :N_SAMP])
    c[:, C_HEAD:C_HEAD + H_B] = (i[:, None] % (H_B * DEC_T) // DEC_T) == np.arange(H_B)[None, :]
    c[:, C_QRY:C_QRY + DEC_T] = (i[:, None] % DEC_T) == np.arange(DEC_T)[None, :]
    return c


def reset_row():
    r = np.ones((P, N_TOK), np.float32)
    r[:, 0:SEQ:P] = 0
    r[:, SAMP0:META0:DEC_T] = 0
    r[:, META0] = 0
    return r


def level_masks(n, decode, levels):
    i = np.arange(n)
    out = np.zeros((n, len(levels), n), np.int32)
    for a, w in enumerate(levels):
        m = i[:, None] == i[None, :]
        if w:
            m = (i[:, None] // (2 * w) == i[None, :] // (2 * w)) & (i[:, None] % (2 * w) < w) & (i[None, :] % (2 * w) >= w)
            if 2 * w > DEC_T:
                m &= (decode[:, None] == 0) & (decode[None, :] == 0)
        out[:, a, :] = m
    return out


class Own:

    def __init__(self, eng, sem):
        self.eng, self.sem, self.n, self.loop, self.per = eng, sem, 0, 0, 0

    def link(self, ins):
        self.n += 1
        ins.then_inc(self.sem, 1)
        self.eng.wait_ge(self.sem, self.loop + self.n)

    def start(self, i, per):
        self.loop, self.per, self.n0 = i * per, per, self.n

    def end(self, trips):
        assert self.n - self.n0 == self.per, f"steps per iteration: {self.n - self.n0}"
        self.n, self.loop = self.n0 + trips * self.per, 0



def build(nc, x, weights, w_gate, w_gdn, w_gup, k_cache, v_cache, pages, c_in, gla_in, m_in, gains, g_even, g_odd,
          b_gate, b_gup, b_sb, b_sbrow, b_sbcol, const, reset, masks, masks4,
          y_out, kv_out, c_prompt, c_sample, m_prompt, m_sample, s_prompt, s_sample):
    f32, f32r, i32 = mybir.dt.float32, mybir.dt.float32r, mybir.dt.int32
    ALU, ACT = mybir.AluOpType, mybir.ActivationFunctionType
    ctx = ExitStack()
    with ctx:
        sbuf0 = (nc.sbuf_base + 63) // 64 * 64

        def at(name, off, shape, dt=f32):
            return nc.alloc_sbuf_tensor_at(name, shape, dt, offset=sbuf0 + off)

        def sem(name):
            return ctx.enter_context(nc.semaphore(name))

        ROW = N_TOK * 4
        o_hT = 0
        o_M = o_hT + KB * ROW
        o_xn = o_M + 24 * ROW
        o_raw = o_xn + KB * ROW
        o_hi = o_raw + 2 * SLAB * 4
        o_lo = o_hi + 2 * SLAB * 4
        o_pj = o_lo + 2 * SLAB * 4
        o_c = o_pj + N_EVEN_BLK * ROW
        o_s = o_c + (C_END * 4 + 31) // 32 * 32
        hT = at("hT", o_hT, [P, KB, N_TOK])
        xhi = at("xhi", o_M, [P, KB, N_TOK], f32r)
        xlo = at("xlo", o_M + KB * ROW, [P, KB, N_TOK], f32r)
        dhi = at("dhi", o_M + 16 * ROW, [P, 4, N_TOK], f32r)
        dlo = at("dlo", o_M + 20 * ROW, [P, 4, N_TOK], f32r)
        xn = at("xn", o_xn, [P, KB, N_TOK])
        raw = at("raw", o_raw, [P, 2, SLAB_TILES, P])
        whi = at("whi", o_hi, [P, 2, SLAB_TILES, P], f32r)
        wlo = at("wlo", o_lo, [P, 2, SLAB_TILES, P], f32r)
        pj = at("pj", o_pj, [P, N_EVEN_BLK, N_TOK])
        relu = at("relu", o_pj + 24 * ROW, [P, 2, HALF])
        rsq = at("rsq", o_pj + 25 * ROW, [P, 2, HALF])
        rstd = at("rstd", o_pj + 26 * ROW, [P, 2, HALF])
        cst = at("cst", o_c, [P, C_END])
        gn = at("gn", o_s, [P, 2, 4, KB])
        gev = at("gev", o_s + 256, [P, H_A])
        god = at("god", o_s + 288, [P, 8])
        bgu = at("bgu", o_s + 320, [P, H_C])
        bsb = at("bsb", o_s + 352, [P, H_B])
        bsr = at("bsr", o_s + 384, [P, 32])
        bg = at("bg", o_s + 512, [H_A, 2])
        nbf = at("nbf", o_s + 544, [H_A, 1])
        one_eps = at("one_eps", o_s + 576, [P, 2])
        one, eps = one_eps[:, 0:1], one_eps[:, 1:2]
        bcol = at("bcol", o_s + 608, [P, 1])
        ptab = at("ptab", o_s + 640, [1, P], i32)
        mst = at("mst", o_s + 1152, [H_A, DEC_B])
        grow = at("grow", o_s + 1184, [H_A, 2, N_TOK])
        assert sbuf0 + o_s + 1184 + 2 * ROW <= nc.sbuf_usable_end
        ident = cst[:, C_ID:C_ID + P]
        ones = cst[:, C_ONE:C_ONE + P]
        after = cst[:, C_U:C_U + P]
        strict = cst[:, C_SBM:C_SBM + P]

        ps = ctx.enter_context(nc.psum_tensor("ps", [P, 8, 512], f32))

        wg = at("wg", o_pj, [P, KB, 40])
        rows = at("rows", o_xn, [H_A, 8, N_TOK])
        R_B, R_M, R_RM, R_W, R_A, R_WK, R_T, R_RST = range(8)
        cfin = at("cfin", o_xn + R_RST * ROW, [P, H_A, P + 1])
        c0 = at("c0", o_M, [P, H_A, DEC_B, P + 1])
        o = o_M + 9 * ROW
        gts = at("gts", o, [P, 5, 16]); o += 320
        ext = at("ext", o_pj + 27 * ROW, [H_A, 3, DEC_B, 5])
        gh = at("gh", o, [P, 5, 4]); o += 96
        wdh = at("wdh", o, [P, 12]); o += 64
        ghc = at("ghc", o, [P, 1]); o += 32
        den = at("den", o, [P, 5]); o += 32
        rec = at("rec", o, [P, 5]); o += 32
        ssq = at("ssq", o, [P, 5]); o += 32
        rs5 = at("rs5", o, [P, 5]); o += 32
        selh = at("selh", o, [H_A, P]); o += 512
        qkv = at("qkv", o, [P, 3, N_TOK]); o += 3 * ROW
        kw = at("kw", o, [P, 5, P]); o += 2560
        vx = at("vx", o, [P, 5, P + 1]); o += 2624
        dec = at("dec", o, [P, N_TOK]); o += ROW
        sT = at("sT", o, [P, N_TOK]); o += ROW
        Cs = at("Cs", o, [P, 5, P + 1]); o += 2624
        qm = at("qm", o, [P, 288]); o += 1152
        hx = at("hx", o, [P, 5, P + 1]); o += 2624
        hn = at("hn", o, [P, 5, P]); o += 2560
        kwm = at("kwm", o, [N_SAMP, DEC_B, P]); o += 4096
        so = at("so", o_s + 1184, [P, N_TOK])
        assert o <= o_xn

        PG = N_PAGES // 4
        GB = PG * 4 * P * 4
        ROWN = 4 * DEC_B
        o_V = o_M + H_A * DEC_B * (P + 1) * 4
        kbuf = [at(f"kbuf{g}", (o_hi + GB, o_lo + GB, o_M, o_M + GB)[g], [P, PG, 4, P]) for g in range(4)]
        vbuf = [at(f"vbuf{g}", o_V + g * GB, [P, PG, 4 * P]) for g in range(4)]
        assert 2 * GB <= o_V - o_M
        o = o_V + 4 * GB
        qbd = at("qbd", o, [P, 4, DEC_B, 8]); o += 1024
        zn = at("zn", o, [N_SAMP, 256]); o += 1024
        ln_ = at("ln_", o, [N_SAMP, 256]); o += 1024
        spn = at("spn", o, [N_SAMP, 256]); o += 1024
        mw = at("mw", o, [N_META, N_META]); o += 64
        assert o <= o_xn
        o = o_raw
        zg = at("zg", o, [P, N_PAGES, ROWN]); o += 2048
        lg = at("lg", o, [P, 2, N_PAGES, ROWN]); o += 4096
        osn = at("osn", o, [P, 256]); o += 1024
        qs = at("qs", o, [P, 4, 40]); o += 640
        assert o <= o_raw + SLAB * 4
        o = o_pj + 4 * ROW
        WZ = 1280
        WA = WZ + SEQ + N_META
        z = at("z", o, [P, WA]); o += 4 * WA
        lz = at("lz", o, [P, WA]); o += 4 * WA
        sp = at("sp", o, [P, WA]); o += 4 * WA
        qz = at("qz", o, [P, 2, N_TOK]); o += 2 * ROW
        assert o <= o_pj + 16 * ROW
        o = o_xn
        vnew = at("vnew", o, [N_SAMP, 4, P])
        outm = at("outm", o, [P, 4 * P]); o += 2048
        kP = at("kP", o, [P, N_TOK]); o += ROW
        vF = at("vF", o, [P, N_TOK]); o += ROW
        vP = at("vP", o, [P, 5, P]); o += 2560
        sg = at("sg", o, [P, ROWN, 1 + N_PAGES]); o += 2176
        ssg = at("ssg", o, [P, ROWN, 1 + N_PAGES]); o += 2176
        smk = at("smk", o, [P, ROWN, 1 + N_PAGES]); o += 2176
        bh = at("bh", o, [P, 2]); o += 32
        assert o <= o_xn + R_RST * ROW
        zr = at("zr", o, [P, PG * P]); o += 2048
        assert o <= o_raw
        KOFF = [0, 512, 896, 1152]

        own = None
        NAMES = """rout mout xld cld out hi lo pj_done pj_act pj_dve gate gate_ev up_done dn_done
            u_act u_hi u_lo d_dve n_sq n_ss n_rs n_xn n_hi n_lo n_h dve act rst rows1 rows2 gt gts_ok
            m_cp m_tr m_bc m_qk m_si m_kv m_D m_so m_S m_kvs m_in m_C m_it m_hn m_rs m_y m_yt m_end m_mix
            a_in a_z a_l a_sp a_A a_t a_w a_v a_o k_used v_used v_turn b_z b_zr b_q b_om b_o b_l b_sp b_A b_t b_w b_ev
            v_tr v_ev r_a r_e c0ld m_a m_sq d_q d_z d_sp d_A d_w d_o d_zs d_l d_t d_e a_x a_x2 a_e b_x wgl gd_ps gd_ok g_sp g_lg g_nb g_a g_l g_ex g_E g_el g_x g_p g_c grst h_cp h_tr h_kv h_kvs h_S h_t4 h_s0 h_rs h_y h_yt h_mix h_a h_sg h_o h_q h_b sst sfree
            """.split()
        S = {n: sem(n) for n in NAMES}

        def expv(act, out, in_, **k):
            return act.activation(out, in_, ACT.Exp, **k)

        RAW = [sem("raw0"), sem("raw1")]
        CREDIT = 16

        def load_pairs(sp_, first, last):
            with sp_.Fori(first // 2, last // 2) as i:
                for par in range(2):
                    sp_.wait_ge(S["lo"], i * 2 + (par + 1))
                    sp_.dma_start(raw[:, par], weights[bass.ds(i * 2 + par, 1), :, :, :]
                                  .rearrange("a p t c -> (a p) t c")).then_inc(RAW[par], 16)

        def split_hi(act, half_s, par):
            act.wait_ge(RAW[par], half_s * 16 + 16)
            act.activation(whi[:, par], raw[:, par], ACT.Copy).then_inc(S["hi"], 1)

        def split_lo(dve, half_s, par):
            dve.wait_ge(S["hi"], half_s * 2 + (par + 1))
            dve.tensor_tensor(wlo[:, par], raw[:, par], whi[:, par].bitcast(f32), ALU.subtract).then_inc(S["lo"], 1)

        def product(pe, out, par, t, hi, lo, first, last):
            pe.matmul(out, whi[:, par, t, :], hi, start=first, stop=False)
            pe.matmul(out, whi[:, par, t, :], lo, start=False, stop=False)
            return pe.matmul(out, wlo[:, par, t, :], hi, start=False, stop=last)

        NS = {"even": S_EVEN, "out0": S_OUT, "odd": S_ODD, "out1": S_OUT}
        PJ0 = {"even": 0, "out0": S_EVEN, "odd": S_EVEN + S_OUT, "out1": S_EVEN + S_OUT + S_ODD}
        COLS = [slice(0, HALF), slice(HALF, N_TOK)]

        def proj_pe(pe, name):
            s0, n0 = SLAB0[name], PJ0[name]
            with pe.Fori(0, NS[name] // 2) as i:
                for par in range(2):
                    pe.wait_ge(S["lo"], i * 2 + (s0 + par + 3))
                    for f in range(2):
                        for h in range(2):
                            bank = 4 * par + 2 * f + h
                            pe.wait_ge(S[("pj_act", "pj_dve")[h]], i * 4 + (2 * n0 + 2 * par + f + 1 + CREDIT - 4))
                            for k in range(KB):
                                mm = product(pe, ps[:, bank, 0:HALF], par, f * KB + k, xhi[:, k, COLS[h]],
                                             xlo[:, k, COLS[h]], k == 0, k == KB - 1)
                            mm.then_inc(S["pj_done"], 1)

        def proj_turns(eng, name, turn, beside):
            if beside:
                turn(0, beside)
            with eng.Fori(1 if beside else 0, NS[name] // 2) as i:
                turn(i, None)

        def proj_act(act, name, beside=None):
            s0, n0 = SLAB0[name], PJ0[name]

            def turn(i, beside):
                for par in range(2):
                    act.wait_ge(S["pj_done"], i * 8 + (4 * (n0 + par) + CREDIT))
                    split_hi(act, i + (s0 + par + 1) // 2, 1 - par)
                    if beside and par == 0:
                        beside(act)
                    for f in range(2):
                        act.wait_ge(S["pj_done"], i * 8 + (4 * (n0 + par) + 2 * f + 1 + CREDIT))
                        act.activation(pj[:, bass.ds(i * 4 + (2 * par + f), 1), COLS[0]], ps[:, 4 * par + 2 * f, 0:HALF],
                                       ACT.Copy).then_inc(S["pj_act"], 1)
            proj_turns(act, name, turn, beside)

        def proj_dve(dve, name, beside=None):
            s0, n0 = SLAB0[name], PJ0[name]

            def turn(i, beside):
                for par in range(2):
                    split_lo(dve, i + (s0 + par + 1) // 2, 1 - par)
                    if beside and par == 0:
                        beside(dve)
                    for f in range(2):
                        dve.wait_ge(S["pj_done"], i * 8 + (4 * (n0 + par) + 2 * f + 2 + CREDIT))
                        dve.tensor_copy(pj[:, bass.ds(i * 4 + (2 * par + f), 1), COLS[1]],
                                        ps[:, 4 * par + 2 * f + 1, 0:HALF]).then_inc(S["pj_dve"], 1)
            proj_turns(dve, name, turn, beside)

        def pj_all(eng, name):
            n = 2 * (PJ0[name] + NS[name]) + CREDIT
            eng.wait_ge(S["pj_act"], n)
            eng.wait_ge(S["pj_dve"], n)

        def mlp_pe(pe, L):
            s0, d0, u0 = SLAB0[f"mlp{L}"], 128 * L + CREDIT, 64 * L
            with pe.Fori(0, MLP_GROUPS) as g:
                for par in range(2):
                    pe.wait_ge(S["lo"], g * 4 + (s0 + par + 3))
                    for f in range(2):
                        for h in range(2):
                            j = 4 * par + 2 * f + h
                            pe.wait_ge(S["d_dve"], g * 16 + (d0 - 8 + j + 1))
                            for k in range(KB):
                                mm = product(pe, ps[:, j, 0:HALF], par, f * KB + k, xhi[:, k, COLS[h]],
                                             xlo[:, k, COLS[h]], k == 0, k == KB - 1)
                            mm.then_inc(S["up_done"], 1)
                for par in range(2):
                    pe.wait_ge(S["lo"], g * 4 + (s0 + par + 5))
                    for h in range(2):
                        if par == 0:
                            pe.wait_ge(S["u_lo"], g * 8 + (u0 + 9 + h))
                        for d in range(4):
                            j = 4 * h + d
                            if par == 0:
                                pe.wait_ge(S["u_act"], g * 8 + (u0 + j + 1))
                            else:
                                pe.wait_ge(S["d_dve"], g * 16 + (d0 + j + 1))
                            for k in range(4):
                                mm = product(pe, ps[:, j, 0:HALF], par, d * 4 + k, dhi[:, k, COLS[h]],
                                             dlo[:, k, COLS[h]], k == 0, k == 3)
                            mm.then_inc(S["dn_done"], 1)

        def mlp_act(act, L):
            s0, d0, u0 = SLAB0[f"mlp{L}"], 128 * L + CREDIT, 64 * L

            def group(g, last=False):
                for par in range(2):
                    if par == 0:
                        act.wait_ge(S["dn_done"], g * 16 + d0)
                    else:
                        act.wait_ge(S["up_done"], g * 8 + (u0 + 4))
                    split_hi(act, g * 2 + (s0 + par + 1) // 2, 1 - par)
                    for f in range(2):
                        for h in range(2):
                            j = 4 * par + 2 * f + h
                            act.wait_ge(S["up_done"], g * 8 + (u0 + j + 1))
                            act.wait_ge(S["u_lo"], g * 8 + (u0 + j + 1))
                            act.activation(relu[:, h], ps[:, j, 0:HALF], ACT.Relu).then_inc(S["u_act"], 1)
                            act.wait_ge(S["u_act"], g * 8 + (u0 + j + 1))
                            act.activation(dhi[:, 2 * par + f, COLS[h]], relu[:, h], ACT.Square).then_inc(S["u_hi"], 1)
                act.wait_ge(S["up_done"], g * 8 + (u0 + 8))
                split_hi(act, g * 2 + (s0 + 2) // 2, 1)
                if not last:
                    act.wait_ge(S["dn_done"], g * 16 + (d0 + 8))
                    split_hi(act, g * 2 + (s0 + 4) // 2, 0)
            with act.Fori(0, MLP_GROUPS - L) as g:
                group(g)
            if L:
                group(MLP_GROUPS - 1, last=True)

        def mlp_dve(dve, L):
            s0, d0, u0 = SLAB0[f"mlp{L}"], 128 * L + CREDIT, 64 * L
            own.link(dve.memset(pj[:, 0:8, :], 0.0))

            def group(g, last=False):
                for par in range(2):
                    split_lo(dve, g * 2 + (s0 + par + 1) // 2, 1 - par)
                    for f in range(2):
                        for h in range(2):
                            j = 4 * par + 2 * f + h
                            dve.wait_ge(S["u_hi"], g * 8 + (u0 + j + 1))
                            own.link(dve.tensor_tensor(rsq[:, h], relu[:, h], relu[:, h], ALU.mult))
                            dve.tensor_tensor(dlo[:, 2 * par + f, COLS[h]], rsq[:, h],
                                              dhi[:, 2 * par + f, COLS[h]].bitcast(f32), ALU.subtract)\
                               .then_inc(S["u_lo"], 1)
                split_lo(dve, g * 2 + (s0 + 2) // 2, 1)
                for par in range(2):
                    if par == 1 and not last:
                        split_lo(dve, g * 2 + (s0 + 4) // 2, 0)
                    for h in range(2):
                        for d in range(4):
                            dve.wait_ge(S["dn_done"], g * 16 + (d0 + 8 * par + 4 * h + d + 1))
                            y = pj[:, 4 * par + d, COLS[h]]
                            dve.tensor_tensor(y, ps[:, 4 * h + d, 0:HALF], y, ALU.add).then_inc(S["d_dve"], 1)
            with dve.Fori(0, MLP_GROUPS - L) as g:
                own.start(g, 8)
                group(g)
                own.end(MLP_GROUPS - L)
            if L:
                group(MLP_GROUPS - 1, last=True)

        def norm_act(act, n, src, split=None, after=None, first=False):
            for h in range(2):
                m = 2 * n + h
                if after is not None:
                    act.wait_ge(S["n_h"], after + h + 1)
                act.activation(xn[:, :, COLS[h]], src[:, :, COLS[h]], ACT.Square).then_inc(S["n_sq"], 1)
            if first:
                act.wait_ge(S["rows1"], 1)
                split_hi(act, 0, 0)
            for h in range(2):
                m = 2 * n + h
                act.wait_ge(S["n_ss"], m + 1)
                act.activation(rstd[:, h], ps[:, h, 0:HALF], ACT.Ln, bias=eps[:, 0:1], scale=1.0 / D)\
                   .then_inc(S["act"], 1)
                act.wait_ge(S["act"], m + 1)
                act.activation(rstd[:, h], rstd[:, h], ACT.Exp, scale=-0.5).then_inc(S["n_rs"], 1)
            if split is not None:
                for h in range(2):
                    act.wait_ge(S["n_xn"], 2 * split + h + 1)
                    act.activation(xhi[:, :, COLS[h]], xn[:, :, COLS[h]], ACT.Copy).then_inc(S["n_hi"], 1)

        def norm_pe(pe, n):
            for h in range(2):
                pe.wait_ge(S["n_sq"], 2 * n + h + 1)
                for k in range(KB):
                    mm = pe.matmul(ps[:, h, 0:HALF], ones, xn[:, k, COLS[h]], start=k == 0, stop=k == KB - 1)
                mm.then_inc(S["n_ss"], 1)

        def prenorm_dve(dve, n, L, g, q):
            for h in range(2):
                dve.wait_ge(S["n_rs"], 2 * n + h + 1)
                for k in range(KB):
                    ins = dve.scalar_tensor_tensor(xn[:, k, COLS[h]], hT[:, k, COLS[h]], gn[:, L, g, k:k + 1],
                                                   rstd[:, h], ALU.mult, ALU.mult)
                ins.then_inc(S["n_xn"], 1)
            split_x(dve, q)

        def split_x(dve, q):
            for h in range(2):
                dve.wait_ge(S["n_hi"], 2 * q + h + 1)
                dve.tensor_tensor(xlo[:, :, COLS[h]], xn[:, :, COLS[h]], xhi[:, :, COLS[h]].bitcast(f32), ALU.subtract)\
                   .then_inc(S["n_lo"], 1)

        def postnorm_dve(dve, n, L, g):
            for h in range(2):
                dve.wait_ge(S["n_rs"], 2 * n + h + 1)
                for k in range(KB):
                    ins = dve.scalar_tensor_tensor(xn[:, k, COLS[h]], pj[:, k, COLS[h]], gn[:, L, g, k:k + 1],
                                                   rstd[:, h], ALU.mult, ALU.mult)
                own.link(ins)
                dve.tensor_tensor(hT[:, :, COLS[h]], hT[:, :, COLS[h]], xn[:, :, COLS[h]], ALU.add).then_inc(S["n_h"], 1)

        def split_mix_act(act, q, parts):
            for src, dst in parts:
                act.activation(xhi[:, dst:dst + 4, :], pj[:, src:src + 4, :], ACT.Copy).then_inc(S["n_hi"], 1)

        def split_mix_dve(dve, q, parts):
            for j, (src, dst) in enumerate(parts):
                dve.wait_ge(S["n_hi"], 2 * q + j + 1)
                dve.tensor_tensor(xlo[:, dst:dst + 4, :], pj[:, src:src + 4, :], xhi[:, dst:dst + 4, :].bitcast(f32),
                                  ALU.subtract).then_inc(S["n_lo"], 1)

        def gates_pe(pe):
            pe.wait_ge(S["n_xn"], 2)
            pe.wait_ge(S["cld"], 16 * N_CONST)
            for h in range(2):
                for k in range(KB):
                    mm = pe.matmul(ps[0:40, 4 + h, 0:HALF], wg[:, k, :], xn[:, k, COLS[h]], start=k == 0, stop=k == KB - 1)
            mm.then_inc(S["gate"], 1)
            pe.wait_ge(S["gate_ev"], 4)

        def gates_act(act):
            act.wait_ge(S["gate"], 1)
            act.wait_ge(S["rows1"], 1)
            for h in range(2):
                act.activation(grow[:, 0, COLS[h]], ps[0:H_A, 4 + h, 0:HALF], ACT.Identity, bias=bg[:, 0:1])\
                   .then_inc(S["gate_ev"], 1)
                act.activation(grow[:, 1, COLS[h]], ps[32:32 + H_A, 4 + h, 0:HALF], ACT.Identity, bias=nbf[:, 0:1], scale=-1.0)\
                   .then_inc(S["gate_ev"], 1)

        def rows_act(act):
            act.wait_ge(S["n_lo"], 2)
            act.wait_ge(S["gate_ev"], 4)
            t = rows[:, R_T, :]
            for k, (src, fn, kw_) in enumerate(((grow[:, 1, :], ACT.Abs, {}), (t, ACT.Exp, {"scale": -1.0}),
                                                (t, ACT.Ln, {"bias": one[0:H_A, 0:1]}))):
                act.activation(t, src, fn, **kw_).then_inc(S["r_a"], 1)
                act.wait_ge(S["r_a"], k + 1)
            act.wait_ge(S["rows2"], 1)
            for r in (R_W, R_WK, R_T):
                act.activation(rows[:, r, :], rows[:, r, :], ACT.Exp, scale=-1.0 if r == R_T else 1.0)\
                   .then_inc(S["r_e"], 1)

        def rows_dve(dve):
            R = lambda k: rows[:, k, :]
            dve.wait_ge(S["r_a"], 3)
            dve.wait_ge(S["rst"], 16)
            lf = grow[:, 1, :]
            own.link(dve.scalar_tensor_tensor(lf, lf, 0.0, R(R_T), ALU.max, ALU.add))
            own.link(dve.tensor_scalar(lf, lf, -1.0, None, ALU.mult))
            own.link(dve.tensor_tensor_scan(R(R_B), R(R_RST), lf, 0.0, ALU.mult, ALU.add))
            gi = grow[:, 0, :]
            own.link(dve.tensor_tensor_scan(rows[:, R_M, META0:N_TOK], lf[:, META0:N_TOK], gi[:, META0:N_TOK],
                                            0.0, ALU.add, ALU.max))
            own.link(dve.tensor_tensor_scan(rows[:, R_M, 0:SEQ], lf[:, 0:SEQ], gi[:, 0:SEQ],
                                            rows[:, R_M, N_TOK - 1:N_TOK], ALU.add, ALU.max))
            dve.memset(ext[:, 0], NEG)
            own.link(dve.tensor_copy(ext[:, 1, :, 0:1], mst[:, :].rearrange("p (s o) -> p s o", o=1)))
            own.link(dve.tensor_copy(ext[:, 0, :, 1:5],
                                     lf[:, SAMP0:META0].rearrange("p (s t) -> p s t", t=DEC_T)))
            own.link(dve.tensor_copy(ext[:, 1, :, 1:5], gi[:, SAMP0:META0].rearrange("p (s t) -> p s t", t=DEC_T)))
            own.link(dve.tensor_tensor_scan(ext[:, 2].rearrange("p s t -> p (s t)"), ext[:, 0].rearrange("p s t -> p (s t)"),
                                            ext[:, 1].rearrange("p s t -> p (s t)"), 0.0, ALU.add, ALU.max))
            own.link(dve.tensor_copy(rows[:, R_M, SAMP0:META0].rearrange("p (s t) -> p s t", t=DEC_T), ext[:, 2, :, 1:5]))
            own.link(dve.tensor_tensor(R(R_RM), R(R_B), R(R_M), ALU.subtract))
            own.link(dve.tensor_tensor(R(R_A), gi, R(R_B), ALU.subtract))
            own.link(dve.memset(rows[:, R_W, META0:N_TOK], 0.0))
            own.link(dve.tensor_copy(rows[:, R_W, 0:P], rows[:, R_M, N_TOK - 1:N_TOK].to_broadcast([H_A, P])))
            chunk = lambda r, a, b: rows[:, r, a:b].rearrange("p (c t) -> p c t", t=P)
            own.link(dve.tensor_copy(chunk(R_W, P, SEQ), chunk(R_M, 0, SEQ - P)[:, :, P - 1:P].to_broadcast([H_A, 3, P])))
            samp = lambda r: rows[:, r, SAMP0:META0].rearrange("p (s t) -> p s t", t=DEC_T)
            own.link(dve.tensor_copy(samp(R_W), ext[:, 2, :, 0:1].to_broadcast([H_A, DEC_B, DEC_T])))
            own.link(dve.tensor_tensor(R(R_W), R(R_W), R(R_RM), ALU.add))
            own.link(dve.tensor_copy(chunk(R_WK, 0, SEQ), chunk(R_RM, 0, SEQ)[:, :, P - 1:P].to_broadcast([H_A, 4, P])))
            own.link(dve.tensor_copy(samp(R_WK), samp(R_RM)[:, :, DEC_T - 1:DEC_T].to_broadcast([H_A, DEC_B, DEC_T])))
            own.link(dve.tensor_copy(rows[:, R_WK, META0:N_TOK], rows[:, R_RM, N_TOK - 1:N_TOK].to_broadcast([H_A, N_META])))
            own.link(dve.tensor_tensor(R(R_WK), R(R_WK), R(R_A), ALU.add))
            dve.tensor_copy(R(R_T), R(R_M)).then_inc(S["rows2"], 1)

        def cols_dve(dve):
            pj_all(dve, "even")
            own.link(dve.memset(gts[:, :, :], 1.0))
            dve.wait_ge(S["gt"], 1)
            dve.tensor_copy(gts[:, 0:4, :], ps[:, 0, 0:64].rearrange("p (c q) -> p c q", q=16))
            own.link(dve.tensor_copy(gts[0:T4, 4, :], ps[0:T4, 0, 64:80]))
            own.link(dve.memset(hx[:, :, :], 1.0))
            own.link(dve.memset(hn[:, :, :], 0.0))
            own.link(dve.memset(qm[:, :], 0.0))
            own.link(dve.tensor_copy(mst[:, :], rows[:, R_M, SAMP0 + DEC_T - 1:META0:DEC_T]))
            dve.sem_inc(S["gts_ok"], 1)

        def rows_pe(pe):
            pj_all(pe, "even")
            pe.wait_ge(S["r_e"], 3)
            for c in range(5):
                n = P if c < 4 else T4
                for q, r in enumerate((R_W, R_A, R_WK, R_T)):
                    mm = pe.transpose(ps[0:n, 0, 16 * c + 4 * q:16 * c + 4 * q + 4], rows[:, r, P * c:P * c + n],
                                      ident[0:H_A, 0:H_A])
            mm.then_inc(S["gt"], 1)

        W_, A_, WK_, EM_ = range(4)
        P1 = P + 1

        def head_dve(dve, i):
            one_ = lambda b: pj[:, bass.ds(i + b, 1), :].rearrange("p a n -> p (a n)")
            dve.tensor_scalar(qkv[:, 0, :], one_(QA), 1.0, None, ALU.mult)
            dve.tensor_scalar(qkv[:, 1, :], one_(KA), float(P) ** -0.5, None, ALU.mult)
            dve.tensor_copy(qkv[:, 2, :], one_(VA))
            dve.tensor_copy(selh[:, :], cst[0:H_A, bass.ds(i * P + C_SEL, P)])
            own.link(dve.tensor_copy(gh[:, :, :], gts[:, :, :].rearrange("p c (q h) -> p c q h", h=4)
                                     [:, :, :, bass.ds(i, 1)].rearrange("p c q h -> p c (q h)")))
            dve.tensor_copy(qm[:, :].rearrange("p (s c) -> p s c", c=36)[:, :, 0:4],
                            qkv[:, 0, SAMP0:META0].rearrange("p (s t) -> p s t", t=DEC_T)).then_inc(S["m_cp"], 1)

        def heads(eng, turn, own_steps=None):
            with eng.Fori(0, H_A - 1) as i:
                if own_steps:
                    own.start(i, own_steps)
                turn(i, False)
                if own_steps:
                    own.end(H_A - 1)
            turn(H_A - 1, True)

        def mlstm_dve(dve):
            def turn(i, last):
                dve.wait_ge(S["m_tr"], i + 1)
                dve.memset(vx[:, :, P:P1], 1.0)
                dve.tensor_copy(vx[:, 0:4, 0:P], ps[:, 1, :].rearrange("p (c n) -> p c n", n=P))
                dve.tensor_copy(vx[0:T4, 4, 0:P], ps[0:T4, 2, P:2 * P])
                dve.tensor_tensor(kw[:, 0:4, :], ps[:, 0, :].rearrange("p (c n) -> p c n", n=P),
                                  gh[:, 0:4, WK_:WK_ + 1].to_broadcast([P, 4, P]), ALU.mult)
                own.link(dve.tensor_scalar(kw[0:T4, 4, :], ps[0:T4, 2, 0:P], gh[0:T4, 4, WK_:WK_ + 1], None, ALU.mult))
                dve.tensor_tensor(kwm[:, :, :], kw[0:N_SAMP, 4:5, :].to_broadcast([N_SAMP, DEC_B, P]),
                                  cst[0:N_SAMP, C_SEQM:C_SEQM + DEC_B].rearrange("p (s o) -> p s o", o=1)
                                  .to_broadcast([N_SAMP, DEC_B, P]), ALU.mult).then_inc(S["m_kv"], 1)
                dve.wait_ge(S["m_bc"], i + 1)
                dve.wait_ge(S["m_D"], i + 1)
                own.link(dve.tensor_copy(wdh[:, :], ps[:, 4, 64:76]))
                dve.wait_ge(S["m_qk"], i + 1)
                dve.tensor_tensor(sT[:, 0:SEQ], ps[:, 5, :], dec[:, 0:SEQ], ALU.mult)
                dve.tensor_tensor(sT[0:T4, SEQ:N_TOK], ps[0:T4, 6, 0:T4], dec[0:T4, SEQ:N_TOK], ALU.mult)\
                   .then_inc(S["m_S"], 1)
                dve.wait_ge(S["m_kvs"], i + 1)
                own.link(dve.tensor_copy(Cs[:, 0, :], ps[:, 0, 0:P1]))
                for c in range(4):
                    kv = ps[:, 0, (c + 1) * P1:(c + 2) * P1] if c < 2 else ps[:, 1, (c - 2) * P1:(c - 1) * P1]
                    own.link(dve.scalar_tensor_tensor(Cs[:, c + 1, :], Cs[:, c, :], wdh[:, c:c + 1], kv, ALU.mult, ALU.add))
                dve.tensor_copy(cfin[:, bass.ds(i, 1), :], Cs[:, 4:5, :]).then_inc(S["m_C"], 1)
                dve.wait_ge(S["m_in"], i + 1)
                dve.tensor_copy(hx[0:T4, 4, :], ps[0:T4, 5, 0:P1])
                dve.tensor_copy(hx[:, 0:2, :], ps[:, 5, P1:3 * P1].rearrange("p (c n) -> p c n", n=P1))
                own.link(dve.tensor_copy(hx[:, 2:4, :], ps[:, 6, 0:2 * P1].rearrange("p (c n) -> p c n", n=P1)))
                dve.wait_ge(S["m_it"], i + 1)
                own.link(dve.scalar_tensor_tensor(hx[0:N_SAMP, 4, :], ps[0:N_SAMP, 7, 0:P1], gh[0:N_SAMP, 4, W_:W_ + 1],
                                                  hx[0:N_SAMP, 4, :], ALU.mult, ALU.add))
                for s in range(DEC_B):
                    kv = ps[:, 2 + s // 3, (s % 3) * P1:(s % 3 + 1) * P1]
                    st = c0[:, bass.ds(i, 1), s, :].rearrange("p a n -> p (a n)")
                    own.link(dve.scalar_tensor_tensor(st, st, wdh[:, 4 + s:5 + s], kv, ALU.mult, ALU.add))
                for c in range(4):
                    it = ps[:, 0, c * P1:(c + 1) * P1] if c < 3 else ps[:, 1, 0:P1]
                    own.link(dve.scalar_tensor_tensor(hx[:, c, :], it, gh[:, c, W_:W_ + 1], hx[:, c, :], ALU.mult, ALU.add))
                own.link(dve.scalar_tensor_tensor(den[:, :], hx[:, :, P], -1.0, gh[:, :, EM_], ALU.mult, ALU.max))
                own.link(dve.tensor_tensor(den[:, :], hx[:, :, P], den[:, :], ALU.max))
                own.link(dve.reciprocal(rec[:, :], den[:, :]))
                dve.tensor_tensor(hn[:, :, :], hx[:, :, 0:P],
                                  rec[:, :].rearrange("p (c o) -> p c o", o=1).to_broadcast([P, 5, P]), ALU.mult)\
                   .then_inc(S["m_hn"], 1)
                if not last:
                    head_dve(dve, i + 1)
                dve.wait_ge(S["m_rs"], i + 1)
                dve.tensor_tensor(hn[:, :, :], hn[:, :, :],
                                  rs5[:, :].rearrange("p (c o) -> p c o", o=1).to_broadcast([P, 5, P]), ALU.mult)\
                   .then_inc(S["m_y"], 1)
                own.link(dve.tensor_copy(ghc[:, :], gev[:, bass.ds(i, 1)]))
                dve.wait_ge(S["m_yt"], i + 1)
                dve.wait_ge(S["m_so"], i + 1)
                dve.scalar_tensor_tensor(pj[:, bass.ds(i, 1), 0:SEQ].rearrange("p a n -> p (a n)"), ps[:, 7, :],
                                         ghc[:, 0:1], so[:, 0:SEQ],
                                         ALU.mult, ALU.mult)
                dve.scalar_tensor_tensor(pj[:, bass.ds(i, 1), SEQ:N_TOK].rearrange("p a n -> p (a n)"),
                                         ps[:, 2, 256:256 + T4], ghc[:, 0:1], so[:, SEQ:N_TOK], ALU.mult, ALU.mult)\
                   .then_inc(S["m_mix"], 1)
                dve.wait_ge(S["m_mix"], i + 2)
            dve.wait_ge(S["c0ld"], 16)
            head_dve(dve, 0)
            heads(dve, turn, 26)

        def mlstm_act(act):
            def turn(i, last):
                act.wait_ge(S["m_bc"], i + 1)
                for c in range(4):
                    act.activation(dec[:, c * P:(c + 1) * P], ps[:, 3, c * P:(c + 1) * P], ACT.Exp, bias=gh[:, c, A_:A_ + 1])
                act.activation(dec[0:T4, SEQ:N_TOK], ps[0:T4, 4, 0:T4], ACT.Exp, bias=gh[0:T4, 4, A_:A_ + 1])\
                   .then_inc(S["m_D"], 1)
                act.wait_ge(S["m_mix"], i + 1)
                act.activation(so[:, :], pj[:, bass.ds(i + OA, 1), :].rearrange("p a n -> p (a n)"), ACT.Exp, scale=-1.0)\
                   .then_inc(S["m_a"], 1)
                act.wait_ge(S["m_a"], i * 3 + 1)
                act.activation(so[:, :], so[:, :], ACT.Ln, bias=one[:, 0:1]).then_inc(S["m_a"], 1)
                act.wait_ge(S["m_a"], i * 3 + 2)
                act.activation(so[:, :], so[:, :], ACT.Exp, scale=-1.0).then_inc(S["m_so"], 1)
                act.wait_ge(S["m_hn"], i + 1)
                for c in range(5):
                    act.activation(sT[:, 0:P], hn[:, c, :], ACT.Square, accum_out=ssq[:, c:c + 1]).then_inc(S["m_sq"], 1)
                    act.wait_ge(S["m_sq"], i * 5 + (c + 1))
                act.activation(rs5[:, :], ssq[:, :], ACT.Ln, bias=eps[:, 0:1], scale=1.0 / P).then_inc(S["m_a"], 1)
                act.wait_ge(S["m_a"], i * 3 + 3)
                act.activation(rs5[:, :], rs5[:, :], ACT.Exp, scale=-0.5).then_inc(S["m_rs"], 1)
            heads(act, turn)

        def start_pe(pe, i):
            pe.wait_ge(S["m_cp"], i + 1)
            q, k, v = qkv[:, 0, :], qkv[:, 1, :], qkv[:, 2, :]
            tile = lambda a, c: a[:, P * c:P * c + (P if c < 4 else T4)]
            for c in range(4):
                pe.transpose(ps[:, 0, c * P:(c + 1) * P], tile(k, c), ident)
                pe.transpose(ps[:, 1, c * P:(c + 1) * P], tile(v, c), ident)
            pe.transpose(ps[0:T4, 2, 0:P], tile(k, 4), ident)
            pe.transpose(ps[0:T4, 2, P:2 * P], tile(v, 4), ident).then_inc(S["m_tr"], 1)
            pe.matmul(ps[:, 3, :], selh[:, :], rows[:, R_RM, 0:SEQ], start=True, stop=False)
            for c in range(4):
                pe.matmul(ps[:, 3, c * P:(c + 1) * P], ident, cst[:, C_NEG:C_NEG + P], start=False, stop=c == 3)
            pe.matmul(ps[0:T4, 4, 0:T4], selh[:, 0:T4], rows[:, R_RM, SEQ:N_TOK], start=True, stop=False)
            pe.matmul(ps[0:T4, 4, 0:T4], ident[0:T4, 0:T4], cst[0:T4, C_NEG4:C_NEG4 + T4], start=False, stop=True)
            pe.matmul(ps[:, 4, 64:68], selh[:, :], rows[:, R_W, P - 1:SEQ:P], start=True, stop=True)
            pe.matmul(ps[:, 4, 68:76], selh[:, :], rows[:, R_W, SAMP0 + DEC_T - 1:META0:DEC_T], start=True, stop=True)\
              .then_inc(S["m_bc"], 1)
            for c in range(4):
                pe.matmul(ps[:, 5, c * P:(c + 1) * P], tile(k, c), tile(q, c), start=True, stop=True)
            pe.matmul(ps[0:T4, 6, 0:T4], tile(k, 4), tile(q, 4), start=True, stop=True).then_inc(S["m_qk"], 1)

        def mlstm_pe(pe):
            q = qkv[:, 0, :]
            tile = lambda a, c: a[:, P * c:P * c + (P if c < 4 else T4)]

            def turn(i, last):
                pe.wait_ge(S["m_mix"], i + 1)
                for s in range(DEC_B):
                    mm = pe.matmul(ps[0:N_SAMP, 7, 0:P1], qm[:, N_SAMP * s:N_SAMP * (s + 1)],
                                   c0[:, bass.ds(i, 1), s, :].rearrange("p a n -> p (a n)"), start=s == 0, stop=s == DEC_B - 1)
                mm.then_inc(S["m_si"], 1)
                pe.wait_ge(S["m_kv"], i + 1)
                pe.wait_ge(S["m_S"], i + 1)
                pe.matmul(ps[:, 0, 0:P1], kw[N_SAMP:T4, 4, :], vx[N_SAMP:T4, 4, :], start=True, stop=True)
                for c in range(4):
                    out = ps[:, 0, (c + 1) * P1:(c + 2) * P1] if c < 2 else ps[:, 1, (c - 2) * P1:(c - 1) * P1]
                    mm = pe.matmul(out, kw[:, c, :], vx[:, c, :], start=True, stop=True)
                mm.then_inc(S["m_kvs"], 1)
                pe.matmul(ps[0:T4, 5, 0:P1], sT[0:T4, SEQ:N_TOK], vx[0:T4, 4, :], start=True, stop=True)
                for c in range(4):
                    out = ps[:, 5, (c + 1) * P1:(c + 2) * P1] if c < 2 else ps[:, 6, (c - 2) * P1:(c - 1) * P1]
                    mm = pe.matmul(out, sT[:, c * P:(c + 1) * P], vx[:, c, :], start=True, stop=True)
                mm.then_inc(S["m_in"], 1)
                for s in range(DEC_B):
                    mm = pe.matmul(ps[:, 2 + s // 3, (s % 3) * P1:(s % 3 + 1) * P1], kwm[:, s, :], vx[0:N_SAMP, 4, :],
                                   start=True, stop=True)
                pe.wait_ge(S["m_C"], i + 1)
                for c in range(4):
                    out = ps[:, 0, c * P1:(c + 1) * P1] if c < 3 else ps[:, 1, 0:P1]
                    mm = pe.matmul(out, tile(q, c), Cs[:, c, :], start=True, stop=True)
                mm.then_inc(S["m_it"], 1)
                if not last:
                    start_pe(pe, i + 1)
                pe.wait_ge(S["m_y"], i + 1)
                for c in range(4):
                    pe.transpose(ps[:, 7, c * P:(c + 1) * P], hn[:, c, :], ident)
                pe.transpose(ps[:, 2, 256:256 + T4], hn[0:T4, 4, :], ident[0:T4, 0:T4]).then_inc(S["m_yt"], 1)
            start_pe(pe, 0)
            heads(pe, turn)

        def new_pe(pe):
            pe.wait_ge(S["d_q"], 1)
            for p in range(4):
                pe.matmul(ps[0:N_SAMP, 5, 64 * p:64 * p + 64], pj[:, KBB + p, SAMP0:META0],
                          qbd[:, p, :, :].rearrange("p s c -> p (s c)"), start=True, stop=True)
                mm = pe.transpose(ps[0:N_SAMP, 6, P * p:P * p + P], pj[:, VB + p, SAMP0:META0], ident)
            mm.then_inc(S["d_z"], 1)
            pe.wait_ge(S["d_sp"], 1)
            pe.matmul(ps[0:N_SAMP, 5, 0:256], after[0:N_SAMP, 0:N_SAMP], spn[:, :], start=True, stop=True).then_inc(S["d_A"], 1)
            pe.wait_ge(S["d_w"], 1)
            for p in range(4):
                mm = pe.matmul(ps[:, 7, 64 * p:64 * p + 64], vnew[:, p, :], zn[:, 64 * p:64 * p + 64], start=True, stop=True)
            mm.then_inc(S["d_o"], 1)

        def softplus_act(act, src, dst, s, k0):
            act.activation(dst, src, ACT.Abs).then_inc(s, 1)
            act.wait_ge(s, k0 + 1)
            act.activation(dst, dst, ACT.Exp, scale=-1.0).then_inc(s, 1)
            act.wait_ge(s, k0 + 2)
            n = dst.shape[0]
            return act.activation(dst, dst, ACT.Ln, bias=one[0:n, 0:1])

        def new_act(act):
            act.wait_ge(S["d_zs"], 1)
            softplus_act(act, zn[:, :], ln_[:, :], S["a_x"], 0).then_inc(S["d_l"], 1)
            act.wait_ge(S["d_t"], 1)
            act.activation(zn[:, :], zn[:, :], ACT.Exp).then_inc(S["d_e"], 1)

        def new_dve(dve):
            own.link(dve.memset(qbd[:, :, :, :], 0.0))
            for r, c in ((0, 0), (64, 4)):
                ins = dve.tensor_copy(qbd[r:r + 64, :, :, c:c + 4],
                                      pj[r:r + 64, QB:QB + 4, SAMP0:META0].rearrange("p b (s t) -> p b s t", t=DEC_T))
                if r == 0:
                    own.link(ins)
            ins.then_inc(S["d_q"], 1)
            dve.wait_ge(S["d_z"], 1)
            dve.tensor_copy(vnew[:, :, :], ps[0:N_SAMP, 6, :].rearrange("p (b n) -> p b n", n=P))
            col = lambda a, p: a[:, 64 * p:64 * p + 64]
            v3 = lambda a: a.rearrange("p (s c) -> p s c", c=8)
            v4 = lambda a: a.rearrange("p (s h t) -> p s h t", h=2, t=DEC_T)
            for p in range(4):
                ins = dve.scalar_tensor_tensor(v3(col(zn, p)), v3(ps[0:N_SAMP, 5, 64 * p:64 * p + 64]), DH_B ** -0.5,
                                               bsr[0:N_SAMP, 8 * p:8 * p + 8].rearrange("p (o c) -> p o c", o=1)
                                               .to_broadcast([N_SAMP, DEC_B, 8]), ALU.mult, ALU.add)
            ins.then_inc(S["d_zs"], 1)
            dve.wait_ge(S["d_l"], 1)
            own.link(dve.scalar_tensor_tensor(spn[:, :], zn[:, :], 0.0, ln_[:, :], ALU.max, ALU.add))
            own.link(dve.scalar_tensor_tensor(zn[:, :], zn[:, :], 0.0, ln_[:, :], ALU.min, ALU.subtract))
            msk = cst[0:N_SAMP, C_NEWM:C_NEWM + N_SAMP].rearrange("p (s o t) -> p s o t", o=1, t=DEC_T)\
                .to_broadcast([N_SAMP, DEC_B, 2, DEC_T])
            for p in range(4):
                ins = dve.tensor_tensor(v4(col(spn, p)), v4(col(spn, p)), msk, ALU.mult)
            ins.then_inc(S["d_sp"], 1)
            dve.wait_ge(S["d_A"], 1)
            dve.tensor_tensor(zn[:, :], zn[:, :], ps[0:N_SAMP, 5, 0:256], ALU.subtract).then_inc(S["d_t"], 1)
            dve.wait_ge(S["d_e"], 1)
            for p in range(4):
                ins = dve.tensor_tensor(v4(col(zn, p)), v4(col(zn, p)), msk, ALU.mult)
            ins.then_inc(S["d_w"], 1)
            dve.wait_ge(S["d_o"], 1)
            own.link(dve.tensor_copy(osn[:, :], ps[:, 7, 0:256]))

        KLD = [sem(f"kld{g}") for g in range(4)]
        VLD = [sem(f"vld{g}") for g in range(4)]
        N_POOL = k_cache.shape[0]

        def load_group(sp_, cache, buf, ready, used, i, u, g):
            if buf is vbuf:
                sp_.wait_ge(S[used], i * 8 + (4 * u + g + 1))
                sp_.sem_inc(S["v_turn"], 1)
            for a in range(PG):
                at_ = u * N_PAGES + N_PAGES - 1 - (4 * a + g)
                page = sp_.value_load(ptab[0:1, bass.ds(i * (2 * N_PAGES) + at_, 1)], min_val=0, max_val=N_POOL - 1)
                if a == 0 and buf is kbuf:
                    sp_.wait_ge(S[used], i * 8 + (4 * u + g + 1))
                sp_.dma_start(buf[g][:, a].rearrange("p b n -> p (b n)") if buf is kbuf else buf[g][:, a],
                              cache[bass.ds(page, 1), :, :].rearrange("a p n -> (a p) n")).then_inc(ready[g], 16)

        def load_k(sp_, i, u, g):
            load_group(sp_, k_cache, kbuf, KLD, "k_used", i, u, g)

        def load_v(sp_, i, u, g):
            load_group(sp_, v_cache, vbuf, VLD, "v_used", i, u, g)

        def qs_dve(dve, i, u):
            dve.tensor_copy(qs[:, :, 0:8], qbd[:, :, bass.ds(i * 2 + u, 1), :].rearrange("p b s c -> p b (s c)"))\
               .then_inc(S["b_q"], 1)

        def qk_pe(pe, i, u):
            pe.wait_ge(S["b_q"], i * 2 + (u + 1))
            for g in range(4):
                pe.wait_ge(KLD[g], i * 128 + 64 * (u + 1))
                for p in range(4):
                    mm = pe.matmul(ps[ROWN * g:ROWN * (g + 1), 5, :], qs[:, :, :].rearrange("p b c -> p (b c)")
                                   [:, ROWN * p:ROWN * (p + 1)], kbuf[g][:, :, p, :],
                                   start=p == 0, stop=p == 3)
                mm.then_inc(S["k_used"], 1)

        def tr_pe(pe, i, u):
            pe.wait_ge(S["b_zr"], i * 2 + (u + 1))
            for a in range(PG):
                mm = pe.transpose(ps[:, 6, P * a:P * a + P], zr[:, P * a:P * a + P], ident)
            mm.then_inc(S["b_z"], 1)

        def suffix_pe(pe, i, u):
            pe.wait_ge(S["b_sp"], i * 2 + (u + 1))
            out = ps[:, 6, :].rearrange("p (c a) -> p c a", a=N_PAGES)
            pe.matmul(out, after, sg[:, :, 1:1 + N_PAGES], start=True, stop=False)
            pe.matmul(out, ones, ssg[:, :, 0:N_PAGES], start=False, stop=True).then_inc(S["b_A"], 1)

        def pv_pe(pe, i, u):
            pe.wait_ge(S["b_w"], i * 2 + (u + 1))
            pe.wait_ge(S["b_ev"], i * 2 + (u + 1))
            for g in range(4):
                pe.wait_ge(VLD[g], i * 128 + 64 * (u + 1))
                for a in range(PG):
                    mm = pe.matmul(ps[ROWN * g:ROWN * (g + 1), 7, :], lg[:, u % 2, 4 * a + g, :], vbuf[g][:, a, :],
                                   start=a == 0, stop=a == PG - 1)
                mm.then_inc(S["v_used"], 1)

        def out_pe(pe, i, u):
            pe.wait_ge(S["b_om"], i * 2 + (u + 1))
            for p in range(4):
                pe.matmul(ps[:, 7, DEC_T * p:DEC_T * (p + 1)], outm[:, P * p:P * p + P],
                               cst[:, C_QRY:C_QRY + DEC_T], start=True, stop=True)
            pe.matmul(ps[:, 7, 64:64 + N_META], vP[0:N_META, 4, :], mw[:, :], start=True, stop=True)\
              .then_inc(S["b_o"], 1)

        def page_z_act(act, i, u):
            act.wait_ge(S["k_used"], i * 8 + (4 * u + 8))
            act.activation(zr[:, :], ps[:, 5, :], ACT.Identity, bias=bcol[:, 0:1], scale=DH_B ** -0.5)\
               .then_inc(S["b_zr"], 1)

        def page_act(act, i, u):
            act.wait_ge(S["b_z"], i * 2 + (u + 1))
            if u:
                act.wait_ge(S["v_used"], i * 8 + 4 * u)
            softplus_act(act, ps[:, 6, :].rearrange("p (a c) -> p a c", c=ROWN), lg[:, u % 2], S["b_x"],
                         i * 4 + 2 * u).then_inc(S["b_l"], 1)

        def page_exp(act, i, u):
            act.wait_ge(S["b_t"], i * 2 + (u + 1))
            act.activation(lg[:, u % 2], lg[:, u % 2], ACT.Exp).then_inc(S["b_w"], 1)

        def page_z_dve(dve, i, u):
            dve.tensor_copy(sg[0:N_SAMP, :, 0:1].rearrange("p (b c) o -> p b (c o)", c=8),
                            spn[:, :].rearrange("p (b s c) -> p b s c", s=DEC_B, c=8)
                            [:, :, bass.ds(i * 2 + u, 1), :].rearrange("p b s c -> p b (s c)"))
            dve.wait_ge(S["b_l"], i * 2 + (u + 1))
            zt = ps[:, 6, :].rearrange("p (a c) -> p a c", c=ROWN)
            dve.scalar_tensor_tensor(zg[:, :, :], zt, 0.0, lg[:, u % 2], ALU.min, ALU.subtract)
            own.link(dve.scalar_tensor_tensor(sg[:, :, 1:].rearrange("p c a -> p a c"), zt, 0.0, lg[:, u % 2],
                                              ALU.max, ALU.add))
            f2 = lambda a: a[:, :, :].rearrange("p c a -> p (c a)")
            dve.tensor_tensor_scan(f2(ssg), f2(smk), f2(sg), 0.0, ALU.mult, ALU.add).then_inc(S["b_sp"], 1)

        def page_sub(dve, i, u):
            dve.wait_ge(S["b_A"], i * 2 + (u + 1))
            dve.tensor_tensor(lg[:, u % 2], zg[:, :, :], ps[:, 6, :].rearrange("p (c a) -> p a c", a=N_PAGES), ALU.subtract)\
               .then_inc(S["b_t"], 1)

        def own_heads_dve(dve, i, u):
            dve.wait_ge(S["v_used"], i * 8 + (4 * u + 8))
            dve.tensor_tensor(outm[:, :].rearrange("p (h d) -> p h d", d=DH_B), ps[:, 7, :]
                              .rearrange("p (h d) -> p h d", d=DH_B),
                              cst[:, C_HEAD:C_HEAD + H_B].rearrange("p (h o) -> p h o", o=1)
                              .to_broadcast([P, H_B, DH_B]), ALU.mult).then_inc(S["b_om"], 1)

        def page_out(dve, i, u):
            for r, c in ((0, 0), (64, 4)):
                ins = dve.tensor_tensor(pj[r:r + 64, QB:QB + 4, bass.ds(i * (2 * DEC_T) + (SAMP0 + DEC_T * u), DEC_T)],
                                        ps[r:r + 64, 7, 0:16].rearrange("p (b c) -> p b c", c=DEC_T),
                                        osn[r:r + 64, :].rearrange("p (b s c) -> p b s c", s=DEC_B, c=8)
                                        [:, :, bass.ds(i * 2 + u, 1), c:c + 4].rearrange("p b s c -> p b (s c)"), ALU.add)
            ins.then_inc(S["b_ev"], 1)

        WID = [SEQ - P * k for k in range(4)]
        ZB = [(0, 0), (1, 0), (2, 0), (2, 256)]
        META = slice(WZ, WZ + SEQ)
        METAQ = slice(WZ + SEQ, WA)

        def pair_dve(dve, i, u):
            blk = lambda b: pj[:, bass.ds(i + (b + u // 2), 1), :].rearrange("p a n -> p (a n)")
            dve.tensor_copy(bh[:, :], bsb[:, bass.ds(i * 2 + u, 2)])
            dve.tensor_copy(kP[:, :], blk(KBB))
            dve.tensor_copy(vF[:, :], blk(VB))
            for j in range(2):
                r = 64 * j
                ins = dve.tensor_copy(qz[r:r + 64, j, :],
                                      pj[r:r + 64, bass.ds(i + (QB + u // 2), 1), :].rearrange("p a n -> p (a n)"))
            ins.then_inc(S["a_in"], 1)

        def values_pe(pe, i, u):
            if u:
                pe.wait_ge(S["b_ev"], i * 2 + (u + 1))
            for c in range(4):
                pe.transpose(ps[:, 4, P * c:P * c + P], vF[:, P * c:P * c + P], ident)
            pe.transpose(ps[0:N_META, 7, 384:512], vF[:, META0:N_TOK], ident).then_inc(S["v_tr"], 1)

        def values_dve(dve, i, u):
            dve.wait_ge(S["v_tr"], i + (u // 2 + 1))
            dve.tensor_copy(vP[:, 0:4, :], ps[:, 4, :].rearrange("p (c n) -> p c n", n=P))
            dve.tensor_copy(vP[0:N_META, 4, :], ps[0:N_META, 7, 384:512]).then_inc(S["v_ev"], 1)

        def pz_pe(pe, i, u):
            j = u % 2
            if j == 0:
                pe.wait_ge(S["a_in"], i + (u // 2 + 1))
            if u:
                pe.wait_ge(S["a_t"], i * 2 + u)
            for k in range(4):
                b, c = ZB[k]
                pe.matmul(ps[:, b, c:c + WID[k]], kP[:, P * k:P * k + P], qz[:, j, P * k:SEQ], start=True, stop=True)
            pe.matmul(ps[0:N_META, 3, 0:SEQ], kP[:, META0:N_TOK], qz[:, j, 0:SEQ], start=True, stop=True)
            pe.matmul(ps[0:N_META, 1, 384:400], kP[:, META0:N_TOK], qz[:, j, META0:N_TOK], start=True, stop=True)\
              .then_inc(S["a_z"], 1)

        def pz_act(act, i, u):
            j = u % 2
            act.wait_ge(S["a_z"], i * 2 + (u + 1))
            c = DH_B ** -0.5
            for dst, src in ((z[:, 0:512], ps[:, 0, :]), (z[:, 512:896], ps[:, 1, 0:384]), (z[:, 896:WZ], ps[:, 2, 0:384])):
                ins = act.activation(dst, src, ACT.Identity, scale=c, bias=bh[:, j:j + 1])
            for dst, src in ((z[0:N_META, META], ps[0:N_META, 3, :]), (z[0:N_META, METAQ], ps[0:N_META, 1, 384:400])):
                ins = act.activation(dst, src, ACT.Identity, scale=c, bias=bh[0:N_META, j:j + 1])
            ins.then_inc(S["a_x2"], 1)

        def psoft_act(act, i, u):
            if u:
                act.wait_ge(S["a_v"], i * 2 + u)
            act.wait_ge(S["a_x2"], i * 10 + (5 * u + 1))
            softplus_act(act, z[:, 0:WZ], lz[:, 0:WZ], S["a_x2"], i * 10 + (5 * u + 1)).then_inc(S["a_l"], 1)
            softplus_act(act, z[0:N_META, WZ:WA], lz[0:N_META, WZ:WA], S["a_x2"], i * 10 + (5 * u + 3)).then_inc(S["a_l"], 1)

        FULL = [(slice(0, P), slice(0, WZ)), (slice(0, N_META), slice(WZ, WA))]

        def diag_mask(dve, buf, meta):
            for k in range(4):
                dve.tensor_tensor(buf[:, KOFF[k]:KOFF[k] + P], buf[:, KOFF[k]:KOFF[k] + P], strict, ALU.mult)
            return dve.tensor_tensor(meta, buf[0:N_META, METAQ], strict[0:N_META, 0:N_META], ALU.mult)

        def psp_dve(dve, i, j):
            for n, (r, c) in enumerate(FULL):
                dve.wait_ge(S["a_l"], i * 4 + (2 * j + n + 1))
                own.link(dve.scalar_tensor_tensor(sp[r, c], z[r, c], 0.0, lz[r, c], ALU.max, ALU.add))
                own.link(dve.scalar_tensor_tensor(z[r, c], z[r, c], 0.0, lz[r, c], ALU.min, ALU.subtract))
            diag_mask(dve, sp, sp[0:N_META, METAQ]).then_inc(S["a_sp"], 1)

        def suffixes_pe(pe, i, j):
            pe.wait_ge(S["a_sp"], i * 2 + (j + 1))
            for k in range(4):
                b, c = ZB[k]
                pe.matmul(ps[:, b, c:c + WID[k]], after, sp[:, KOFF[k]:KOFF[k] + WID[k]], start=True, stop=k == 3)
                for l in range(k + 1, 4):
                    o_ = P * (l - k)
                    pe.matmul(ps[:, b, c + o_:c + WID[k]], ones, sp[:, KOFF[l]:KOFF[l] + WID[l]], start=False, stop=l == 3)
            pe.matmul(ps[0:N_META, 3, 0:SEQ], after[0:N_META, 0:N_META], sp[0:N_META, META], start=True, stop=False)
            for l in range(4):
                pe.matmul(ps[0:N_META, 3, P * l:SEQ], ones[:, 0:N_META], sp[:, KOFF[l]:KOFF[l] + WID[l]],
                          start=False, stop=l == 3)
            pe.matmul(ps[0:N_META, 1, 384:400], after[0:N_META, 0:N_META], sp[0:N_META, METAQ], start=True, stop=True)\
              .then_inc(S["a_A"], 1)

        def psub_dve(dve, i, j):
            dve.wait_ge(S["a_A"], i * 2 + (j + 1))
            for dst, src in (((slice(0, P), slice(0, 512)), ps[:, 0, :]), ((slice(0, P), slice(512, 896)), ps[:, 1, 0:384]),
                             ((slice(0, P), slice(896, WZ)), ps[:, 2, 0:384]), ((slice(0, N_META), META), ps[0:N_META, 3, :]),
                             ((slice(0, N_META), METAQ), ps[0:N_META, 1, 384:400])):
                ins = dve.tensor_tensor(lz[dst], z[dst], src, ALU.subtract)
            ins.then_inc(S["a_t"], 1)

        def pexp_act(act, i, j):
            act.wait_ge(S["a_t"], i * 2 + (j + 1))
            for r, c in FULL:
                ins = act.activation(lz[r, c], lz[r, c], ACT.Exp)
            ins.then_inc(S["a_e"], 1)

        def pmask_dve(dve, i, j):
            dve.wait_ge(S["a_e"], i * 2 + (j + 1))
            diag_mask(dve, lz, mw[:, :]).then_inc(S["a_w"], 1)

        def pv_prompt_pe(pe, i, j):
            pe.wait_ge(S["a_w"], i * 2 + (j + 1))
            pe.wait_ge(S["a_o"], i * 2 + (j + 1))
            if j == 0:
                pe.wait_ge(S["v_ev"], i + 1)
            pe.matmul(ps[:, 4, :], vP[0:N_META, 4, :], lz[0:N_META, META], start=True, stop=False)
            for k in range(4):
                mm = pe.matmul(ps[:, 4, P * k:SEQ], vP[:, k, :], lz[:, KOFF[k]:KOFF[k] + WID[k]], start=False, stop=k == 3)
            mm.then_inc(S["a_v"], 1)

        def pout_dve(dve, i, j):
            dve.wait_ge(S["b_o"], i * 2 + (j + 1))
            r = slice(64 * j, 64 * j + 64)
            blk = pj[r, bass.ds(i + QB, 1), :].rearrange("p a n -> p (a n)")
            dve.tensor_scalar(blk[:, 0:SEQ], ps[r, 4, :], 1.0, None, ALU.mult)
            dve.tensor_scalar(blk[:, META0:N_TOK], ps[r, 7, 64:64 + N_META], 1.0, None, ALU.mult).then_inc(S["a_o"], 1)

        def turns(eng, step, own_steps=None):
            with eng.Fori(0, 3) as i:
                if own_steps:
                    own.start(i, own_steps)
                for u in range(2):
                    step(i, u, False)
                if own_steps:
                    own.end(3)
            for u in range(2):
                step(3, u, u == 1)

        def load_keys(sp_):
            for g in range(4):
                if g == 2:
                    sp_.wait_ge(S["mout"], 32)
                load_k(sp_, 0, 0, g)

            def step(i, u, last):
                for g in range(4 if not last else 0):
                    load_k(sp_, i, u + 1, g)
            turns(sp_, step)

        def load_values(pool):
            with pool.Fori(0, DEC_B // 2) as i:
                for u in range(2):
                    for g in range(4):
                        load_v(pool, i, u, g)

        def attn_pe(pe):
            def step(i, u, last):
                suffixes_pe(pe, i, u)
                suffix_pe(pe, i, u)
                if not last:
                    qk_pe(pe, i, u + 1)
                    pz_pe(pe, i, u + 1)
                pv_prompt_pe(pe, i, u)
                if not last:
                    tr_pe(pe, i, u + 1)
                pv_pe(pe, i, u)
                out_pe(pe, i, u)
                if u == 1 and not last:
                    values_pe(pe, i, u + 1)
            pz_pe(pe, 0, 0)
            values_pe(pe, 0, 0)
            qk_pe(pe, 0, 0)
            tr_pe(pe, 0, 0)
            turns(pe, step)

        def attn_act(act):
            def step(i, u, last):
                pexp_act(act, i, u)
                page_exp(act, i, u)
                if not last:
                    page_z_act(act, i, u + 1)
                    pz_act(act, i, u + 1)
                    psoft_act(act, i, u + 1)
                    page_act(act, i, u + 1)
            pz_act(act, 0, 0)
            psoft_act(act, 0, 0)
            act.wait_ge(S["mout"], 32)
            page_z_act(act, 0, 0)
            page_act(act, 0, 0)
            turns(act, step)

        def attn_dve(dve):
            def step(i, u, last):
                if not last:
                    qs_dve(dve, i, u + 1)
                if u == 1 and not last:
                    pair_dve(dve, i, u + 1)
                psub_dve(dve, i, u)
                page_sub(dve, i, u)
                pmask_dve(dve, i, u)
                own_heads_dve(dve, i, u)
                pout_dve(dve, i, u)
                page_out(dve, i, u)
                if u == 1 and not last:
                    values_dve(dve, i, u + 1)
                if not last:
                    psp_dve(dve, i, u + 1)
                    page_z_dve(dve, i, u + 1)
            dve.memset(qz[:, :, :], 0.0)
            own.link(dve.memset(qs[:, :, :], 0.0))
            qs_dve(dve, 0, 0)
            dve.wait_ge(S["rout"], 32)
            pair_dve(dve, 0, 0)
            dve.memset(sg[:, :, 0:1], 0.0)
            own.link(dve.memset(smk[:, :, :], 1.0))
            own.link(dve.memset(smk[:, :, 0:1], 0.0))
            values_dve(dve, 0, 0)
            psp_dve(dve, 0, 0)
            page_z_dve(dve, 0, 0)
            turns(dve, step, 10)

        LEVELS = [64, 32, 16, 8, 4, 2, 1, 0]
        X = [at("X0", o_M, [P, H_C, N_TOK]), at("X1", o_M + 4 * ROW, [P, H_C, N_TOK])]
        E = at("E", o_M + 8 * ROW, [P, H_C, N_TOK])
        cum = at("cum", o_M + 12 * ROW, [P, H_C, N_TOK])
        o = o_M + 16 * ROW
        AT = at("AT", o, [P, 5, H_C, P]); o += 5 * H_C * P * 4
        sfin = at("sfin", o, [P, H_C, DV_C])
        gmk = at("gmk", o, [P, 8, P], i32); o += 4096
        gm4 = at("gm4", o, [T4, 5, T4], i32); o += 960
        el = at("el", o, [P, H_C, 13]); o += 224
        assert o <= o_xn
        lgp = at("lgp", o_M + 16 * ROW, [P, H_C, N_TOK])
        lgn = at("lgn", o_M + 20 * ROW, [P, H_C, N_TOK])
        o = o_M + 8 * ROW
        ATh = at("ATh", o, [P, 5, P]); o += 2560
        KT = at("KT", o, [P, 5, P]); o += 2560
        VT = at("VT", o, [P, 5, DV_C]); o += 5120
        Ss = at("Ss", o, [P, 5, DV_C]); o += 5120
        gqm = at("gqm", o, [P, 416]); o += 1664
        elh = at("elh", o, [P, 13]); o += 64
        gos = at("gos", o, [P, 2]); o += 32
        gsq = at("gsq", o, [P, 5]); o += 32
        grs = at("grs", o, [P, 5]); o += 32
        assert o <= o_M + 16 * ROW
        o = o_pj
        gq = at("gq", o, [P, N_TOK]); o += ROW
        gk = at("gk", o, [P, N_TOK]); o += ROW
        gv = at("gv", o, [P, 2, N_TOK]); o += 2 * ROW
        sr = at("sr", o, [P, 2, N_TOK]); o += 2 * ROW
        gkm = at("gkm", o, [N_SAMP, DEC_B, P]); o += 4096
        assert o <= o_pj + 8 * ROW
        on = at("on", o_pj + 24 * ROW, [P, 5, DV_C])
        rst = at("rst", o_pj + 24 * ROW, [P, N_TOK])
        wgd = at("wgd", o_pj + 27 * ROW, [P, KB, 16])
        wgu = at("wgu", o_s + 1184, [16, H_C * P])
        gd = at("gd", o_s + 1184 + 2048, [16, N_TOK])
        s0b = at("s0b", o_xn, [P, 2, DEC_B, DV_C])
        TAU = 16.0
        flat = lambda a: a.rearrange("p h t -> p (h t)")
        UNITS = [(l, c) for l in range(8) for c in range(5) if c < 4 or LEVELS[l] <= 8]

        def gdown_pe(pe):
            pe.wait_ge(S["n_xn"], 6)
            pe.wait_ge(S["wgl"], 32)
            for h in range(2):
                for k in range(KB):
                    mm = pe.matmul(ps[0:16, 4 + h, 0:HALF], wgd[:, k, :], xn[:, k, COLS[h]], start=k == 0, stop=k == KB - 1)
            mm.then_inc(S["gd_ps"], 1)
            pe.wait_ge(S["gd_ok"], 2)

        def gdown_act(act):
            act.wait_ge(S["gd_ps"], 1)
            for h in range(2):
                act.activation(gd[:, COLS[h]], ps[0:16, 4 + h, 0:HALF], ACT.Copy).then_inc(S["gd_ok"], 1)

        def lgate_pe(pe):
            for h in range(H_C):
                pe.matmul(ps[:, 3, T4 * h:T4 * h + T4], wgu[:, P * h:P * h + P], gd[:, SEQ:N_TOK], start=True, stop=True)
            for h in range(H_C):
                mm = pe.matmul(ps[:, 4 + h, :], wgu[:, P * h:P * h + P], gd[:, 0:SEQ], start=True, stop=True)
            mm.then_inc(S["g_lg"], 1)
            pe.wait_ge(S["g_nb"], 1)

        def lgate_act(act):
            act.wait_ge(S["g_lg"], 1)
            for h in range(H_C):
                ins = act.activation(lgn[:, h, SEQ:N_TOK], ps[:, 3, T4 * h:T4 * h + T4], ACT.Identity, scale=-1.0,
                                     bias=bgu[:, h:h + 1])
            ins.then_inc(S["g_nb"], 1)
            for h in range(H_C):
                ins = act.activation(lgn[:, h, 0:SEQ], ps[:, 4 + h, :], ACT.Identity, scale=-1.0, bias=bgu[:, h:h + 1])
            ins.then_inc(S["g_a"], 1)

        def softgate_act(act):
            act.wait_ge(S["g_a"], 1)
            softplus_act(act, flat(lgn[:, :, :]), flat(lgp[:, :, :]), S["g_a"], 1).then_inc(S["g_l"], 1)

        def softgate_dve(dve):
            dve.wait_ge(S["g_l"], 1)
            dve.scalar_tensor_tensor(flat(lgp[:, :, :]), flat(lgn[:, :, :]), 0.0, flat(lgp[:, :, :]), ALU.max, ALU.add)\
               .then_inc(S["g_sp"], 1)

        def gla_pre_act(act):
            for l, w in enumerate(LEVELS[:-1]):
                act.wait_ge(S["g_ex"], l + 1)
                e = E[:, :, 0:SEQ] if w > 8 else E[:, :, :]
                act.activation(e, e, ACT.Exp, scale=1.0 / TAU).then_inc(S["g_E"], 1)
            act.wait_ge(S["g_x"], 7)
            act.activation(E[:, :, :], cum[:, :, :], ACT.Exp, scale=-1.0 / TAU).then_inc(S["g_E"], 1)
            act.wait_ge(S["g_ex"], 8)
            act.activation(E[:, :, :], E[:, :, :], ACT.Exp, scale=1.0 / TAU).then_inc(S["g_E"], 1)
            for a, b, c in ((0, 4, cum[:, :, P - 1:SEQ:P]), (4, 12, cum[:, :, SAMP0 + DEC_T - 1:META0:DEC_T]),
                            (12, 13, cum[:, :, N_TOK - 1:N_TOK])):
                act.activation(el[:, :, a:b], c, ACT.Exp, scale=-1.0 / TAU).then_inc(S["g_el"], 1)

        def level_exp_dve(dve, l):
            w = LEVELS[l]
            if w > 8:
                v = lambda a: a[:, :, 0:SEQ].rearrange("p h (b c) -> p h b c", c=2 * w)
                lo, hi, ref = (slice(0, w), slice(w, 2 * w), slice(w - 1, w))
                sl = lambda a, r: v(a)[:, :, :, r]
                shape = [P, H_C, SEQ // (2 * w), w]
            else:
                v = lambda a: flat(a).rearrange("p (b c) -> p b c", c=2 * w)
                lo, hi, ref = (slice(0, w), slice(w, 2 * w), slice(w - 1, w))
                sl = lambda a, r: v(a)[:, :, r]
                shape = [P, H_C * N_TOK // (2 * w), w]
            if l:
                dve.wait_ge(S["g_x"], l)
            r = sl(cum[:, :, :], ref).to_broadcast(shape)
            dve.tensor_tensor(sl(E[:, :, :], lo), sl(cum[:, :, :], lo), r, ALU.subtract)
            dve.tensor_tensor(sl(E[:, :, :], hi), r, sl(cum[:, :, :], hi), ALU.subtract).then_inc(S["g_ex"], 1)

            def scale():
                x = X[l % 2]
                q, k = pj[:, QC:QC + 4, :], pj[:, KC:KC + 4, :]
                dve.wait_ge(S["g_E"], l + 1)
                if l >= 2:
                    dve.wait_ge(S["g_p"], UNITS.index((l - 1, 0)))
                dve.tensor_tensor(sl(x[:, :, :], lo), sl(k, lo), sl(E[:, :, :], lo), ALU.mult)
                dve.tensor_tensor(sl(x[:, :, :], hi), sl(q, hi), sl(E[:, :, :], hi), ALU.mult).then_inc(S["g_x"], 1)
            return scale

        def level_pick(dve, l):
            if l:
                dve.wait_ge(S["g_c"], UNITS.index((l, 0)))
            for c in range(5):
                if (l, c) not in UNITS:
                    continue
                u = UNITS.index((l, c))
                dve.wait_ge(S["g_p"], u + 1)
                if c < 4:
                    dve.copy_predicated(AT[:, c, :, :], gmk[:, l:l + 1, :].to_broadcast([P, H_C, P]),
                                        ps[:, u % 8, :].rearrange("p (h n) -> p h n", n=P)).then_inc(S["g_c"], 1)
                else:
                    dve.copy_predicated(AT[0:T4, 4, :, 0:T4], gm4[:, l - 3:l - 2, :].to_broadcast([T4, H_C, T4]),
                                        ps[0:T4, u % 8, 0:H_C * T4].rearrange("p (h n) -> p h n", n=T4)).then_inc(S["g_c"], 1)

        def levels_pe(pe):
            for u, (l, c) in enumerate(UNITS):
                if c == 0 and l < 7:
                    pe.wait_ge(S["g_x"], l + 1)
                if u >= 8:
                    pe.wait_ge(S["g_c"], u - 7)
                cols = slice(P * c, P * c + (P if c < 4 else T4))
                n = P if c < 4 else T4
                for h in range(H_C):
                    k, q = (X[l % 2][:, h, cols],) * 2 if l < 7 else (pj[:, KC + h, cols], pj[:, QC + h, cols])
                    mm = pe.matmul(ps[0:n, u % 8, h * n:h * n + n], k, q, start=True, stop=True)
                mm.then_inc(S["g_p"], 1)

        def gla_pre_dve(dve):
            pj_all(dve, "odd")
            dve.wait_ge(S["grst"], 48)
            dve.wait_ge(S["g_sp"], 1)
            for h in range(H_C):
                own.link(dve.tensor_tensor_scan(cum[:, h, :], rst[:, :], lgp[:, h, :], 0.0, ALU.mult, ALU.add))
            own.link(dve.memset(AT[:, :, :, :], 0.0))
            dve.tensor_scalar(pj[:, QC:QC + 4, :], pj[:, QC:QC + 4, :], float(P) ** -0.5, None, ALU.mult)
            for l in range(7):
                scale = level_exp_dve(dve, l)
                if l:
                    level_pick(dve, l - 1)
                scale()
            level_pick(dve, 6)
            dve.wait_ge(S["g_E"], 8)
            level_pick(dve, 7)
            own.link(dve.tensor_tensor(X[0][:, :, :], pj[:, QC:QC + 4, :], E[:, :, :], ALU.mult))
            ch = lambda a: a[:, :, 0:SEQ].rearrange("p h (c t) -> p h c t", t=P)
            sm = lambda a: a[:, :, SAMP0:META0].rearrange("p h (s t) -> p h s t", t=DEC_T)
            dve.tensor_tensor(ch(E), ch(cum), ch(cum)[:, :, :, P - 1:P].to_broadcast([P, H_C, 4, P]), ALU.subtract)
            dve.tensor_tensor(sm(E), sm(cum), sm(cum)[:, :, :, DEC_T - 1:DEC_T].to_broadcast([P, H_C, DEC_B, DEC_T]), ALU.subtract)
            dve.tensor_tensor(E[:, :, META0:N_TOK], cum[:, :, META0:N_TOK],
                              cum[:, :, N_TOK - 1:N_TOK].to_broadcast([P, H_C, N_META]), ALU.subtract).then_inc(S["g_ex"], 1)
            dve.wait_ge(S["g_E"], 9)
            own.link(dve.tensor_tensor(X[1][:, :, :], pj[:, KC:KC + 4, :], E[:, :, :], ALU.mult))
            dve.wait_ge(S["g_el"], 3)
            own.link(dve.memset(gqm[:, :], 0.0))
            own.link(dve.memset(gsq[:, :], 1.0))
            dve.memset(on[:, :, :], 0.0)

        def gla_turns(eng, step, own_steps=None):
            with eng.Fori(0, H_C // 2 - 1) as i:
                if own_steps:
                    own.start(i, own_steps)
                for u in range(2):
                    step(i, u, False)
                if own_steps:
                    own.end(H_C // 2 - 1)
            for u in range(2):
                step(H_C // 2 - 1, u, u == 1)

        one_ = lambda a: a.rearrange("p a n -> p (a n)")

        def gla_head_dve(dve, i, u):
            hd = bass.ds(i * 2 + u, 1)
            dve.tensor_scalar(gq[:, :], one_(X[0][:, hd, :]), 1.0, None, ALU.mult)
            dve.tensor_copy(gk[:, :], one_(X[1][:, hd, :]))
            dve.tensor_copy(ATh[:, :, :], AT[:, :, hd, :].rearrange("p c h n -> p c (h n)"))
            dve.tensor_copy(gv[:, :, :], pj[:, bass.ds(i * 4 + (VC + 2 * u), 2), :])
            own.link(dve.tensor_copy(elh[:, :], one_(el[:, hd, :])))
            dve.tensor_copy(gqm[:, :].rearrange("p (s c) -> p s c", c=52)[:, :, 0:4],
                            gq[:, SAMP0:META0].rearrange("p (s t) -> p s t", t=DEC_T)).then_inc(S["h_cp"], 1)

        def gla_evac_dve(dve, i, u):
            dve.wait_ge(S["h_tr"], i * 2 + (u + 1))
            dve.tensor_scalar(KT[:, 0:4, :], ps[:, 0, :].rearrange("p (c n) -> p c n", n=P), 1.0, None, ALU.mult)
            own.link(dve.tensor_copy(KT[0:T4, 4, :], ps[0:T4, 1, 0:P]))
            dve.tensor_copy(VT[:, 0:2, :], ps[:, 2, :].rearrange("p (c n) -> p c n", n=DV_C))
            dve.tensor_copy(VT[:, 2:4, :], ps[:, 3, :].rearrange("p (c n) -> p c n", n=DV_C))
            dve.tensor_copy(VT[0:T4, 4, :], ps[0:T4, 1, P:P + DV_C])
            dve.tensor_tensor(gkm[:, :, :], KT[0:N_SAMP, 4:5, :].to_broadcast([N_SAMP, DEC_B, P]),
                              cst[0:N_SAMP, C_SEQM:C_SEQM + DEC_B].rearrange("p (s o) -> p s o", o=1)
                              .to_broadcast([N_SAMP, DEC_B, P]), ALU.mult).then_inc(S["h_kv"], 1)

        def gla_dve(dve):
            def step(i, u, last):
                n = i * 2 + (u + 1)
                hd = i * 2 + u
                dve.wait_ge(S["h_kvs"], n)
                own.link(dve.tensor_copy(Ss[:, 0, :], ps[:, 4, 0:DV_C]))
                for c in range(4):
                    b, o_ = divmod(c + 1, 2)
                    own.link(dve.scalar_tensor_tensor(Ss[:, c + 1, :], Ss[:, c, :], elh[:, c:c + 1],
                                                      ps[:, 4 + b, o_ * DV_C:(o_ + 1) * DV_C], ALU.mult, ALU.add))
                dve.tensor_copy(sfin[:, bass.ds(hd, 1), :], Ss[:, 4:5, :]).then_inc(S["h_S"], 1)
                dve.wait_ge(S["h_t4"], n)
                for s in range(DEC_B):
                    b, o_ = SKV[s]
                    ins = dve.scalar_tensor_tensor(s0b[:, u, s, :], s0b[:, u, s, :], elh[:, 4 + s:5 + s],
                                                   ps[:, b, o_:o_ + DV_C], ALU.mult, ALU.add)
                ins.then_inc(S["h_s0"], 1)
                dve.wait_ge(S["h_s0"], n)
                dve.wait_ge(S["h_rs"], n)
                for c in range(4):
                    dve.tensor_scalar(on[:, c, :], ps[:, 4 + c // 2, (c % 2) * DV_C:(c % 2 + 1) * DV_C],
                                      grs[:, c:c + 1], None, ALU.mult)
                dve.tensor_scalar(on[0:T4, 4, :], ps[0:T4, 1, 0:DV_C], grs[0:T4, 4:5], None, ALU.mult)\
                   .then_inc(S["h_y"], 1)
                if not last:
                    gla_head_dve(dve, i, u + 1)
                dve.tensor_copy(gos[:, :], god[:, bass.ds(i * 4 + 2 * u, 2)])
                dve.wait_ge(S["h_sg"], n)
                own.link(dve.tensor_tensor(sr[:, :, :], sr[:, :, :], pj[:, bass.ds(i * 4 + (RC + 2 * u), 2), :], ALU.mult))
                dve.wait_ge(S["h_yt"], n)
                for b in range(2):
                    blk = one_(pj[:, bass.ds(i * 4 + (VC + 2 * u + b), 1), :])
                    own.link(dve.scalar_tensor_tensor(blk[:, 0:SEQ], ps[:, 6 + b, :], gos[:, b:b + 1], sr[:, b, 0:SEQ],
                                                      ALU.mult, ALU.mult))
                    ins = dve.scalar_tensor_tensor(blk[:, SEQ:N_TOK], ps[:, 4, T4 * b:T4 * b + T4], gos[:, b:b + 1],
                                                   sr[:, b, SEQ:N_TOK], ALU.mult, ALU.mult)
                ins.then_inc(S["h_mix"], 1)
                dve.wait_ge(S["h_mix"], n + 1)
                if not last:
                    gla_evac_dve(dve, i, u + 1)
            gla_head_dve(dve, 0, 0)
            gla_evac_dve(dve, 0, 0)
            gla_turns(dve, step, 20)

        SKV = [(6, 256), (7, 0), (7, 256), (0, 0), (0, 256), (2, 0), (2, 256), (3, 0)]

        def gla_act(act):
            def step(i, u, last):
                n = i * 2 + (u + 1)
                act.wait_ge(S["h_cp"], n)
                act.wait_ge(S["h_mix"], n)
                rr = pj[:, bass.ds(i * 4 + (RC + 2 * u), 2), :]
                act.activation(sr[:, :, :], rr, ACT.Exp, scale=-1.0).then_inc(S["h_a"], 1)
                act.wait_ge(S["h_a"], i * 4 + (2 * u + 1))
                act.activation(sr[:, :, :], sr[:, :, :], ACT.Ln, bias=one[:, 0:1]).then_inc(S["h_a"], 1)
                act.wait_ge(S["h_a"], i * 4 + (2 * u + 2))
                act.activation(sr[:, :, :], sr[:, :, :], ACT.Exp, scale=-1.0).then_inc(S["h_sg"], 1)
                act.wait_ge(S["h_o"], n)
                for c in range(5):
                    src = ps[:, 4 + c // 2, (c % 2) * DV_C:(c % 2 + 1) * DV_C] if c < 4 else ps[0:T4, 1, 0:DV_C]
                    m = P if c < 4 else T4
                    act.activation(on[0:m, c, :], src, ACT.Square, accum_out=gsq[0:m, c:c + 1]).then_inc(S["h_q"], 1)
                act.wait_ge(S["h_q"], i * 10 + (5 * u + 5))
                act.activation(grs[:, :], gsq[:, :], ACT.Ln, bias=eps[:, 0:1], scale=1.0 / DV_C).then_inc(S["h_b"], 1)
                act.wait_ge(S["h_b"], n)
                act.activation(grs[:, :], grs[:, :], ACT.Exp, scale=-0.5).then_inc(S["h_rs"], 1)
            gla_turns(act, step)

        def gla_start_pe(pe, i, u):
            tile = lambda a, c: a[:, P * c:P * c + (P if c < 4 else T4)]
            pe.wait_ge(S["h_cp"], i * 2 + (u + 1))
            pe.wait_ge(SLD[u % 2], i * 16 + 16 * (u // 2 + 1))
            for c in range(4):
                pe.transpose(ps[:, 0, c * P:(c + 1) * P], tile(gk, c), ident)
                for b in range(2):
                    pe.transpose(ps[:, 2 + c // 2, (c % 2) * DV_C + b * P:(c % 2) * DV_C + (b + 1) * P],
                                 tile(gv[:, b], c), ident)
            pe.transpose(ps[0:T4, 1, 0:P], tile(gk, 4), ident)
            for b in range(2):
                mm = pe.transpose(ps[0:T4, 1, P + b * P:2 * P + b * P], tile(gv[:, b], 4), ident)
            mm.then_inc(S["h_tr"], 1)

        def gla_pe(pe):
            tile = lambda a, c: a[:, P * c:P * c + P]

            def step(i, u, last):
                n = i * 2 + (u + 1)
                pe.wait_ge(S["h_kv"], n)
                pe.matmul(ps[:, 4, 0:DV_C], KT[N_SAMP:T4, 4, :], VT[N_SAMP:T4, 4, :], start=True, stop=True)
                for c in range(4):
                    b, o_ = divmod(c + 1, 2)
                    mm = pe.matmul(ps[:, 4 + b, o_ * DV_C:(o_ + 1) * DV_C], KT[:, c, :], VT[:, c, :], start=True, stop=True)
                for s in range(DEC_B):
                    b, o_ = SKV[s]
                    mm = pe.matmul(ps[:, b, o_:o_ + DV_C], gkm[:, s, :], VT[0:N_SAMP, 4, :], start=True, stop=True)
                mm.then_inc(S["h_kvs"], 1)
                pe.matmul(ps[0:T4, 1, 0:DV_C], ATh[0:T4, 4, 0:T4], VT[0:T4, 4, :], start=True, stop=False)
                for s in range(DEC_B):
                    mm = pe.matmul(ps[0:T4, 1, 0:DV_C], gqm[:, T4 * s:T4 * s + T4], s0b[:, u, s, :], start=False,
                                   stop=s == DEC_B - 1)
                mm.then_inc(S["h_t4"], 1)
                pe.wait_ge(S["h_S"], n)
                for c in range(4):
                    out = ps[:, 4 + c // 2, (c % 2) * DV_C:(c % 2 + 1) * DV_C]
                    pe.matmul(out, ATh[:, c, :], VT[:, c, :], start=True, stop=False)
                    mm = pe.matmul(out, tile(gq, c), Ss[:, c, :], start=False, stop=True)
                mm.then_inc(S["h_o"], 1)
                pe.wait_ge(S["h_y"], n)
                for b in range(2):
                    for c in range(4):
                        pe.transpose(ps[:, 6 + b, c * P:(c + 1) * P], on[:, c, b * P:(b + 1) * P], ident)
                for b in range(2):
                    mm = pe.transpose(ps[:, 4, T4 * b:T4 * b + T4], on[0:T4, 4, b * P:(b + 1) * P], ident[0:T4, 0:T4])
                mm.then_inc(S["h_yt"], 1)
                if not last:
                    gla_start_pe(pe, i, u + 1)
            gla_start_pe(pe, 0, 0)
            gla_turns(pe, step)

        SLD = [sem("sld0"), sem("sld1")]

        N_CONST, N_OUT = 12, 4
        block = ctx.enter_context(nc.Block())

        @block.sync
        def _(sp_):
            for half in range(2):
                sp_.dma_start(hT[:, 4 * half:4 * half + 4, :], x[:, 4 * half:4 * half + 4, :]).then_inc(S["xld"], 16)
            for dst, src in ((cst[:, :], const), (gn[:, :, :, :], gains), (gev[:, :], g_even), (god[:, :], g_odd),
                             (bgu[:, :], b_gup), (bsb[:, :], b_sb), (bsr[:, :], b_sbrow), (bcol[:, :], b_sbcol), (bg[:, :], b_gate),
                             (ptab[:, :], pages), (mst[:, :], m_in), (wg[:, :, :], w_gate)):
                sp_.dma_start(dst, src).then_inc(S["cld"], 16)
            load_pairs(sp_, 0, SLAB0["out0"] + 2)
            sp_.wait_ge(S["cld"], 16 * N_CONST)
            sp_.wait_ge(S["pj_done"], 4 * S_EVEN + CREDIT)
            load_keys(sp_)
            sp_.wait_ge(S["b_ev"], 9)
            load_pairs(sp_, SLAB0["out0"] + 2, N_SLABS)
            sp_.wait_ge(S["out"], 16 * N_OUT)

        @block.gpsimd
        def _(pool):
            pool.wait_ge(S["gate"], 1)
            pool.wait_ge(S["n_lo"], 2)
            pool.dma_start(rows[:, R_RST, :], reset[0:H_A, :]).then_inc(S["rst"], 16)
            pool.wait_ge(S["pj_done"], 4 * S_EVEN + CREDIT)
            pool.dma_start(c0[:, :, :, :], c_in).then_inc(S["c0ld"], 16)
            pool.wait_ge(S["pj_act"], 2 * S_EVEN + CREDIT)
            pool.wait_ge(S["pj_dve"], 2 * S_EVEN + CREDIT)
            for b in range(2):
                pool.dma_start(kv_out[:, 4 * b:4 * b + 4, :], pj[:, KBB + 4 * b:KBB + 4 * b + 4, :]).then_inc(S["out"], 16)
            pool.wait_ge(S["gts_ok"], 1)
            pool.dma_start(m_prompt, rows[:, R_M, SEQ - 1:SEQ]).then_inc(S["rout"], 16)
            pool.dma_start(m_sample, mst[:, :]).then_inc(S["rout"], 16)
            pool.wait_ge(S["m_end"], 1)
            pool.dma_start(c_prompt, cfin[:, :, :]).then_inc(S["mout"], 16)
            pool.dma_start(c_sample, c0[:, :, :, :]).then_inc(S["mout"], 16)
            pool.wait_ge(S["cld"], 16 * N_CONST)
            load_values(pool)
            pool.wait_ge(S["n_h"], 2)
            pool.dma_start(wgd[:, :, :], w_gdn).then_inc(S["wgl"], 16)
            pool.dma_start(wgu[:, :], w_gup).then_inc(S["wgl"], 16)
            pool.wait_ge(S["n_h"], 4)
            pool.dma_start(rst[:, :], reset).then_inc(S["grst"], 16)
            pool.wait_ge(S["pj_done"], 4 * (PJ0["odd"] + S_ODD) + CREDIT)
            pool.wait_ge(S["g_sp"], 1)
            pool.dma_start(gmk[:, :, :], masks).then_inc(S["grst"], 16)
            pool.dma_start(gm4[:, :, :], masks4).then_inc(S["grst"], 16)
            for j in range(2):
                pool.dma_start(s0b[:, j, :, :], gla_in[j]).then_inc(SLD[j], 16)
            for h in range(H_C):
                pool.wait_ge(S["h_s0"], h + 1)
                pool.dma_start(s_sample[h], s0b[:, h % 2, :, :]).then_inc(S["sst"], 16)
                pool.wait_ge(S["sst"], 16 * h + 16)
                if h + 2 < H_C:
                    pool.dma_start(s0b[:, h % 2, :, :], gla_in[h + 2]).then_inc(SLD[h % 2], 16)
            pool.dma_start(s_prompt.rearrange("h p n -> p h n"), sfin[:, :, :]).then_inc(S["sst"], 16)
            pool.wait_ge(S["sst"], 16 * (H_C + 1))
            pool.sem_inc(S["sfree"], 1)
            for h in range(2):
                pool.wait_ge(S["n_h"], 7 + h)
                pool.dma_start(y_out[:, :, COLS[h]], hT[:, :, COLS[h]]).then_inc(S["out"], 16)

        @block.tensor
        def _(pe):
            for name, n in (("lo", 2), ("pj_done", CREDIT), ("pj_act", CREDIT), ("pj_dve", CREDIT), ("dn_done", CREDIT),
                            ("d_dve", CREDIT), ("u_lo", 2), ("k_used", 4), ("v_used", 4), ("b_ev", 1), ("m_mix", 1), ("h_mix", 1),
                            ("a_o", 1)):
                pe.sem_inc(S[name], n)
            pe.wait_ge(S["cld"], 16 * N_CONST)
            norm_pe(pe, 0)
            gates_pe(pe)
            pe.wait_ge(S["n_lo"], 2)
            proj_pe(pe, "even")
            rows_pe(pe)
            mlstm_pe(pe)
            new_pe(pe)
            attn_pe(pe)
            pe.wait_ge(S["n_lo"], 4)
            proj_pe(pe, "out0")
            norm_pe(pe, 1)
            norm_pe(pe, 2)
            pe.wait_ge(S["n_lo"], 6)
            mlp_pe(pe, 0)
            norm_pe(pe, 3)
            norm_pe(pe, 4)
            gdown_pe(pe)
            lgate_pe(pe)
            pe.wait_ge(S["n_lo"], 8)
            proj_pe(pe, "odd")
            pj_all(pe, "odd")
            levels_pe(pe)
            gla_pe(pe)
            pe.wait_ge(S["n_lo"], 10)
            proj_pe(pe, "out1")
            norm_pe(pe, 5)
            norm_pe(pe, 6)
            pe.wait_ge(S["n_lo"], 12)
            mlp_pe(pe, 1)
            norm_pe(pe, 7)

        @block.scalar
        def _(act):
            act.preload_act_table_set("natural_log_exp_and_others")
            act.wait_ge(S["xld"], 32)
            norm_act(act, 0, hT, split=0, first=True)
            gates_act(act)
            proj_act(act, "even", beside=rows_act)
            mlstm_act(act)
            new_act(act)
            attn_act(act)
            act.wait_ge(S["a_o"], 9)
            act.wait_ge(S["b_ev"], 9)
            split_mix_act(act, 1, ((0, 0), (QB, 4)))
            proj_act(act, "out0")
            pj_all(act, "out0")
            norm_act(act, 1, pj[:, 0:8, :])
            norm_act(act, 2, hT, split=1, after=0)
            mlp_act(act, 0)
            act.wait_ge(S["d_dve"], 128 + CREDIT)
            norm_act(act, 3, pj[:, 0:8, :])
            norm_act(act, 4, hT, split=2, after=2)
            gdown_act(act)
            lgate_act(act)
            proj_act(act, "odd", beside=softgate_act)
            pj_all(act, "odd")
            gla_pre_act(act)
            gla_act(act)
            act.wait_ge(S["h_mix"], H_C + 1)
            act.wait_ge(S["sfree"], 1)
            split_mix_act(act, 4, ((VC, 0), (VC + 4, 4)))
            proj_act(act, "out1")
            pj_all(act, "out1")
            norm_act(act, 5, pj[:, 0:8, :])
            norm_act(act, 6, hT, split=3, after=4)
            mlp_act(act, 1)
            act.wait_ge(S["d_dve"], 256 + CREDIT)
            norm_act(act, 7, pj[:, 0:8, :])

        @block.vector
        def _(dve):
            nonlocal own
            own = Own(dve, S["dve"])
            dve.memset(one[:, :], 1.0)
            dve.memset(eps[:, :], EPS)
            dve.wait_ge(S["cld"], 16 * N_CONST)
            dve.tensor_scalar(bgu[:, :], bgu[:, :], -1.0, None, ALU.mult)
            dve.tensor_scalar(nbf[:, :], bg[:, 1:2], -1.0, None, ALU.mult).then_inc(S["rows1"], 1)
            split_lo(dve, 0, 0)
            prenorm_dve(dve, 0, 0, 0, 0)
            proj_dve(dve, "even", beside=rows_dve)
            cols_dve(dve)
            mlstm_dve(dve)
            dve.sem_inc(S["m_end"], 1)
            new_dve(dve)
            attn_dve(dve)
            split_mix_dve(dve, 1, ((0, 0), (QB, 4)))
            proj_dve(dve, "out0")
            postnorm_dve(dve, 1, 0, 1)
            prenorm_dve(dve, 2, 0, 2, 2)
            mlp_dve(dve, 0)
            postnorm_dve(dve, 3, 0, 3)
            prenorm_dve(dve, 4, 1, 0, 3)
            proj_dve(dve, "odd", beside=softgate_dve)
            gla_pre_dve(dve)
            gla_dve(dve)
            split_mix_dve(dve, 4, ((VC, 0), (VC + 4, 4)))
            proj_dve(dve, "out1")
            postnorm_dve(dve, 5, 1, 1)
            prenorm_dve(dve, 6, 1, 2, 5)
            mlp_dve(dve, 1)
            postnorm_dve(dve, 7, 1, 3)


_INS = ["x", "weights", "w_gate", "w_gdn", "w_gup", "k_cache", "v_cache", "pages", "c_in", "gla_in", "m_in", "gains",
        "g_even", "g_odd", "b_gate", "b_gup", "b_sb", "b_sbrow", "b_sbcol",
        "const", "reset", "masks", "masks4"]
_OUTS = [(P, KB, N_TOK), (P, 8, N_TOK), (P, H_A, P + 1), (P, H_A, DEC_B, P + 1), (H_A, 1), (H_A, DEC_B),
         (H_C, P, DV_C), (H_C, P, DEC_B, DV_C)]


def lay_out(i):
    np_ = lambda a: np.ascontiguousarray(a)
    feat = lambda a: np_(a.reshape(a.shape[0], -1, P).transpose(2, 1, 0))
    col = lambda a: np_(a.reshape(-1, P).T)

    def slabs(w):
        n = w.shape[1]
        return w.reshape(KB, P, n // 256, 2, P).transpose(2, 1, 3, 0, 4).reshape(n // 256, P, SLAB_TILES, P)

    def mlp(up, down):
        u = slabs(up).reshape(MLP_GROUPS, 2, P, SLAB_TILES, P)
        d = down.reshape(MLP_GROUPS, 4, P, 2, 4, P).transpose(0, 3, 2, 4, 1, 5).reshape(MLP_GROUPS, 2, P, SLAB_TILES, P)
        return np.concatenate([u, d], axis=1).reshape(-1, P, SLAB_TILES, P)

    we, wo = i["w_in_even"][0], i["w_in_odd"][0]
    ga = 4 * H_A * P
    tok = np.concatenate([i["x_prompt"][0], i["x_sample"].reshape(N_SAMP, D), i["meta_tokens"]])
    stream = np.concatenate([slabs(np.concatenate([we[:, :ga], we[:, ga + 2 * H_A:]], axis=1)), slabs(i["w_out_even"][0]),
                             mlp(i["w_up"][0], i["w_down"][0]), slabs(wo[:, :3072]), slabs(i["w_out_odd"][0]),
                             mlp(i["w_up"][1], i["w_down"][1])])
    gates = np.zeros((P, KB, 40), np.float32)
    gates[:, :, 0:H_A] = we[:, ga:ga + H_A].reshape(KB, P, H_A).transpose(1, 0, 2)
    gates[:, :, 32:32 + H_A] = we[:, ga + H_A:ga + 2 * H_A].reshape(KB, P, H_A).transpose(1, 0, 2)
    n_pool = i["cache_sb_k"].shape[1]
    return {
        "x": feat(tok),
        "weights": np_(stream),
        "w_gate": gates,
        "w_gdn": np_(wo[:, 3072:].reshape(KB, P, 16).transpose(1, 0, 2)),
        "w_gup": np_(i["w_gate_up_odd"][0]),
        "k_cache": np_(i["cache_sb_k"][0].reshape(n_pool, P, 4, P).transpose(0, 3, 2, 1).reshape(n_pool, P, 512)),
        "v_cache": np_(i["cache_sb_v"][0].reshape(n_pool, P, 512)),
        "pages": np_(i["page_table"].reshape(1, -1)),
        "c_in": np_(np.concatenate([i["state_mlstm_c"][0], i["state_mlstm_n"][0][..., None]], axis=-1).transpose(2, 1, 0, 3)),
        "gla_in": np_(i["state_gla_s"][0].transpose(1, 2, 0, 3)),
        "m_in": np_(i["state_mlstm_m"][0].T),
        "gains": np_(i["norm_gains"].reshape(2, 4, KB, P).transpose(3, 0, 1, 2)),
        "g_even": col(i["g_head_even"][0]),
        "g_odd": col(i["g_head_odd"][0]),
        "b_gate": np_(i["b_gate_even"][0].reshape(2, H_A).T),
        "b_gup": col(i["b_gate_up_odd"][0]),
        "b_sb": np_(np.broadcast_to(i["b_sb_even"][0], (P, H_B))),
        "b_sbrow": np_(np.broadcast_to(np.repeat(i["b_sb_even"][0], DEC_T), (P, 32))),
        "b_sbcol": np_(np.tile(np.repeat(i["b_sb_even"][0], DEC_T), 4)[:, None]),
        "const": constants(),
        "reset": reset_row(),
        "masks": level_masks(P, np.zeros(P, int), (64, 32, 16, 8, 4, 2, 1, 0)),
        "masks4": level_masks(T4, (np.arange(T4) < N_SAMP).astype(int), (8, 4, 2, 1, 0)),
    }


def kernel(**inputs):
    import concourse.bacc as _bacc
    from concourse.bass_utils import run_bass_kernel_spmd as _run

    laid = lay_out({k: np.asarray(v) for k, v in inputs.items()})
    nc = _bacc.Bacc("TRN2", target_bir_lowering=False, num_devices=1)
    arrays, args = {}, []
    for name in _INS:
        arrays[f"in_{name}_dram"] = laid[name]
        args.append(nc.dram_tensor(f"in_{name}_dram", laid[name].shape, mybir.dt.from_np(laid[name].dtype),
                                   kind="ExternalInput").ap())
    for i, shape in enumerate(_OUTS):
        args.append(nc.dram_tensor(f"out_{i}_dram", shape, mybir.dt.float32, kind="ExternalOutput").ap())
    build(nc, *args)
    r = _run(nc, [arrays], core_ids=[0])
    y, kv, cp, cs, mp, ms, sp, ss = (r.results[0][f"out_{i}_dram"] for i in range(len(_OUTS)))
    rows = lambda a: a.transpose(2, 1, 0).reshape(N_TOK, -1)
    y, k, v = rows(y), rows(kv[:, 0:4]), rows(kv[:, 4:8])
    prompt = lambda a: np.concatenate([a[META0:], a[:SEQ]]).reshape(1, 1, N_META + SEQ, H_B, DH_B)
    samp = lambda a: a[SAMP0:META0].reshape(1, DEC_B, DEC_T, H_B, DH_B)
    cp, cs = cp.transpose(1, 0, 2), cs.transpose(2, 1, 0, 3)
    out = (y[:SEQ].reshape(1, SEQ, D), y[SAMP0:META0].reshape(DEC_B, DEC_T, D), prompt(k), prompt(v),
           cp[None, None, :, :, :P], cp[None, None, :, :, P], mp.reshape(1, 1, H_A), sp[None, None],
           samp(k), samp(v), cs[None, :, :, :, :P], cs[None, :, :, :, P], ms.T[None], ss.transpose(2, 0, 1, 3)[None])
    return tuple(np.ascontiguousarray(o) for o in out)
```
